# Optimizing a Trainium2 kernel written in Bass

```python
import math
import jax, jax.numpy as jnp
from jax import lax
import numpy as np

D_MODEL = 1024
BATCH = 1
SEQ = 512
DEPTH = 2

GRID_W = 64
CTX_LEN = 256
HEAD_DIM = 64
ROPE_THETA = 10000.0
EPS = 1e-6
Q_BLOCK = 128
A_Q_HEADS = 8
A_KV_HEADS = 2
A_WIDTH = A_Q_HEADS * HEAD_DIM
A_KV_WIDTH = A_KV_HEADS * HEAD_DIM
B_WIDTH = D_MODEL // 2
B_WINDOWS = (2, 4, 8, 16)
B_GROUPS = len(B_WINDOWS)
B_GROUP_W = B_WIDTH // B_GROUPS
EVEN_IN = A_WIDTH + 2 * A_KV_WIDTH + B_WIDTH
EVEN_MIX = A_WIDTH + B_WIDTH
C_Q_HEADS = 16
C_KV_HEADS = 4
C_WIDTH = C_Q_HEADS * HEAD_DIM
C_KV_WIDTH = C_KV_HEADS * HEAD_DIM
ODD_IN = C_WIDTH + 2 * C_KV_WIDTH
WINDOW = 128
N_SIDE = WINDOW // Q_BLOCK
BAND_BLOCKS = 2 * N_SIDE + 1
BAND_LEN = BAND_BLOCKS * Q_BLOCK
FFN_HIDDEN = int(math.ceil(8 * D_MODEL / 3 / 256)) * 256
N_EVEN = (DEPTH + 1) // 2
N_ODD = DEPTH // 2


def rmsnorm(x, g):
    xf = x.astype(jnp.float32)
    y = xf * lax.rsqrt(jnp.mean(xf * xf, axis=-1, keepdims=True) + EPS)
    return (y * g.astype(jnp.float32)).astype(x.dtype)

def modulate(x, g, shift, scale):
    return rmsnorm(x, g) * (1 + scale) + shift

def split_heads(t, h):
    return t.reshape(t.shape[0], t.shape[1], h, HEAD_DIM)

def axial_rope(x, rows, cols):
    hd = x.shape[-1]
    quarter = hd // 4
    freqs = ROPE_THETA ** (-jnp.arange(quarter, dtype=jnp.float32) / quarter)

    def rot(a, pos):
        ang = pos.astype(jnp.float32)[:, None] * freqs[None, :]
        cos = jnp.cos(ang)[None, :, None, :]
        sin = jnp.sin(ang)[None, :, None, :]
        a1, a2 = a[..., :quarter], a[..., quarter:]
        return jnp.concatenate([a1 * cos - a2 * sin, a2 * cos + a1 * sin], axis=-1)

    out = jnp.concatenate([rot(x[..., :hd // 2], rows), rot(x[..., hd // 2:], cols)], axis=-1)
    return out.astype(x.dtype)

def dense_gqa_blocks(q, k, v):
    B, S, H, hd = q.shape
    KV = k.shape[2]
    G = H // KV
    nb = S // Q_BLOCK
    scale = 1.0 / math.sqrt(hd)
    qb = q.reshape(B, nb, Q_BLOCK, KV, G, hd).transpose(1, 0, 2, 3, 4, 5)

    def one(qblk):
        s = jnp.einsum('bqkgd,btkd->bkgqt', qblk, k, preferred_element_type=jnp.float32) * scale
        p = jax.nn.softmax(s, axis=-1).astype(v.dtype)
        return jnp.einsum('bkgqt,btkd->bqkgd', p, v)

    o = lax.map(one, qb)
    return o.transpose(1, 0, 2, 3, 4, 5).reshape(B, S, H * hd)

def ctx_attention(q, k, v, sink=None):
    B, T, H, hd = q.shape
    KV = k.shape[2]
    G = H // KV
    scale = 1.0 / math.sqrt(hd)
    qg = q.reshape(B, T, KV, G, hd)
    s = jnp.einsum('bqkgd,btkd->bkgqt', qg, k, preferred_element_type=jnp.float32) * scale
    if sink is not None:
        s_sink = jnp.broadcast_to(sink.reshape(KV, G)[None, :, :, None, None].astype(jnp.float32),
                                  (B, KV, G, T, 1))
        s = jnp.concatenate([s, s_sink], axis=-1)
    p = jax.nn.softmax(s, axis=-1)
    if sink is not None:
        p = p[..., :-1]
    o = jnp.einsum('bkgqt,btkd->bqkgd', p.astype(v.dtype), v)
    return o.reshape(B, T, H * hd)

def window_gqa_blocks(q, k, v, k_ctx, v_ctx, sink):
    B, S, H, hd = q.shape
    KV = k.shape[2]
    G = H // KV
    C = k_ctx.shape[1]
    nb = S // Q_BLOCK
    scale = 1.0 / math.sqrt(hd)
    qb = q.reshape(B, nb, Q_BLOCK, KV, G, hd).transpose(1, 0, 2, 3, 4, 5)

    def band(t):
        tp = jnp.pad(t, ((0, 0), (WINDOW, WINDOW), (0, 0), (0, 0)))
        tp = tp.reshape(B, nb + 2 * N_SIDE, Q_BLOCK, KV, hd)
        tb = jnp.concatenate([tp[:, j:j + nb] for j in range(BAND_BLOCKS)], axis=2)
        return tb.transpose(1, 0, 2, 3, 4)

    kb, vb = band(k), band(v)
    n_i = jnp.arange(nb)[:, None, None]
    q_i = jnp.arange(Q_BLOCK)[None, :, None]
    k_j = jnp.arange(BAND_LEN)[None, None, :]
    qpos = n_i * Q_BLOCK + q_i
    kpos = n_i * Q_BLOCK - WINDOW + k_j
    mask = (kpos >= 0) & (kpos < S) & (jnp.abs(qpos - kpos) <= WINDOW)
    sink_l = sink.reshape(KV, G)[None, :, :, None, None].astype(jnp.float32)

    def one(args):
        qblk, kblk, vblk, m = args
        s_w = jnp.einsum('bqkgd,btkd->bkgqt', qblk, kblk, preferred_element_type=jnp.float32) * scale
        s_w = jnp.where(m[None, None, None], s_w, -jnp.inf)
        s_c = jnp.einsum('bqkgd,btkd->bkgqt', qblk, k_ctx, preferred_element_type=jnp.float32) * scale
        s_s = jnp.broadcast_to(sink_l, (B, KV, G, Q_BLOCK, 1))
        p = jax.nn.softmax(jnp.concatenate([s_w, s_c, s_s], axis=-1), axis=-1).astype(v.dtype)
        o = jnp.einsum('bkgqt,btkd->bqkgd', p[..., :BAND_LEN], vblk)
        o = o + jnp.einsum('bkgqt,btkd->bqkgd', p[..., BAND_LEN:BAND_LEN + C], v_ctx)
        return o

    o = lax.map(one, (qb, kb, vb, mask))
    return o.transpose(1, 0, 2, 3, 4, 5).reshape(B, S, H * hd)

def centred_mean(u, w):
    S = u.shape[1]
    cs = jnp.pad(jnp.cumsum(u.astype(jnp.float32), axis=1), ((0, 0), (1, 0), (0, 0)))
    t = jnp.arange(S)
    lo = jnp.clip(t - w // 2, 0, S)
    hi = jnp.clip(t + w - w // 2, 0, S)
    cnt = (hi - lo).astype(jnp.float32)
    return ((cs[:, hi] - cs[:, lo]) / cnt[None, :, None]).astype(u.dtype)

def pool_mixer(u, w_pool, pool_scale):
    B, S, _ = u.shape
    diffs = []
    for g, w in enumerate(B_WINDOWS):
        ug = u[..., g * B_GROUP_W:(g + 1) * B_GROUP_W]
        diffs.append(centred_mean(ug, w) - ug)
    d = jnp.stack(diffs, axis=2)
    y = jnp.einsum('bsgc,gcd->bsgd', d, w_pool).reshape(B, S, B_WIDTH)
    return y * pool_scale

def even_mixer(h, hc, w_in, w_out, q_gain, k_gain, w_pool, pool_scale, rows, cols, with_ctx):
    def project(t):
        p = t @ w_in
        q, k, v, u = jnp.split(p, [A_WIDTH, A_WIDTH + A_KV_WIDTH, A_WIDTH + 2 * A_KV_WIDTH], axis=-1)
        q = rmsnorm(split_heads(q, A_Q_HEADS), q_gain)
        k = rmsnorm(split_heads(k, A_KV_HEADS), k_gain)
        return q, k, split_heads(v, A_KV_HEADS), u

    q, k, v, u = project(h)
    qc, kc, vc, uc = project(hc)
    q = axial_rope(q, rows, cols)
    k = axial_rope(k, rows, cols)
    a = dense_gqa_blocks(q, jnp.concatenate([k, kc], axis=1), jnp.concatenate([v, vc], axis=1))
    b = pool_mixer(u, w_pool, pool_scale)
    y = jnp.concatenate([a, b], axis=-1) @ w_out
    yc = None
    if with_ctx:
        ac = ctx_attention(qc, kc, vc)
        bc = pool_mixer(uc, w_pool, pool_scale)
        yc = jnp.concatenate([ac, bc], axis=-1) @ w_out
    return y, yc

def odd_mixer(h, hc, w_in, w_out, sink, rows, cols, with_ctx):
    def project(t):
        p = t @ w_in
        q, k, v = jnp.split(p, [C_WIDTH, C_WIDTH + C_KV_WIDTH], axis=-1)
        return split_heads(q, C_Q_HEADS), split_heads(k, C_KV_HEADS), split_heads(v, C_KV_HEADS)

    q, k, v = project(h)
    qc, kc, vc = project(hc)
    q = axial_rope(q, rows, cols)
    k = axial_rope(k, rows, cols)
    y = window_gqa_blocks(q, k, v, kc, vc, sink) @ w_out
    yc = None
    if with_ctx:
        yc = ctx_attention(qc, kc, vc, sink) @ w_out
    return y, yc

def swiglu(h, w_in, w_out):
    g, u = jnp.split(h @ w_in, 2, axis=-1)
    return (jax.nn.silu(g) * u) @ w_out

def first_inputs(seed: int = 0) -> dict:
    key = jax.random.key(seed)
    ks = jax.random.split(key, 24)
    D = D_MODEL

    def nrm(k, shape, std):
        return jax.random.normal(k, shape, dtype=jnp.float32) * std

    return {
        "x": nrm(ks[0], (BATCH, SEQ, D), 1.0),
        "c": nrm(ks[1], (BATCH, D), 1.0),
        "ctx": nrm(ks[2], (BATCH, CTX_LEN, D), 1.0),
        "c_ctx": nrm(ks[3], (D,), 1.0),
        "w_mod": nrm(ks[4], (DEPTH, D, 6 * D), 0.5 * D ** -0.5),
        "b_mod": nrm(ks[5], (DEPTH, 6 * D), 0.02),
        "g_pre_mix": 1.0 + nrm(ks[6], (DEPTH, D), 0.05),
        "g_post_mix": 1.0 + nrm(ks[7], (DEPTH, D), 0.05),
        "g_pre_ffn": 1.0 + nrm(ks[8], (DEPTH, D), 0.05),
        "g_post_ffn": 1.0 + nrm(ks[9], (DEPTH, D), 0.05),
        "we_in": nrm(ks[10], (N_EVEN, D, EVEN_IN), D ** -0.5),
        "we_out": nrm(ks[11], (N_EVEN, EVEN_MIX, D), EVEN_MIX ** -0.5),
        "we_q_gain": 1.0 + nrm(ks[12], (N_EVEN, HEAD_DIM), 0.05),
        "we_k_gain": 1.0 + nrm(ks[13], (N_EVEN, HEAD_DIM), 0.05),
        "we_pool": nrm(ks[14], (N_EVEN, B_GROUPS, B_GROUP_W, B_GROUP_W), B_GROUP_W ** -0.5),
        "we_pool_scale": 1.0 + nrm(ks[15], (N_EVEN, B_WIDTH), 0.1),
        "wo_in": nrm(ks[16], (N_ODD, D, ODD_IN), D ** -0.5),
        "wo_out": nrm(ks[17], (N_ODD, C_WIDTH, D), C_WIDTH ** -0.5),
        "wo_sink": nrm(ks[18], (N_ODD, C_Q_HEADS), 0.5),
        "w_ffn_in": nrm(ks[19], (DEPTH, D, 2 * FFN_HIDDEN), D ** -0.5),
        "w_ffn_out": nrm(ks[20], (DEPTH, FFN_HIDDEN, D), FFN_HIDDEN ** -0.5),
    }

def first_block(x, c, ctx, c_ctx, w_mod, b_mod, g_pre_mix, g_post_mix, g_pre_ffn, g_post_ffn,
              we_in, we_out, we_q_gain, we_k_gain, we_pool, we_pool_scale,
              wo_in, wo_out, wo_sink, w_ffn_in, w_ffn_out):
    S = x.shape[1]
    ROWS = S // GRID_W
    rows = jnp.repeat(jnp.arange(ROWS, dtype=jnp.int32), GRID_W)
    cols = jnp.tile(jnp.arange(GRID_W, dtype=jnp.int32), ROWS)
    silu_c = jax.nn.silu(c)
    silu_cc = jax.nn.silu(c_ctx)

    for l in range(DEPTH):
        with_ctx = l < DEPTH - 1
        mod = (silu_c @ w_mod[l] + b_mod[l])[:, None, :]
        mod_c = (silu_cc @ w_mod[l] + b_mod[l])[None, None, :]
        sh_m, sc_m, gt_m, sh_f, sc_f, gt_f = jnp.split(mod, 6, axis=-1)
        csh_m, csc_m, cgt_m, csh_f, csc_f, cgt_f = jnp.split(mod_c, 6, axis=-1)

        h = modulate(x, g_pre_mix[l], sh_m, sc_m)
        hc = modulate(ctx, g_pre_mix[l], csh_m, csc_m)
        i = l // 2
        if l % 2 == 0:
            y, yc = even_mixer(h, hc, we_in[i], we_out[i], we_q_gain[i], we_k_gain[i],
                               we_pool[i], we_pool_scale[i], rows, cols, with_ctx)
        else:
            y, yc = odd_mixer(h, hc, wo_in[i], wo_out[i], wo_sink[i], rows, cols, with_ctx)

        x = x + gt_m * rmsnorm(y, g_post_mix[l])
        h = modulate(x, g_pre_ffn[l], sh_f, sc_f)
        x = x + gt_f * rmsnorm(swiglu(h, w_ffn_in[l], w_ffn_out[l]), g_post_ffn[l])

        if with_ctx:
            ctx = ctx + cgt_m * rmsnorm(yc, g_post_mix[l])
            hc = modulate(ctx, g_pre_ffn[l], csh_f, csc_f)
            ctx = ctx + cgt_f * rmsnorm(swiglu(hc, w_ffn_in[l], w_ffn_out[l]), g_post_ffn[l])
    return x


DEPTH_2 = 1

CHUNK = 64
LEFT_CHUNKS = 8
BAND = (LEFT_CHUNKS + 1) * CHUNK
ATT_HEADS = 8
ATT_HEAD_DIM = 64
ATT_WIDTH = ATT_HEADS * ATT_HEAD_DIM
MAX_REL = 128
LRU_WIDTH = D_MODEL
LRU_BLOCKS = 16
LRU_BLOCK = LRU_WIDTH // LRU_BLOCKS
CONV_WIDTH = 4
LRU_C = 8.0
D_FF = 2816
N_SUB = 3
PROJ_SIZES = (ATT_WIDTH, ATT_WIDTH, ATT_WIDTH, LRU_WIDTH, LRU_WIDTH, D_MODEL, D_MODEL)
PROJ_WIDTH = sum(PROJ_SIZES)


def rmsnorm_2(x, g):
    xf = x.astype(jnp.float32)
    y = xf * lax.rsqrt(jnp.mean(xf * xf, axis=-1, keepdims=True) + EPS)
    return (y * g.astype(jnp.float32)).astype(x.dtype)

def modulate_2(h, shift, scale):
    return h * (1 + scale[:, None, :]) + shift[:, None, :]

def swiglu_2(h, w_gu, w_down):
    g, u = jnp.split(h @ w_gu, 2, axis=-1)
    return (jax.nn.silu(g) * u) @ w_down

def chunked_attention(q, k, v, rel_bias):
    b, s, _ = q.shape
    nc = s // CHUNK
    q = q.reshape(b, nc, CHUNK, ATT_HEADS, ATT_HEAD_DIM)
    k = k.reshape(b, nc, CHUNK, ATT_HEADS, ATT_HEAD_DIM)
    v = v.reshape(b, nc, CHUNK, ATT_HEADS, ATT_HEAD_DIM)
    pad = ((0, 0), (LEFT_CHUNKS, 0), (0, 0), (0, 0), (0, 0))
    kp, vp = jnp.pad(k, pad), jnp.pad(v, pad)
    kb = jnp.concatenate([kp[:, j:j + nc] for j in range(LEFT_CHUNKS + 1)], axis=2)
    vb = jnp.concatenate([vp[:, j:j + nc] for j in range(LEFT_CHUNKS + 1)], axis=2)
    scores = jnp.einsum('bnqhd,bnkhd->bhnqk', q, kb).astype(jnp.float32) * (ATT_HEAD_DIM ** -0.5)
    qi = jnp.arange(CHUNK)[:, None]
    kj = jnp.arange(BAND)[None, :]
    rel = jnp.clip(qi - kj + LEFT_CHUNKS * CHUNK, -MAX_REL, MAX_REL) + MAX_REL
    bias = rel_bias.astype(jnp.float32)[:, rel]
    scores = scores + bias[None, :, None, :, :]
    valid = (jnp.arange(nc)[:, None] - LEFT_CHUNKS + jnp.arange(BAND)[None, :] // CHUNK) >= 0
    scores = jnp.where(valid[None, None, :, None, :], scores, jnp.finfo(jnp.float32).min)
    p = jax.nn.softmax(scores, axis=-1).astype(v.dtype)
    out = jnp.einsum('bhnqk,bnkhd->bnqhd', p, vb)
    return out.reshape(b, s, ATT_WIDTH)

def causal_depthwise_conv(x, w, bias):
    rhs = w[:, None, :]
    y = lax.conv_general_dilated(x, rhs, window_strides=(1,), padding=[(CONV_WIDTH - 1, 0)],
                                 dimension_numbers=('NWC', 'WIO', 'NWC'),
                                 feature_group_count=x.shape[-1])
    return y + bias

def block_diag_linear(x, w, bias):
    b, s, _ = x.shape
    xb = x.reshape(b, s, LRU_BLOCKS, LRU_BLOCK)
    return jnp.einsum('bsnk,nkj->bsnj', xb, w).reshape(b, s, LRU_WIDTH) + bias

def rg_lru(x, w_a, b_a, w_x, b_x, lam):
    r = jax.nn.sigmoid(block_diag_linear(x, w_a, b_a).astype(jnp.float32))
    i = jax.nn.sigmoid(block_diag_linear(x, w_x, b_x).astype(jnp.float32))
    log_a = -LRU_C * r * jax.nn.softplus(-lam.astype(jnp.float32))
    a = jnp.exp(log_a)
    mult = jnp.sqrt(-jnp.expm1(2.0 * log_a))
    u = mult * (i * x.astype(jnp.float32))

    def combine(left, right):
        a1, b1 = left
        a2, b2 = right
        return a1 * a2, a2 * b1 + b2

    _, h = lax.associative_scan(combine, (a, u), axis=1)
    return h.astype(x.dtype)

def mixer(h, w_in, rel_bias, conv_w, conv_b, lru_wa, lru_ba, lru_wx, lru_bx, lru_lambda,
          w_att_o, w_rec_o, w_out):
    proj = h @ w_in
    idx = [int(v) for v in np.cumsum(PROJ_SIZES)[:-1]]
    q, k, v, xr, yr, g_att, g_rec = jnp.split(proj, idx, axis=-1)
    att = chunked_attention(q, k, v, rel_bias) @ w_att_o
    xr = causal_depthwise_conv(xr, conv_w, conv_b)
    rec = (rg_lru(xr, lru_wa, lru_ba, lru_wx, lru_bx, lru_lambda) * jax.nn.gelu(yr)) @ w_rec_o
    merged = jax.nn.sigmoid(g_att) * att + jax.nn.sigmoid(g_rec) * rec
    return merged @ w_out

def sandwich(x, fn, g_pre, g_post, shift, scale, gate, res_w):
    h = modulate_2(rmsnorm_2(x, g_pre), shift, scale)
    y = rmsnorm_2(fn(h), g_post)
    return x + res_w * gate[:, None, :] * y

def second_inputs(seed: int = 0) -> dict:
    key = jax.random.key(seed)
    ks = jax.random.split(key, 24)
    L, D, F, W = DEPTH_2, D_MODEL, D_FF, LRU_WIDTH
    nrm = lambda k, shape, fan_in: jax.random.normal(k, shape, jnp.float32) * (fan_in ** -0.5)
    u = jax.random.uniform(ks[20], (L, W), jnp.float32, 0.9, 0.999)
    p = u ** (1.0 / LRU_C)
    lam = jnp.log(p) - jnp.log1p(-p)
    return {
        "x": jax.random.normal(ks[0], (BATCH, SEQ, D), jnp.float32),
        "c": jax.random.normal(ks[1], (BATCH, D), jnp.float32),
        "w_ada": nrm(ks[2], (L, D, N_SUB * 3 * D), D) * 0.5,
        "b_ada": 0.02 * jax.random.normal(ks[3], (L, N_SUB * 3 * D), jnp.float32),
        "norm_pre": 1.0 + 0.05 * jax.random.normal(ks[4], (L, N_SUB, D), jnp.float32),
        "norm_post": 1.0 + 0.05 * jax.random.normal(ks[5], (L, N_SUB, D), jnp.float32),
        "ffn1_w_gu": nrm(ks[6], (L, D, 2 * F), D),
        "ffn1_w_down": nrm(ks[7], (L, F, D), F),
        "w_in": nrm(ks[8], (L, D, PROJ_WIDTH), D),
        "rel_bias": 0.5 * jax.random.normal(ks[9], (L, ATT_HEADS, 2 * MAX_REL + 1), jnp.float32),
        "conv_w": nrm(ks[10], (L, CONV_WIDTH, W), CONV_WIDTH),
        "conv_b": 0.02 * jax.random.normal(ks[11], (L, W), jnp.float32),
        "lru_wa": nrm(ks[12], (L, LRU_BLOCKS, LRU_BLOCK, LRU_BLOCK), LRU_BLOCK),
        "lru_ba": 0.02 * jax.random.normal(ks[13], (L, W), jnp.float32),
        "lru_wx": nrm(ks[14], (L, LRU_BLOCKS, LRU_BLOCK, LRU_BLOCK), LRU_BLOCK),
        "lru_bx": 0.02 * jax.random.normal(ks[15], (L, W), jnp.float32),
        "lru_lambda": lam,
        "w_att_o": nrm(ks[16], (L, ATT_WIDTH, D), ATT_WIDTH),
        "w_rec_o": nrm(ks[17], (L, W, D), W),
        "w_out": nrm(ks[18], (L, D, D), D),
        "ffn2_w_gu": nrm(ks[19], (L, D, 2 * F), D),
        "ffn2_w_down": nrm(ks[21], (L, F, D), F),
    }

def second_block(x, c, w_ada, b_ada, norm_pre, norm_post, ffn1_w_gu, ffn1_w_down, w_in, rel_bias,
              conv_w, conv_b, lru_wa, lru_ba, lru_wx, lru_bx, lru_lambda, w_att_o, w_rec_o,
              w_out, ffn2_w_gu, ffn2_w_down):
    b = x.shape[0]
    c_act = jax.nn.silu(c)
    for l in range(DEPTH_2):
        mod = (c_act @ w_ada[l] + b_ada[l]).reshape(b, N_SUB, 3, D_MODEL)
        ffn1 = lambda h: swiglu_2(h, ffn1_w_gu[l], ffn1_w_down[l])
        mix = lambda h: mixer(h, w_in[l], rel_bias[l], conv_w[l], conv_b[l], lru_wa[l], lru_ba[l],
                              lru_wx[l], lru_bx[l], lru_lambda[l], w_att_o[l], w_rec_o[l], w_out[l])
        ffn2 = lambda h: swiglu_2(h, ffn2_w_gu[l], ffn2_w_down[l])
        x = sandwich(x, ffn1, norm_pre[l, 0], norm_post[l, 0], mod[:, 0, 0], mod[:, 0, 1], mod[:, 0, 2], 0.5)
        x = sandwich(x, mix, norm_pre[l, 1], norm_post[l, 1], mod[:, 1, 0], mod[:, 1, 1], mod[:, 1, 2], 1.0)
        x = sandwich(x, ffn2, norm_pre[l, 2], norm_post[l, 2], mod[:, 2, 0], mod[:, 2, 1], mod[:, 2, 2], 0.5)
    return x


def setup_inputs(seed=0):
    out = dict(first_inputs(seed))
    for name, value in second_inputs(seed + 1).items():
        if name != "x":
            out[name + "_2"] = value
    return out


def reference(
    x, c, ctx, c_ctx, w_mod, b_mod, g_pre_mix, g_post_mix, g_pre_ffn, g_post_ffn, we_in, we_out,
    we_q_gain, we_k_gain, we_pool, we_pool_scale, wo_in, wo_out, wo_sink, w_ffn_in, w_ffn_out,
    c_2, w_ada_2, b_ada_2, norm_pre_2, norm_post_2, ffn1_w_gu_2, ffn1_w_down_2, w_in_2,
    rel_bias_2, conv_w_2, conv_b_2, lru_wa_2, lru_ba_2, lru_wx_2, lru_bx_2, lru_lambda_2,
    w_att_o_2, w_rec_o_2, w_out_2, ffn2_w_gu_2, ffn2_w_down_2,
):
    x = first_block(
        x, c, ctx, c_ctx, w_mod, b_mod, g_pre_mix, g_post_mix, g_pre_ffn, g_post_ffn, we_in,
        we_out, we_q_gain, we_k_gain, we_pool, we_pool_scale, wo_in, wo_out, wo_sink, w_ffn_in,
        w_ffn_out,
    )
    return second_block(
        x, c_2, w_ada_2, b_ada_2, norm_pre_2, norm_post_2, ffn1_w_gu_2, ffn1_w_down_2, w_in_2,
        rel_bias_2, conv_w_2, conv_b_2, lru_wa_2, lru_ba_2, lru_wx_2, lru_bx_2, lru_lambda_2,
        w_att_o_2, w_rec_o_2, w_out_2, ffn2_w_gu_2, ffn2_w_down_2,
    )


_drawn_inputs = setup_inputs


def setup_inputs(seed=0):
    import zlib

    import numpy as np

    out = dict(_drawn_inputs(seed))
    spreads = {}
    factors = {'g_pre_mix': 2.855,
     'g_post_ffn': 2.748,
     'we_q_gain': 8.0,
     'we_k_gain': 8.0,
     'wo_sink': 64.0,
     'norm_pre_2': 2.729,
     'norm_post_2': 3.616,
     'rel_bias_2': 3.744,
     'conv_b_2': 4.348,
     'lru_ba_2': 38.666,
     'lru_bx_2': 26.462}
    for name, (base, spread) in spreads.items():
        noise = np.random.default_rng([zlib.crc32(name.encode()), seed]).standard_normal(out[name].shape)
        drawn = base * np.exp(spread * noise) if base else spread * noise
        out[name] = __import__('jax').numpy.asarray(drawn.astype(out[name].dtype))
    for name, factor in factors.items():
        out[name] = (out[name] * factor).astype(out[name].dtype)
    return out
```

```python
from contextlib import ExitStack

import numpy as np

import concourse.bass as bass
from concourse import mybir

F32 = mybir.dt.float32
F32R = mybir.dt.float32r
ACT = mybir.ActivationFunctionType
ALU = mybir.AluOpType
AX = mybir.AxisListType

P = 128
D = 1024
KC = D // P
S, C = 512, 256
T = S + C
NQ = S // P
HD = 64
EPS = 1e-6
FH = 2816
NH = FH // P
NG = NH // 2
FFN_BLOCKS = 3 * NH
SCALE = HD ** -0.5
MASKED = -float(2.0 ** 100)
LRU_C = 8.0
CONV = 4
RING = 4
BLK = 8 * P
POOL_W = (2, 4, 8, 16)
PAD = 16
UCOLS = PAD + S + 2 * PAD + C + PAD
ROT = [(i + 16) % 32 for i in range(32)]

STAGES = [("l0_in", 10), ("l0_pool", 1), ("l0_out", 8), ("l0_ffn", FFN_BLOCKS),
          ("l1_in", 12), ("l1_out", 8), ("l1_ffn", FFN_BLOCKS),
          ("s_ffn1", FFN_BLOCKS), ("s_in", 12), ("s_atto", 4), ("s_gatt", 8), ("s_rec", 16),
          ("s_grec", 8), ("s_reco", 8), ("s_out", 8), ("s_ffn2", FFN_BLOCKS)]
FIRST = {}
NBLK = 0
for _name, _count in STAGES:
    FIRST[_name] = NBLK
    NBLK += _count
MOD0, MOD1, MOD2, NMOD = 0, 48, 96, 168
MOD_FIRST = 16

PASSES = ["l0_mix_pre", "l0_mix_post", "l0_ffn_pre", "l0_ffn_post", "l1_mix_pre", "l1_mix_post",
          "l1_ffn_pre", "l1_ffn_post", "s0_pre", "s0_post", "s1_pre", "s1_post", "s2_pre", "s2_post"]
PASS_SEGS = {p: 2 if p[:2] == "l0" or p == "l1_mix_pre" else 1 for p in PASSES}


CONSTS = [("ident", [P]), ("blkones", [P]), ("cos", [S]), ("sin", [S]), ("cvec", [KC, 2]), ("cvec2", [KC, 2]),
          ("bmod", [NMOD]),
          ("gpre", [7, KC]), ("gpost", [7, KC]), ("qk_gain", [2]), ("pool_scale", [4]),
          ("edges", [4, 2, 8]),
          ("nsink", [16]),
          ("relc", [8]),
          ("conv_w", [KC, CONV]), ("conv_b", [KC]), ("lru_ba", [KC]), ("lru_bx", [KC]),
          ("lru_s8", [KC])]


def padded(cols):
    return (int(np.prod(cols)) + 7) // 8 * 8


PACKED = sum(padded(c) for _, c in CONSTS)


def segs(n):
    return [(0, S), (S, C)][:n]


def before(name, kind=""):
    return sum(PASS_SEGS[p] for p in PASSES[:PASSES.index(name)] if p.endswith(kind))


def build(nc, A):
    with ExitStack() as ctx:
        write_program(nc, A, ctx)


def write_program(nc, A, ctx):
    sems = {}

    def sem(name):
        if name not in sems:
            sems[name] = ctx.enter_context(nc.semaphore(name))
        return sems[name]

    X = 16512
    MIX = X + KC * S * 4
    XC, Y, HID = MIX, MIX + KC * C * 4, MIX + KC * C * 4 + KC * T * 4
    H = HID + 8 * T * 4
    HSPARE = H + 2 * KC * S * 4
    WHL = H + 2 * KC * T * 4
    RAW = WHL + 2 * RING * BLK * 4
    MODRAW = RAW + RING * BLK * 4
    SCR = MODRAW + RING * BLK * 4
    CONST = SCR + 15360
    cursor = [CONST]

    def at(name, cols, off, dt=F32):
        return nc.alloc_sbuf_tensor_at(name, [P] + cols, dt, offset=off)

    def const(name, cols, dt=F32):
        t = at(name, cols, cursor[0], dt)
        cursor[0] += 4 * padded(cols)
        return t

    xl, xc = at("xl", [KC, S], X), at("xc", [KC, C], XC)
    xs = [xl, xc]
    h_hi, h_lo = at("h_hi", [KC, T], H, F32R), at("h_lo", [KC, T], H + KC * T * 4, F32R)
    n_hi, n_lo = at("n_hi", [KC, S], H, F32R), at("n_lo", [KC, S], H + KC * S * 4, F32R)
    y = at("y", [KC, T], Y)
    y1 = at("y1", [KC, S], Y)
    w_hi, w_lo = at("w_hi", [RING, BLK], WHL, F32R), at("w_lo", [RING, BLK], WHL + RING * BLK * 4, F32R)
    raw = at("raw", [RING, BLK], RAW)
    modraw = at("modraw", [RING, BLK], MODRAW)

    loaded = const("loaded", [PACKED])
    place = {}
    for name, cols in CONSTS:
        place[name] = sum(padded(c) for _, c in CONSTS[:len(place)])

    def part(name, cols):
        view = loaded[:, place[name]:place[name] + int(np.prod(cols))]
        if len(cols) == 1:
            return view
        names = "abc"[:len(cols)]
        sizes = dict(zip(names, cols))
        return view.rearrange(f"p ({' '.join(names)}) -> p {' '.join(names)}", **sizes)

    (ident, blkones, cos, sin, cvec, cvec2, bmod, gpre, gpost, qk_gain, pool_scale, edges, nsink, relc, conv_w,
     conv_b, lru_ba, lru_bx, lru_s8) = (part(n, c) for n, c in CONSTS)
    ones = const("ones", [P])
    lru_n8 = const("lru_n8", [KC])
    modv = const("modv", [72, 2])
    vec_a = const("vec_a", [3, KC, 2])
    vec_b = const("vec_b", [3, KC, 2])
    vec_g = const("vec_g", [3, KC, 2])
    eps_col = const("eps_col", [1])
    smax, negm, rsum, esink, rinv = (const(n, [4]) for n in ("smax", "negm", "rsum", "esink", "rinv"))
    assert cursor[0] <= nc.sbuf_usable_end, (cursor[0], nc.sbuf_usable_end)

    sq = at("sq", [2, S], SCR)
    rstd = at("rstd", [T], SCR + 4096)
    tn = at("tn", [2, S], SCR + 7168)
    qn, qraw, tsh = at("qn", [T], SCR + 7168), at("qraw", [T], SCR + 10240), at("tsh", [S], SCR + 13312)
    upad, sA, sB = (at(n, [UCOLS], SCR + 4096 + i * UCOLS * 4) for i, n in enumerate(("upad", "sA", "sB")))
    prob = at("prob", [2, T], SCR)
    qs_hi, qs_lo = at("qs_hi", [2, 2, P], SCR + 6144, F32R), at("qs_lo", [2, 2, P], SCR + 8192, F32R)
    otok = at("otok", [2, P], SCR + 10240)
    pt_hi, pt_lo = at("pt_hi", [2, T], MODRAW, F32R), at("pt_lo", [2, T], MODRAW + 6144, F32R)

    def mixer_buffers(tag, off, nq, tq, nk, tk, nv, wv):
        out = []
        for n, cols in (("q", [nq, tq]), ("k", [nk, tk]), ("v", [nv, wv])):
            for part in ("hi", "lo"):
                out.append(at(f"{tag}_{n}_{part}", cols, off, F32R))
                off += 4 * int(np.prod(cols))
        return out, off

    l0_qkv, _off = mixer_buffers("l0", Y, 4, T, 1, T, 6, P)
    d_hi, d_lo = at("d_hi", [2, T], _off, F32R), at("d_lo", [2, T], _off + 8 * T, F32R)
    assert _off + 16 * T == H
    l1_qkv, _off = mixer_buffers("l1", XC, 8, S, 2, T, 6, 2 * P)
    assert _off <= H
    s_qkv, _off = mixer_buffers("s", XC, 4, S, 4, S, 4, 4 * P)
    rel = at("rel", [8, 2 * P], _off)
    mask_raw, mask = at("mask_raw", [2, P], HSPARE), at("mask", [2, P], HSPARE + 1024, F32R)
    ident_r = at("ident_r", [P], HSPARE + 2048, F32R)
    o_hi, o_lo = at("o_hi", [4, S], HSPARE, F32R), at("o_lo", [4, S], HSPARE + 16 * S, F32R)

    ps = ctx.enter_context(nc.psum_tensor("ps", [P, 8, 512], F32))
    flat = ps[:].rearrange("p b n -> p (b n)")
    modps = ps[:, 7, 0:144].rearrange("p (n m) -> p n m", m=2)

    raw_landed = [sem(f"raw_landed{i}") for i in range(RING)]
    hi_ready, lo_ready = sem("hi_ready"), sem("lo_ready")
    w_used = sem("w_used")
    mod_landed = [sem(f"mod_landed{i}") for i in range(RING)]
    mod_used = sem("mod_used")
    x_landed, const_landed, late_landed = sem("x_landed"), sem("const_landed"), sem("late_landed")
    setup = sem("setup")
    cact_ready = sem("cact_ready")
    modv_ready = sem("modv_ready")
    n_sq, n_ss, n_rms = sem("n_sq"), sem("n_ss"), sem("n_rms")
    n_t, n_h, h_ready, x_ready, y_zero = sem("n_t"), sem("n_h"), sem("h_ready"), sem("x_ready"), sem("y_zero")
    dve_chain = sem("dve_chain")
    chain = [0]

    def link(dve, ins):
        chain[0] += 1
        ins.then_inc(dve_chain, 1)
        dve.wait_ge(dve_chain, chain[0])

    def load_block(sp, c, d=0):
        if c >= RING:
            sp.wait_ge(lo_ready, c - RING + 1 + d)
        sp.dma_start(raw[:, c % RING, :], A["w_stream"][bass.ds(c + d, 1)].rearrange("o p n -> (o p) n")
                     ).then_inc(raw_landed[c % RING], 16)

    def split_hi(act, c, d=0):
        if c >= NBLK:
            return
        act.wait_ge(raw_landed[c % RING], 16 * (c // RING + 1) + 4 * d)
        if c >= RING:
            act.wait_ge(w_used, c - RING + 1 + d)
        nc.scalar.activation(w_hi[:, c % RING, :], raw[:, c % RING, :], ACT.Copy).then_inc(hi_ready, 1)

    def split_lo(pool, c, d=0):
        if c >= NBLK:
            return
        pool.wait_ge(hi_ready, c + 1 + d)
        nc.gpsimd.tensor_tensor(w_lo[:, c % RING, :], raw[:, c % RING, :], w_hi[:, c % RING, :].bitcast(F32),
                                ALU.subtract).then_inc(lo_ready, 1)

    def repeat(eng, c0, c1, step):
        turns = (c1 - c0) // RING
        if turns > 1:
            with eng.Fori(0, turns) as i:
                for j in range(RING):
                    step(eng, c0 + j, i * RING)
            c0 += turns * RING
        for c in range(c0, c1):
            step(eng, c)

    def tiles(c):
        s = c % RING
        return [(w_hi[:, s, k * P:(k + 1) * P], w_lo[:, s, k * P:(k + 1) * P]) for k in range(8)]

    def product(w, x, outs, first, last):
        for i, (a, b) in enumerate(((0, 0), (0, 1), (1, 0))):
            for out, off, n in outs:
                mm = nc.tensor.matmul(out, w[a], x[b][:, off:off + n], start=first and i == 0, stop=last and i == 2)
        return mm

    def project(x_hi, x_lo, c, outs, ready=None):
        for k, w in enumerate(tiles(c)):
            mm = product(w, (x_hi[:, k, :], x_lo[:, k, :]), outs, k == 0, k == 7)
        return mm

    def load_mod(sp, c, d=0):
        if c >= RING:
            sp.wait_ge(mod_used, c - RING + 1 + d)
        sp.dma_start(modraw[:, c % RING, :], A["mod_stream"][bass.ds(c + d, 1)].rearrange("o p n -> (o p) n")
                     ).then_inc(mod_landed[c % RING], 16)

    def mod_block(pe, c, base, cv, d=0):
        pe.wait_ge(mod_landed[c % RING], 16 * (c // RING + 1) + 4 * d)
        for k in range(KC):
            mm = nc.tensor.matmul(flat[:, bass.ds(7 * 512 + 2 * (c - base) + 2 * d, 2)],
                                  modraw[:, c % RING, k * P:(k + 1) * P], cv[:, k, :], start=k == 0, stop=k == KC - 1)
        mm.then_inc(mod_used, 1)

    def mod_evict(dve, c0, c1, base):
        dve.wait_ge(mod_used, c1)
        for m in range(2):
            ins = nc.vector.tensor_tensor(modv[:, c0 - base:c1 - base, m], modps[:, c0 - base:c1 - base, m],
                                          bmod[:, c0:c1], ALU.add)
        link(dve, ins)

    def vectors(dve, sub, slot, shift, scale, gate, res=1.0):
        for m in range(2):
            if scale is not None:
                nc.vector.scalar_tensor_tensor(out=vec_a[:, slot, :, m], in0=modv[:, scale * KC:scale * KC + KC, m],
                                               scalar=1.0, in1=gpre[:, sub, :], op0=ALU.add, op1=ALU.mult)
                ins = nc.vector.tensor_copy(vec_b[:, slot, :, m], modv[:, shift * KC:shift * KC + KC, m])
            if gate is not None:
                ins = nc.vector.scalar_tensor_tensor(out=vec_g[:, slot, :, m], in0=modv[:, gate * KC:gate * KC + KC, m],
                                                     scalar=res, in1=gpost[:, sub, :], op0=ALU.mult, op1=ALU.mult)
        return ins

    SS_BANK = (0, 1)

    def norm_act(act, name, src, ready):
        base = 8 * before(name)
        for si, (off, n) in enumerate(segs(PASS_SEGS[name])):
            for k in range(KC):
                j = base + 8 * si + k
                ready(act, si, k)
                if j >= 2:
                    act.wait_ge(n_ss, j - 1)
                nc.scalar.activation(sq[:, j % 2, 0:n], src(si, k), ACT.Square).then_inc(n_sq, 1)
            act.wait_ge(n_ss, base + 8 * si + 8)
            nc.scalar.activation(rstd[:, off:off + n], ps[:, SS_BANK[si], 0:n], ACT.Sqrt, scale=1.0 / D,
                                 bias=eps_col[:, 0:1]).then_inc(n_rms, 1)

    def norm_pe(pe, name):
        base = 8 * before(name)
        for si, (off, n) in enumerate(segs(PASS_SEGS[name])):
            for k in range(KC):
                j = base + 8 * si + k
                pe.wait_ge(n_sq, j + 1)
                nc.tensor.matmul(ps[:, SS_BANK[si], 0:n], ones[:, :], sq[:, j % 2, 0:n], start=k == 0,
                                 stop=k == KC - 1).then_inc(n_ss, 1)

    def rms_dve(dve, name, si, off, n):
        dve.wait_ge(n_rms, before(name) + si + 1)
        link(dve, nc.vector.reciprocal(rstd[:, off:off + n], rstd[:, off:off + n]))

    def pre_dve(dve, name, slot, dst_hi, dst_lo):
        hb = 8 * before(name, "_pre")
        if before(name, "_post"):
            dve.wait_ge(x_ready, 8 * before(name, "_post"))
        for si, (off, n) in enumerate(segs(PASS_SEGS[name])):
            rms_dve(dve, name, si, off, n)
            for k in range(KC + 1):
                if k < KC:
                    nc.vector.scalar_tensor_tensor(out=tn[:, k % 2, 0:n], in0=xs[si][:, k, :],
                                                   scalar=vec_a[:, slot, k, si:si + 1], in1=rstd[:, off:off + n],
                                                   op0=ALU.mult, op1=ALU.mult).then_inc(n_t, 1)
                if k >= 1:
                    j = k - 1
                    dve.wait_ge(n_h, hb + 8 * si + j + 1)
                    nc.vector.scalar_tensor_tensor(out=dst_lo[:, j, off:off + n], in0=tn[:, j % 2, 0:n],
                                                   scalar=vec_b[:, slot, j, si:si + 1],
                                                   in1=dst_hi[:, j, off:off + n].bitcast(F32),
                                                   op0=ALU.add, op1=ALU.subtract).then_inc(h_ready, 1)
                    dve.wait_ge(h_ready, hb + 8 * si + j + 1)

    def pre_act(act, name, slot, dst_hi):
        tb, hb = 8 * before(name), 8 * before(name, "_pre")
        for si, (off, n) in enumerate(segs(PASS_SEGS[name])):
            for k in range(KC):
                act.wait_ge(n_t, tb + 8 * si + k + 1)
                nc.scalar.activation(dst_hi[:, k, off:off + n], tn[:, k % 2, 0:n], ACT.Identity,
                                     bias=vec_b[:, slot, k, si:si + 1]).then_inc(n_h, 1)

    def post_dve(dve, name, slot, src):
        tb, xb = 8 * before(name), 8 * before(name, "_post")
        for si, (off, n) in enumerate(segs(PASS_SEGS[name])):
            rms_dve(dve, name, si, off, n)
            for k in range(KC):
                j = xb + 8 * si + k
                if k >= 2 or si:
                    dve.wait_ge(x_ready, j - 1)
                nc.vector.scalar_tensor_tensor(out=tn[:, k % 2, 0:n], in0=src(si, k),
                                               scalar=vec_g[:, slot, k, si:si + 1], in1=rstd[:, off:off + n],
                                               op0=ALU.mult, op1=ALU.mult).then_inc(n_t, 1)

    def post_pool(pool, name):
        tb = 8 * before(name)
        for si, (off, n) in enumerate(segs(PASS_SEGS[name])):
            for k in range(KC):
                pool.wait_ge(n_t, tb + 8 * si + k + 1)
                nc.gpsimd.tensor_tensor(xs[si][:, k, :], xs[si][:, k, :], tn[:, k % 2, 0:n], ALU.add
                                        ).then_inc(x_ready, 1)

    def x_done(name):
        xb = 8 * before(name, "_post")
        prev = PASS_SEGS[PASSES[PASSES.index(name) - 1]]

        def ready(eng, si, k):
            eng.wait_ge(x_ready, xb - 8 * prev + 8 * si + k + 1)
        return ready

    CREDIT = 2

    def ffn_buffers(nseg):
        n = segs(nseg)[-1][0] + segs(nseg)[-1][1]
        tag = f"ffn{nseg}_"
        return dict(hi=at(tag + "hi", [2, n], HID, F32R), lo=at(tag + "lo", [2, n], HID + 8 * n, F32R),
                    silu=at(tag + "silu", [2, n], HID + 16 * n), hid=at(tag + "hid", [2, n], HID + 24 * n))

    FFN_BUFS = {1: ffn_buffers(1), 2: ffn_buffers(2)}

    def ffn(name, nseg, x, acc, mods=None):
        return dict(name=name, c0=FIRST[name], segs=segs(nseg), x=x, y=acc, mods=mods, index=[
            "l0_ffn", "l1_ffn", "s_ffn1", "s_ffn2"].index(name), **FFN_BUFS[nseg])

    def gate_bank(buf, si):
        return ps[:, 3 * buf, 0:S] if si == 0 else ps[:, 3 * buf + 2, 0:C]

    def up_bank(buf, si):
        return ps[:, 3 * buf + 1, 0:S] if si == 0 else ps[:, 3 * buf + 2, C:2 * C]

    def out_bank(f, n, si):
        if len(f["segs"]) == 1:
            return ps[:, 5 + n % 2, 0:S]
        return (ps[:, (6, 3)[n % 2], 0:S], ps[:, (5, 4)[n % 2], 0:C])[si]

    def ffn_groups(eng, f, step):
        n0 = f["c0"] + 2
        with eng.Fori(0, (NG - 1) // 2) as i:
            for half in range(2):
                step(n0 + 6 * half, i * 12, (half, i * 2), False)
        step(n0 + 6 * (NG - 1), 0, (NG - 1, 0), True)

    def ffn_pe(pe, f):
        hid_ready, out_ready, out_free = (sem(f["name"] + s) for s in ("_hid_ready", "_out_ready", "_out_free"))
        ns = len(f["segs"])

        def in_block(c, d, bank, buf):
            pe.wait_ge(lo_ready, c + 1 + d)
            project(f["x"][0], f["x"][1], c, [(bank(buf, si), off, n) for si, (off, n) in enumerate(f["segs"])]
                    ).then_inc(w_used, 1)

        def mods(pair, d, last=False):
            if f["mods"]:
                m0, each, tail, cv = f["mods"]
                for j in range(tail if last else each):
                    mod_block(pe, m0 + each * pair + j, m0, cv, each * d)

        pe.wait_ge(h_ready, f["h_count"])
        in_block(f["c0"], 0, gate_bank, 0)
        in_block(f["c0"] + 1, 0, up_bank, 0)
        mods(0, 0)

        def step(c, d, group, last):
            g, gd = group
            pe.wait_ge(hid_ready, CREDIT + 2 * g + 2 * gd)
            if ns == 2:
                pe.wait_ge(out_free, CREDIT + 8 * g + 8 * gd)
            in_block(c, d, gate_bank, 1)
            in_block(c + 1, d, up_bank, 1)
            mods(2 * g + 1, 2 * gd, last)
            if not last:
                pe.wait_ge(hid_ready, CREDIT + 2 * g + 1 + 2 * gd)
                in_block(c + 2, d, gate_bank, 0)
                in_block(c + 3, d, up_bank, 0)
                mods(2 * g + 2, 2 * gd)
            oa = c + 2 if last else c + 4
            pe.wait_ge(lo_ready, oa + 2 + d)
            pe.wait_ge(hid_ready, CREDIT + 2 * g + 2 + 2 * gd)
            for n in range(KC):
                pe.wait_ge(out_free, CREDIT + 8 * g + n - 1 + 8 * gd)
                outs = [(out_bank(f, n, si), off, w) for si, (off, w) in enumerate(f["segs"])]
                for b in range(2):
                    mm = product(tiles(oa + b)[n], (f["hi"][:, b, :], f["lo"][:, b, :]), outs, b == 0, b == 1)
                if n < KC - 1:
                    mm.then_inc(out_ready, 1)
            mm.then_inc(w_used, 2)

        ffn_groups(pe, f, step)

    def ffn_silu(act, f, c, d, buf):
        act.wait_ge(w_used, c + 2 + d)
        for si, (off, n) in enumerate(f["segs"]):
            nc.scalar.activation(f["silu"][:, buf, off:off + n], gate_bank(buf, si), ACT.Silu
                                 ).then_inc(sem(f["name"] + "_silu"), 1)

    def ffn_hidden_hi(act, f, m, md, out_c, out_d):
        ns = len(f["segs"])
        if out_c is not None:
            act.wait_ge(w_used, out_c + out_d)
        for si, (off, n) in enumerate(f["segs"]):
            act.wait_ge(sem(f["name"] + "_hid"), ns * m + si + 1 + ns * md)
            nc.scalar.activation(f["hi"][:, m % 2, off:off + n], f["hid"][:, m % 2, off:off + n], ACT.Copy
                                 ).then_inc(sem(f["name"] + "_hid_hi"), 1)

    def ffn_act(act, f):
        c0 = f["c0"]
        split_hi(act, c0 + RING)
        split_hi(act, c0 + RING + 1)
        ffn_silu(act, f, c0, 0, 0)
        ffn_hidden_hi(act, f, 0, 0, None, 0)

        def step(c, d, group, last):
            g, gd = group
            split_hi(act, c + RING, d)
            split_hi(act, c + RING + 1, d)
            ffn_silu(act, f, c, d, 1)
            ffn_hidden_hi(act, f, 2 * g + 1, 2 * gd, c, d)
            split_hi(act, c + RING + 2, d)
            split_hi(act, c + RING + 3, d)
            if not last:
                ffn_silu(act, f, c + 2, d, 0)
                split_hi(act, c + RING + 4, d)
                split_hi(act, c + RING + 5, d)
                ffn_hidden_hi(act, f, 2 * g + 2, 2 * gd, c + 6, d)

        ffn_groups(act, f, step)

    def ffn_mult(dve, f, m, md):
        ns = len(f["segs"])
        for si, (off, n) in enumerate(f["segs"]):
            dve.wait_ge(sem(f["name"] + "_silu"), ns * m + si + 1 + ns * md)
            nc.vector.tensor_tensor(f["hid"][:, m % 2, off:off + n], f["silu"][:, m % 2, off:off + n],
                                    up_bank(m % 2, si), ALU.mult).then_inc(sem(f["name"] + "_hid"), 1)

    def ffn_hidden_lo(dve, f, m, md):
        ns = len(f["segs"])
        for si, (off, n) in enumerate(f["segs"]):
            dve.wait_ge(sem(f["name"] + "_hid_hi"), ns * m + si + 1 + ns * md)
            ins = nc.vector.tensor_tensor(f["lo"][:, m % 2, off:off + n], f["hid"][:, m % 2, off:off + n],
                                          f["hi"][:, m % 2, off:off + n].bitcast(F32), ALU.subtract)
        ins.then_inc(sem(f["name"] + "_hid_ready"), 1)

    def ffn_dve(dve, f):
        out_ready, out_free = sem(f["name"] + "_out_ready"), sem(f["name"] + "_out_free")
        dve.sem_inc(sem(f["name"] + "_hid_ready"), CREDIT)
        dve.sem_inc(out_free, CREDIT)
        ffn_mult(dve, f, 0, 0)
        ffn_hidden_lo(dve, f, 0, 0)
        dve.wait_ge(y_zero, f["index"] + 1)

        def step(c, d, group, last):
            g, gd = group
            ffn_mult(dve, f, 2 * g + 1, 2 * gd)
            ffn_hidden_lo(dve, f, 2 * g + 1, 2 * gd)
            if not last:
                ffn_mult(dve, f, 2 * g + 2, 2 * gd)
            dve.wait_ge(out_free, CREDIT + 8 * g + 8 * gd)
            for n in range(KC):
                if n < KC - 1:
                    dve.wait_ge(out_ready, (KC - 1) * g + n + 1 + (KC - 1) * gd)
                else:
                    dve.wait_ge(w_used, (c + 4 if last else c + 6) + d)
                for si, (off, w) in enumerate(f["segs"]):
                    acc = f["y"][:, n, off:off + w]
                    ins = nc.vector.tensor_tensor(acc, acc, out_bank(f, n, si), ALU.add)
                ins.then_inc(out_free, 1)
            if not last:
                ffn_hidden_lo(dve, f, 2 * g + 2, 2 * gd)

        ffn_groups(dve, f, step)

    def ffn_y_ready(f):
        def ready(eng, si, k):
            eng.wait_ge(sem(f["name"] + "_out_free"), CREDIT + KC * (NG - 1) + k + 1)
        return ready

    def out_pe_two(pe, name, x):
        for n in range(KC):
            c = FIRST[name] + n
            pe.wait_ge(lo_ready, c + 1)
            if n >= 4:
                pe.wait_ge(sem(name + "_y"), n - 3)
            project(x[0], x[1], c, [(ps[:, 2 * (n % 4) + si, 0:w], off, w) for si, (off, w) in enumerate(segs(2))]
                    ).then_inc(w_used, 1)

    def out_pe_one(pe, name, x):
        c = FIRST[name]
        with pe.Fori(0, KC // RING) as i:
            for j in range(RING):
                pe.wait_ge(lo_ready, c + j + 1 + i * RING)
                project(x[0], x[1], c + j, [(flat[:, bass.ds(512 * j + i * (512 * RING), 512)], 0, S)]
                        ).then_inc(w_used, 1)

    def out_act(act, name):
        repeat(act, FIRST[name] + RING, FIRST[name] + KC + RING, split_hi)

    def out_dve(dve, name, acc, nseg):
        for n in range(KC):
            dve.wait_ge(w_used, FIRST[name] + n + 1)
            for si, (off, w) in enumerate(segs(nseg)):
                src = ps[:, 2 * (n % 4) + si, 0:w] if nseg == 2 else ps[:, n, 0:w]
                ins = nc.vector.tensor_copy(acc[:, n, off:off + w], src)
            ins.then_inc(sem(name + "_y"), 1)

    def out_y_ready(name):
        def ready(eng, si, k):
            eng.wait_ge(sem(name + "_y"), k + 1)
        return ready

    def pair(i, si, n):
        return ps[:, 2 * (i % 2) + si, 0:n]

    def in_plan(layer):
        q, k, v = ((l0_qkv, l1_qkv)[layer][j:j + 2] for j in (0, 2, 4))
        if layer == 0:
            return ([("qk", k, 0, 1, 2), ("v", v, 0, None, 2)] + [("qk", q, n, 0, 2) for n in range(4)]
                    + [("u", None, g, None, 2) for g in range(4)])
        return ([("qk", k, n, None, 2) for n in range(2)] + [("v", v, n, None, 2) for n in range(2)]
                + [("qk", q, n, None, 1) for n in range(8)])

    def in_stage(layer):
        name = f"l{layer}_in"
        return dict(name=name, plan=in_plan(layer), c0=FIRST[name], norm=layer == 0,
                    **{s: sem(f"{name}_{s}") for s in ["out", "v_lo", "sh", "sin", "q", "hi", "lo"] + (
                        ["sq", "ss", "rms", "qn", "pads", "pool", "d_hi", "d_lo", "mix", "mix_hi", "mix_lo"]
                        if layer == 0 else [])})

    def qk_buf(st, j):
        if st["norm"]:
            return qn, tsh
        return (qraw, tsh) if j % 2 else (qn, sq[:, 0, :])

    SS_IN = (4, 5)

    def in_pe(pe, st, mods=None):
        plan, c0 = st["plan"], st["c0"]
        qk_seen = v_seen = 0
        pending = None

        def head_sums(j):
            for si, (off, n) in enumerate(segs(2)):
                pe.wait_ge(st["sq"], 2 * j + si + 1)
                nc.tensor.matmul(ps[:, SS_IN[si], 0:n], blkones[:, :], sq[:, si, 0:n], start=True, stop=True
                                 ).then_inc(st["ss"], 1)

        for i, (kind, buf, n, gain, ns) in enumerate(plan):
            c = c0 + i
            if i == 0:
                pe.wait_ge(h_ready, st["h_count"])
            pe.wait_ge(lo_ready, c + 1)
            if i >= 2:
                pe.wait_ge(st["out"], i - 1)
                if plan[i - 2][0] == "v":
                    pe.wait_ge(st["v_lo"], v_seen if plan[i - 1][0] != "v" else v_seen - 1)
            if kind == "v":
                v_seen += 1
                for t in range(T // P):
                    out = pair(i, t // 4, 512)[:, (t % 4) * P:(t % 4 + 1) * P]
                    for k, w in enumerate(tiles(c)):
                        for m, (a, b) in enumerate(((0, 0), (0, 1), (1, 0))):
                            mm = nc.tensor.matmul(out, (h_hi, h_lo)[a][:, k, t * P:(t + 1) * P], w[b],
                                                  start=k == 0 and m == 0, stop=k == 7 and m == 2)
                mm.then_inc(w_used, 1)
            else:
                project(h_hi, h_lo, c, [(pair(i, si, w), off, w) for si, (off, w) in enumerate(segs(ns))]
                        ).then_inc(w_used, 1)
            if pending is not None:
                head_sums(pending)
                pending = None
            if kind == "qk":
                if st["norm"]:
                    pending = qk_seen
                qk_seen += 1
            if mods and i < mods[1]:
                if i == 0:
                    pe.wait_ge(modv_ready, 1)
                for m in range(4):
                    mod_block(pe, mods[0] + 4 * i + m, MOD0, mods[2])

    def in_act(act, st):
        plan, c0 = st["plan"], st["c0"]
        j = 0
        vs = 0
        pending = None

        def head_rms(j):
            for si, (off, n) in enumerate(segs(2)):
                act.wait_ge(st["ss"], 2 * j + si + 1)
                nc.scalar.activation(rstd[:, off:off + n], ps[:, SS_IN[si], 0:n], ACT.Sqrt, scale=1.0 / HD,
                                     bias=eps_col[:, 0:1]).then_inc(st["rms"], 1)

        def qk_hi(j, buf, n, ns):
            act.wait_ge(st["q"], j + 1)
            w = segs(ns)[-1][0] + segs(ns)[-1][1]
            nc.scalar.activation(buf[0][:, n, 0:w], qk_buf(st, j)[0][:, 0:w], ACT.Copy).then_inc(st["hi"], 1)

        def pool_hi(g):
            act.wait_ge(st["pool"], g + 1)
            if g >= 2:
                act.wait_ge(st["mix"], g - 1)
            s = (sA, sB)[g % 2]
            nc.scalar.activation(d_hi[:, g % 2, 0:S], s[:, PAD:PAD + S], ACT.Copy)
            nc.scalar.activation(d_hi[:, g % 2, S:T], s[:, S + 3 * PAD:S + 3 * PAD + C], ACT.Copy
                                 ).then_inc(st["d_hi"], 1)

        for i, (kind, buf, n, gain, ns) in enumerate(plan):
            split_hi(act, c0 + i + RING)
            act.wait_ge(w_used, c0 + i + 1)
            if pending is not None and st["norm"]:
                head_rms(pending[0])
            if kind == "qk":
                if st["norm"]:
                    for si, (off, w) in enumerate(segs(2)):
                        if j >= 1:
                            act.wait_ge(st["ss"], 2 * j - 1 + si)
                        nc.scalar.activation(sq[:, si, 0:w], pair(i, si, w), ACT.Square).then_inc(st["sq"], 1)
                dst = qraw if st["norm"] else qk_buf(st, j)[0]
                if st["norm"] and j >= 1:
                    act.wait_ge(st["qn"], j)
                if not st["norm"] and j >= 2:
                    act.wait_ge(st["lo"], j - 1)
                for si, (off, w) in enumerate(segs(ns)):
                    ins = nc.scalar.activation(dst[:, off:off + w], pair(i, si, w), ACT.Copy)
                ins.then_inc(st["out"], 1)
            elif kind == "v":
                for t0, t1, si in ((0, 4, 0), (4, 6, 1)):
                    ins = nc.scalar.activation(buf[0][:, t0:t1, n * P:(n + 1) * P],
                                               pair(i, si, (t1 - t0) * P).rearrange("p (t c) -> p t c", c=P), ACT.Copy)
                ins.then_inc(st["out"], 1)
            if pending is not None:
                qk_hi(*pending)
                pending = None
            if kind == "u":
                if n >= 1:
                    pool_hi(n - 1)
                else:
                    act.wait_ge(st["lo"], j)
                act.wait_ge(st["pads"], 1)
                nc.scalar.activation(upad[:, PAD:PAD + S], pair(i, 0, S), ACT.Copy)
                nc.scalar.activation(upad[:, S + 3 * PAD:S + 3 * PAD + C], pair(i, 1, C), ACT.Copy
                                     ).then_inc(st["out"], 1)
            if kind == "qk":
                pending = (j, buf, n, ns)
                j += 1
        if pending is not None:
            qk_hi(*pending)
        if st["norm"]:
            pool_hi(3)

    def in_dve(dve, st):
        plan = st["plan"]
        j = vs = 0
        for i, (kind, buf, n, gain, ns) in enumerate(plan):
            if kind == "v":
                dve.wait_ge(st["out"], i + 1)
                for t0, t1, si in ((0, 4, 0), (4, 6, 1)):
                    cols = slice(n * P, (n + 1) * P)
                    ins = nc.vector.tensor_tensor(buf[1][:, t0:t1, cols],
                                                  pair(i, si, (t1 - t0) * P).rearrange("p (t c) -> p t c", c=P),
                                                  buf[0][:, t0:t1, cols].bitcast(F32), ALU.subtract)
                ins.then_inc(st["v_lo"], 1)
            if kind == "qk":
                w = segs(ns)[-1][0] + segs(ns)[-1][1]
                q, sh = qk_buf(st, j)
                if st["norm"]:
                    dve.wait_ge(st["rms"], 2 * j + 2)
                    link(dve, nc.vector.reciprocal(rstd[:, :], rstd[:, :]))
                    dve.wait_ge(st["out"], i + 1)
                    nc.vector.scalar_tensor_tensor(out=q[:, 0:w], in0=qraw[:, 0:w], scalar=qk_gain[:, gain:gain + 1],
                                                   in1=rstd[:, 0:w], op0=ALU.mult, op1=ALU.mult).then_inc(st["qn"], 1)
                    dve.wait_ge(st["qn"], j + 1)
                else:
                    dve.wait_ge(st["out"], i + 1)
                nc.vector.stream_shuffle(sh[:, 0:S], q[:, 0:S], ROT).then_inc(st["sh"], 1)
                dve.wait_ge(st["sh"], j + 1)
                link(dve, nc.vector.tensor_tensor(q[:, 0:S], q[:, 0:S], cos[:, :], ALU.mult))
                dve.wait_ge(st["sin"], j + 1)
                nc.vector.tensor_tensor(q[:, 0:S], q[:, 0:S], sh[:, 0:S], ALU.add).then_inc(st["q"], 1)
                dve.wait_ge(st["hi"], j + 1)
                nc.vector.tensor_tensor(buf[1][:, n, 0:w], q[:, 0:w], buf[0][:, n, 0:w].bitcast(F32), ALU.subtract
                                        ).then_inc(st["lo"], 1)
                dve.wait_ge(st["lo"], j + 1)
                j += 1
            if kind == "u":
                pool_mean(dve, st, n, i)

    def pool_mean(dve, st, g, i):
        dve.wait_ge(st["out"], i + 1)
        src, lo, hi = upad, 0, UCOLS
        for level in range(g + 1):
            dst = (sA, sB)[level % 2]
            back, ahead = (1, 0) if level == 0 else (2 ** (level - 1), 2 ** (level - 1))
            lo, hi = lo + back, hi - ahead
            link(dve, nc.vector.tensor_tensor(dst[:, lo:hi], src[:, lo - back:hi - back], src[:, lo + ahead:hi + ahead],
                                              ALU.add))
            src = dst
        for first, n in ((PAD, S), (S + 3 * PAD, C)):
            for e, at_ in ((0, first), (1, first + n - 8)):
                ins = nc.vector.tensor_tensor(src[:, at_:at_ + 8], src[:, at_:at_ + 8], edges[:, g, e, :], ALU.mult)
        link(dve, ins)
        nc.vector.scalar_tensor_tensor(out=src[:, PAD:UCOLS - PAD], in0=src[:, PAD:UCOLS - PAD],
                                       scalar=1.0 / POOL_W[g], in1=upad[:, PAD:UCOLS - PAD], op0=ALU.mult,
                                       op1=ALU.subtract).then_inc(st["pool"], 1)
        dve.wait_ge(st["d_hi"], g + 1)
        nc.vector.tensor_tensor(d_lo[:, g % 2, 0:S], src[:, PAD:PAD + S], d_hi[:, g % 2, 0:S].bitcast(F32), ALU.subtract)
        nc.vector.tensor_tensor(d_lo[:, g % 2, S:T], src[:, S + 3 * PAD:S + 3 * PAD + C],
                                d_hi[:, g % 2, S:T].bitcast(F32), ALU.subtract).then_inc(st["d_lo"], 1)
        dve.wait_ge(st["d_lo"], g + 1)

    def in_pool(pool, st):
        j = 0
        for i, (kind, buf, n, gain, ns) in enumerate(st["plan"]):
            split_lo(pool, st["c0"] + i + RING)
            if kind == "qk":
                q, sh = qk_buf(st, j)
                pool.wait_ge(st["sh"], j + 1)
                nc.gpsimd.tensor_tensor(sh[:, 0:S], sh[:, 0:S], sin[:, :], ALU.mult).then_inc(st["sin"], 1)
                j += 1
            if kind == "u" and n == 0:
                pool.wait_ge(st["lo"], j)
                for k, (a, b) in enumerate(((0, PAD), (PAD + S, S + 3 * PAD), (UCOLS - PAD, UCOLS))):
                    ins = nc.gpsimd.memset(upad[:, a:b], 0.0)
                ins.then_inc(st["pads"], 1)

    def pool_pe(pe, st):
        c = FIRST["l0_pool"]
        pe.wait_ge(lo_ready, c + 1)
        for g in range(4):
            i = len(st["plan"]) + g
            pe.wait_ge(st["d_lo"], g + 1)
            pe.wait_ge(st["out"], i - 1) if g < 2 else pe.wait_ge(st["mix_lo"], g - 1)
            mm = product(tiles(c)[g], (d_hi[:, g % 2, :], d_lo[:, g % 2, :]),
                         [(pair(i, si, w), off, w) for si, (off, w) in enumerate(segs(2))], True, True)
            mm.then_inc(st["mix"] if g < 3 else w_used, 1)

    def pool_out_ready(eng, st, g):
        if g < 3:
            eng.wait_ge(st["mix"], g + 1)
        else:
            eng.wait_ge(w_used, FIRST["l0_pool"] + 1)

    def pool_act(act, st):
        for g in range(4):
            pool_out_ready(act, st, g)
            for si, (off, w) in enumerate(segs(2)):
                ins = nc.scalar.activation(h_hi[:, 4 + g, off:off + w], pair(len(st["plan"]) + g, si, w), ACT.Copy,
                                           scale=pool_scale[:, g:g + 1])
            ins.then_inc(st["mix_hi"], 1)
        split_hi(act, FIRST["l0_pool"] + RING)

    def pool_dve(dve, st):
        for g in range(4):
            dve.wait_ge(st["mix_hi"], g + 1)
            for si, (off, w) in enumerate(segs(2)):
                ins = nc.vector.scalar_tensor_tensor(out=h_lo[:, 4 + g, off:off + w],
                                                     in0=pair(len(st["plan"]) + g, si, w),
                                                     scalar=pool_scale[:, g:g + 1],
                                                     in1=h_hi[:, 4 + g, off:off + w].bitcast(F32),
                                                     op0=ALU.mult, op1=ALU.subtract)
            ins.then_inc(st["mix_lo"], 1)

    def attention(name, units, q, k, v, out, scale, qchunk, kchunk, vcol, outchunk, extra=None, sink=None):
        groups = []
        for x in units:
            nb = len(x[4])
            groups.append([(0, (nb + 1) // 2), ((nb + 1) // 2, nb)] if nb > 1 else [(0, 1)])
        cum = [0]
        for g in groups:
            cum.append(cum[-1] + len(g))
        return dict(name=name, units=units, q=q, k=k, v=v, out=out, scale=scale, qchunk=qchunk, kchunk=kchunk,
                    vcol=vcol, outchunk=outchunk, extra=extra, sink=sink, groups=groups, cum=cum, nu=len(units),
                    **{"s_" + s: sem(f"{name}_{s}") for s in (
                        "staged", "qk", "max", "negm", "p", "t", "hi", "lo", "pv", "rcp", "o", "ot", "m_hi", "m_lo")})

    ATT_ITERS = 4

    def att_loop(eng, body):
        body(0, True, False)
        with eng.Fori(0, ATT_ITERS - 2) as i:
            body(i + 1, False, False)
        body(ATT_ITERS - 1, False, True)

    def ahead(a, c, u, last):
        if u + 2 < a["nu"]:
            return c, u + 2
        return None if last else (c + 1, u + 2 - a["nu"])

    def behind(a, c, u, first, n, size):
        if u >= n:
            return c, u - n
        return None if first else (c - 1, size + u - n)

    def score(u, col, n):
        return flat[:, (u % 2) * 1024 + col:(u % 2) * 1024 + col + n]

    def att_pe(pe, a, free):
        nu, cum = a["nu"], a["cum"]

        def qk(c, u):
            qt, half, _, keys, _, tag = a["units"][u]
            if half == 0:
                pe.wait_ge(a["s_staged"], c * (nu // 2) + qt + 1)
            more = a["extra"](c, a["units"][u]) if a["extra"] else []
            kc = a["kchunk"](c, a["units"][u])
            for col, kcol, w in keys:
                added = [m for m in more if col <= m[0] < col + w]
                for i, (x, z) in enumerate(((0, 0), (0, 1), (1, 0))):
                    mm = nc.tensor.matmul(score(u, col, w), (qs_hi, qs_lo)[x][:, qt % 2, half, :],
                                          a["k"][z][:, kc, kcol:kcol + w], start=i == 0, stop=i == 2 and not added)
                for j, (mcol, mw, lhs, rhs) in enumerate(added):
                    mm = nc.tensor.matmul(score(u, mcol, mw), lhs, rhs, start=False, stop=j == len(added) - 1)
            mm.then_inc(a["s_qk"], 1)

        def turn(c, u, first):
            pe.wait_ge(a["s_p"], c * nu + u + 1)
            if not (first and u == 0):
                pe.wait_ge(a["s_lo"], c * cum[-1] + cum[u])
            for g, (b0, b1) in enumerate(a["groups"][u]):
                for b in range(b0, b1):
                    mm = nc.tensor.transpose(ps[:, 4 + g, (b - b0) * P:(b - b0 + 1) * P],
                                             prob[:, u % 2, b * P:(b + 1) * P], ident[:, :])
                mm.then_inc(a["s_t"], 1)

        def values(c, u, first):
            x = a["units"][u]
            if not (first and u == 0):
                pe.wait_ge(a["s_o"], c * nu + u)
            nb = len(x[4])
            for g, (b0, b1) in enumerate(a["groups"][u]):
                pe.wait_ge(a["s_lo"], c * cum[-1] + cum[u] + g + 1)
                for b in range(b0, b1):
                    for i, (p, z) in enumerate(((0, 0), (0, 1), (1, 0))):
                        mm = nc.tensor.matmul(ps[:, 6, x[1] * HD:(x[1] + 1) * HD],
                                              (pt_hi, pt_lo)[p][:, u % 2, b * P:(b + 1) * P],
                                              a["v"][z][:, x[4][b], a["vcol"](c, x)], start=b == 0 and i == 0,
                                              stop=b == nb - 1 and i == 2)
            mm.then_inc(a["s_pv"], 1)

        def turn_back(c, p, first):
            pe.wait_ge(a["s_o"], c * nu + 2 * p + 2)
            if not (first and p == 0):
                pe.wait_ge(a["s_m_lo"], c * (nu // 2) + p)
            nc.tensor.transpose(ps[:, 7, 0:P], otok[:, p % 2, :], ident[:, :]).then_inc(a["s_ot"], 1)

        def body(c, first, last):
            for u in range(nu):
                turn(c, u, first)
                n = ahead(a, c, u, last)
                if n:
                    qk(*n)
                n = behind(a, c, u, first, 1, nu)
                if n:
                    values(*n, first)
                n = behind(a, c, (u - 1) // 2, first, 1, nu // 2) if u % 2 else None
                if n:
                    turn_back(*n, first)
            if last:
                values(c, nu - 1, False)
                turn_back(c, nu // 2 - 1, False)

        free(pe)
        qk(0, 0)
        qk(0, 1)
        att_loop(pe, body)

    def att_act(act, a):
        nu, cum = a["nu"], a["cum"]

        def exps(c, u):
            act.wait_ge(a["s_negm"], c * nu + u + 1)
            x = a["units"][u]
            w = P * len(x[4])
            e = u % 4
            nc.scalar.activation(prob[:, u % 2, 0:w], score(u, 0, w), ACT.Exp, scale=a["scale"],
                                 bias=negm[:, e:e + 1], accum_out=rsum[:, e:e + 1]).then_inc(a["s_p"], 1)
            if a["sink"]:
                nc.scalar.activation(esink[:, e:e + 1], nsink[:, a["sink"](c, x)], ACT.Exp, scale=-1.0,
                                     bias=negm[:, e:e + 1])

        def m_hi(c, p):
            act.wait_ge(a["s_ot"], c * (nu // 2) + p + 1)
            x = a["units"][2 * p]
            nc.scalar.activation(a["out"][0][:, a["outchunk"](c, x), x[2]:x[2] + P], ps[:, 7, 0:P], ACT.Copy
                                 ).then_inc(a["s_m_hi"], 1)

        def body(c, first, last):
            for u in range(nu):
                if not (first and u < 2):
                    act.wait_ge(a["s_pv"], c * nu + u - 1)
                for g, (b0, b1) in enumerate(a["groups"][u]):
                    act.wait_ge(a["s_t"], c * cum[-1] + cum[u] + g + 1)
                    nc.scalar.activation(pt_hi[:, u % 2, b0 * P:b1 * P], ps[:, 4 + g, 0:(b1 - b0) * P], ACT.Copy
                                         ).then_inc(a["s_hi"], 1)
                n = ahead(a, c, u, last)
                if n:
                    exps(*n)
                n = behind(a, c, (u - 1) // 2, first, 1, nu // 2) if u % 2 else None
                if n:
                    m_hi(*n)
            if last:
                m_hi(c, nu // 2 - 1)

        exps(0, 0)
        exps(0, 1)
        att_loop(act, body)

    def att_dve(dve, a):
        nu, cum = a["nu"], a["cum"]

        def row_max(c, u):
            dve.wait_ge(a["s_qk"], c * nu + u + 1)
            x = a["units"][u]
            e = u % 4
            nc.vector.reduce_max(smax[:, e:e + 1], score(u, 0, P * len(x[4])), AX.X).then_inc(a["s_max"], 1)
            dve.wait_ge(a["s_max"], c * nu + u + 1)
            if a["sink"]:
                ins = nc.vector.tensor_scalar(negm[:, e:e + 1], smax[:, e:e + 1], -a["scale"], nsink[:, a["sink"](c, x)],
                                              ALU.mult, ALU.min)
            else:
                ins = nc.vector.tensor_scalar(negm[:, e:e + 1], smax[:, e:e + 1], -a["scale"], None, ALU.mult)
            ins.then_inc(a["s_negm"], 1)

        def low(c, u, g):
            b0, b1 = a["groups"][u][g]
            dve.wait_ge(a["s_hi"], c * cum[-1] + cum[u] + g + 1)
            nc.vector.tensor_tensor(pt_lo[:, u % 2, b0 * P:b1 * P], ps[:, 4 + g, 0:(b1 - b0) * P],
                                    pt_hi[:, u % 2, b0 * P:b1 * P].bitcast(F32), ALU.subtract).then_inc(a["s_lo"], 1)

        def out(c, u):
            e, steps = u % 4, 2 if a["sink"] else 1
            dve.wait_ge(a["s_pv"], c * nu + u + 1)
            if a["sink"]:
                nc.vector.tensor_tensor(rsum[:, e:e + 1], rsum[:, e:e + 1], esink[:, e:e + 1], ALU.add
                                        ).then_inc(a["s_rcp"], 1)
                dve.wait_ge(a["s_rcp"], steps * (c * nu + u) + 1)
            nc.vector.reciprocal(rinv[:, e:e + 1], rsum[:, e:e + 1]).then_inc(a["s_rcp"], 1)
            dve.wait_ge(a["s_rcp"], steps * (c * nu + u + 1))
            half = a["units"][u][1]
            nc.vector.tensor_scalar(otok[:, (u // 2) % 2, half * HD:(half + 1) * HD], ps[:, 6, half * HD:(half + 1) * HD],
                                    rinv[:, e:e + 1], None, ALU.mult).then_inc(a["s_o"], 1)

        def m_lo(c, p):
            dve.wait_ge(a["s_m_hi"], c * (nu // 2) + p + 1)
            x = a["units"][2 * p]
            n = a["outchunk"](c, x)
            nc.vector.tensor_tensor(a["out"][1][:, n, x[2]:x[2] + P], ps[:, 7, 0:P],
                                    a["out"][0][:, n, x[2]:x[2] + P].bitcast(F32), ALU.subtract).then_inc(a["s_m_lo"], 1)

        def body(c, first, last):
            for u in range(nu):
                low(c, u, 0)
                n = ahead(a, c, u, last)
                if n:
                    row_max(*n)
                if len(a["groups"][u]) > 1:
                    low(c, u, 1)
                n = behind(a, c, u, first, 1, nu)
                if n:
                    out(*n)
                n = behind(a, c, (u - 1) // 2, first, 1, nu // 2) if u % 2 else None
                if n:
                    m_lo(*n)
            if last:
                out(c, nu - 1)
                m_lo(c, nu // 2 - 1)

        row_max(0, 0)
        row_max(0, 1)
        att_loop(dve, body)

    def att_pool(pool, a, ready):
        nt = a["nu"] // 2
        halves = [blkones[:, h * HD:h * HD + 1].to_broadcast([P, P]) for h in range(2)]
        ready(pool)
        def body(c, first, last):
            for qt in range(nt):
                x = a["units"][2 * qt]
                if not (first and qt < 2):
                    pool.wait_ge(a["s_qk"], c * 2 * nt + 2 * qt - 2)
                n = a["qchunk"](c, x)
                for t, src in ((qs_hi, a["q"][0]), (qs_lo, a["q"][1])):
                    for half in range(2):
                        ins = nc.gpsimd.tensor_tensor(t[:, qt % 2, half, :], src[:, n, x[2]:x[2] + P].bitcast(F32),
                                                      halves[half], ALU.mult)
                ins.then_inc(a["s_staged"], 1)

        att_loop(pool, body)

    def m_done(eng, a):
        eng.wait_ge(a["s_m_lo"], ATT_ITERS * a["nu"] // 2)

    l0_att = attention(
        "l0_att",
        [(t, half, t * P, [(0, 0, S), (S, S, C)] if t < NQ else [(0, S, C)], list(range(6)) if t < NQ else [4, 5], None)
         for t in range(T // P) for half in range(2)],
        l0_qkv[0:2], l0_qkv[2:4], l0_qkv[4:6], (h_hi, h_lo), SCALE, lambda c, x: c, lambda c, x: 0,
        lambda c, x: slice(x[1] * HD, (x[1] + 1) * HD), lambda c, x: c)

    def l1_units():
        units = []
        for kc in range(2):
            for t in range(NQ):
                b0, b1 = max(t - 1, 0), min(t + 2, NQ)
                w = (b1 - b0) * P
                keys = [(0, S, C), (C, b0 * P, min(w, C))] + ([(2 * C, b0 * P + C, w - C)] if w > C else [])
                for half in range(2):
                    units.append((kc * NQ + t, half, t * P, keys, [4, 5] + list(range(b0, b1)), (kc, t, b0, b1)))
        return units

    def l1_extra(c, x):
        kc, t, b0, b1 = x[5]
        return [(C + (b - b0) * P, P, ident_r[:, :], mask[:, 0 if b < t else 1, :]) for b in range(b0, b1) if b != t]

    l1_att = attention(
        "l1_att", l1_units(), l1_qkv[0:2], l1_qkv[2:4], l1_qkv[4:6], (n_hi, n_lo), SCALE,
        lambda c, x: c * 2 + x[5][0], lambda c, x: x[5][0],
        lambda c, x: slice((2 * x[5][0] + x[1]) * HD, (2 * x[5][0] + x[1] + 1) * HD), lambda c, x: c * 2 + x[5][0],
        extra=l1_extra, sink=lambda c, x: bass.ds(c * 4 + 2 * x[5][0] + x[1], 1))

    def s_extra(c, x):
        t = x[0]
        head = c * 2 + x[1]
        if t == 0:
            return [(0, P, ident[:, :], rel[:, head, P:2 * P])]
        return [((t - 1) * P, 2 * P, ident[:, :], rel[:, head, :])]

    s_att = attention(
        "s_att", [(t, half, t * P, [(0, 0, (t + 1) * P)], list(range(t + 1)), None) for t in range(NQ) for half in range(2)],
        s_qkv[0:2], s_qkv[2:4], s_qkv[4:6], (o_hi, o_lo), 1.0, lambda c, x: c, lambda c, x: c,
        lambda c, x: bass.ds(c * P + x[1] * HD, HD), lambda c, x: c, extra=s_extra)

    s_hi, s_lo = sem("s_in_hi"), sem("s_in_lo")
    att_done, gated, rec_lo = sem("s_att_done"), sem("s_gated"), sem("s_rec_lo")
    s_sig, s_grs, merged, merged_hi, merged_lo = (sem(n) for n in (
        "s_sig", "s_grs", "s_merged", "s_merged_hi", "s_merged_lo"))

    def bank_of(j, i):
        return flat[:, bass.ds(512 * j + i * (512 * RING), 512)]

    def s_in_pe(pe):
        c0 = FIRST["s_in"]
        pe.wait_ge(h_ready, 8 * before("s1_post", "_pre"))
        for i in range(12):
            pe.wait_ge(lo_ready, c0 + i + 1)
            if i >= 4:
                pe.wait_ge(s_lo, i - 3)
            if i < 8:
                mm = project(n_hi, n_lo, c0 + i, [(ps[:, i % 4, :], 0, S)])
            else:
                for t in range(NQ):
                    for k, w in enumerate(tiles(c0 + i)):
                        for m, (a, b) in enumerate(((0, 0), (0, 1), (1, 0))):
                            mm = nc.tensor.matmul(ps[:, i % 4, t * P:(t + 1) * P], (n_hi, n_lo)[a][:, k, t * P:(t + 1) * P],
                                                  w[b], start=k == 0 and m == 0, stop=k == 7 and m == 2)
            mm.then_inc(w_used, 1)

    def s_in_dst(i, part):
        bank = ps[:, i % 4, :]
        if i < 8:
            return s_qkv[2 * (i // 4) + part][:, i % 4, :], bank
        return (s_qkv[4 + part][:, :, (i - 8) * P:(i - 7) * P], bank.rearrange("p (t c) -> p t c", c=P))

    def s_in_act(act):
        c0 = FIRST["s_in"]
        for i in range(12):
            split_hi(act, c0 + i + RING)
            act.wait_ge(w_used, c0 + i + 1)
            dst, bank = s_in_dst(i, 0)
            nc.scalar.activation(dst, bank, ACT.Copy, scale=SCALE if i < 4 else 1.0).then_inc(s_hi, 1)

    def s_in_dve(dve):
        for i in range(12):
            dve.wait_ge(s_hi, i + 1)
            hi, bank = s_in_dst(i, 0)
            lo, _ = s_in_dst(i, 1)
            nc.vector.scalar_tensor_tensor(out=lo, in0=bank, scalar=SCALE if i < 4 else 1.0, in1=hi.bitcast(F32),
                                           op0=ALU.mult, op1=ALU.subtract).then_inc(s_lo, 1)

    def bias_dve(dve):
        dve.wait_ge(late_landed, 16 * (LATE.index("rel_in") + 1))
        for h in range(8):
            ins = nc.vector.tensor_scalar(rel[:, h, :], rel[:, h, :], relc[:, h:h + 1], None, ALU.subtract)
        link(dve, ins)
        nc.vector.memset(rel[0:HD, :, P + HD:2 * P], -1e30).then_inc(sem("rel_ready"), 1)

    LRU = MODRAW
    lru_wa, lru_wx = at("lru_wa_sb", [KC, P], LRU), at("lru_wx_sb", [KC, P], LRU + KC * P * 4)
    _lru = LRU + 2 * KC * P * 4
    xpad = at("xpad", [S + 8], _lru)
    xconv, gy, rec = (at(n, [2, S], _lru + 4 * (S + 8) + 8 * S * i) for i, n in enumerate(("xconv", "gy", "rec")))
    r_g, i_g, a_g, tau = (at(n, [S], _lru + 4 * (S + 8) + 24 * S + 4 * S * i) for i, n in enumerate(("r_g", "i_g", "a_g", "tau")))
    assert _lru + 4 * (S + 8) + 40 * S <= SCR + 15360
    att = at("att", [KC, S], MIX)
    rec_hi, rec_l = at("rec_hi", [KC, S], MIX + 4 * KC * S, F32R), at("rec_lo", [KC, S], MIX + 8 * KC * S, F32R)
    grs = at("grs", [KC, S], HSPARE)
    sg = at("sg", [2, S], SCR + 8192)
    xp, cv, ga, sig, ex, th, qq, sqr, uu, rc, rhi, gl = (sem("lru_" + n) for n in (
        "xpad", "conv", "gates", "sigmoid", "a", "tanh", "ratio", "sqrt", "u", "rec", "hi", "gelu"))

    def s_atto_pe(pe):
        c0 = FIRST["s_atto"]
        m_done(pe, s_att)
        for b in range(4):
            pe.wait_ge(lo_ready, c0 + b + 1)
            for j in range(2):
                for k in range(4):
                    mm = product(tiles(c0 + b)[4 * j + k], (o_hi[:, k, :], o_lo[:, k, :]), [(ps[:, 2 * b + j, :], 0, S)],
                                 k == 0, k == 3)
            mm.then_inc(w_used, 1)

    def s_atto_dve(dve):
        for b in range(4):
            dve.wait_ge(w_used, FIRST["s_atto"] + b + 1)
            nc.vector.tensor_copy(att[:, 2 * b:2 * b + 2, :], ps[:, 2 * b:2 * b + 2, :]).then_inc(att_done, 1)

    def eight_pe(pe, name, x, free):
        c = FIRST[name]
        with pe.Fori(0, KC // RING) as i:
            for j in range(RING):
                pe.wait_ge(lo_ready, c + j + 1 + i * RING)
                free(i, j)
                project(x[0], x[1], c + j, [(bank_of(j, i), 0, S)]).then_inc(w_used, 1)

    def s_gatt_act(act):
        for n in range(KC):
            split_hi(act, FIRST["s_gatt"] + n + RING)
            act.wait_ge(w_used, FIRST["s_gatt"] + n + 1)
            if n >= 2:
                act.wait_ge(gated, n - 1)
            nc.scalar.activation(sg[:, n % 2, :], ps[:, n, :], ACT.Sigmoid).then_inc(s_sig, 1)

    def s_gatt_dve(dve):
        dve.wait_ge(att_done, 4)
        for n in range(KC):
            dve.wait_ge(s_sig, n + 1)
            nc.vector.tensor_tensor(att[:, n, :], att[:, n, :], sg[:, n % 2, :], ALU.mult).then_inc(gated, 1)

    def s_rec_pe(pe):
        c0 = FIRST["s_rec"]
        pe.wait_ge(late_landed, 16 * (LATE.index("lru_wx_in") + 1))

        def block(c, bank, waits):
            pe.wait_ge(lo_ready, c + 1)
            pe.wait_ge(*waits)
            project(n_hi, n_lo, c, [(ps[:, bank, :], 0, S)]).then_inc(w_used, 1)

        def gates(n):
            pe.wait_ge(cv, n + 1)
            if n >= 2:
                pe.wait_ge(sig, n - 1)
            nc.tensor.matmul(ps[:, 4 + n % 2, :], lru_wa[:, n, :], xconv[:, n % 2, :], start=True, stop=True)
            nc.tensor.matmul(ps[:, 6 + n % 2, :], lru_wx[:, n, :], xconv[:, n % 2, :], start=True, stop=True
                             ).then_inc(ga, 1)

        for n in range(KC):
            block(c0 + 2 * n, n % 2, (xp, n - 1) if n >= 2 else (s_sig, n + 1))
            if n >= 1:
                if n == 1:
                    pe.wait_ge(s_sig, KC)
                gates(n - 1)
            block(c0 + 2 * n + 1, 2 + n % 2, (gl, n - 1) if n >= 2 else (s_sig, 3 + n))
        gates(KC - 1)

    def s_rec_act(act):
        c0 = FIRST["s_rec"]

        def high(n):
            act.wait_ge(rc, n + 1)
            nc.scalar.activation(rec_hi[:, n, :], rec[:, n % 2, :], ACT.Copy).then_inc(rhi, 1)

        for n in range(KC + 1):
            m = n - 1
            if n < KC:
                split_hi(act, c0 + 2 * n + RING)
                act.wait_ge(w_used, c0 + 2 * n + 1)
                if n >= 1:
                    act.wait_ge(cv, n)
                nc.scalar.activation(xpad[:, CONV - 1:CONV - 1 + S], ps[:, n % 2, :], ACT.Copy).then_inc(xp, 1)
            if m >= 0:
                act.wait_ge(ga, m + 1)
                if m >= 1:
                    act.wait_ge(rc, m)
                nc.scalar.activation(r_g[:], ps[:, 4 + m % 2, :], ACT.Sigmoid, bias=lru_ba[:, m:m + 1])
                nc.scalar.activation(i_g[:], ps[:, 6 + m % 2, :], ACT.Sigmoid, bias=lru_bx[:, m:m + 1]
                                     ).then_inc(sig, 1)
                act.wait_ge(sig, m + 1)
                nc.scalar.activation(a_g[:], r_g[:], ACT.Exp, scale=lru_s8[:, m:m + 1]).then_inc(ex, 1)
                nc.scalar.activation(tau[:], r_g[:], ACT.Tanh, scale=lru_n8[:, m:m + 1]).then_inc(th, 1)
            if n < KC:
                split_hi(act, c0 + 2 * n + 1 + RING)
                act.wait_ge(w_used, c0 + 2 * n + 2)
                if n >= 2:
                    act.wait_ge(rc, n - 1)
                nc.scalar.activation(gy[:, n % 2, :], ps[:, 2 + n % 2, :], ACT.Gelu_apprx_tanh).then_inc(gl, 1)
            if m >= 1:
                high(m - 1)
            if m >= 0:
                act.wait_ge(qq, m + 1)
                nc.scalar.activation(tau[:], tau[:], ACT.Sqrt, scale=2.0).then_inc(sqr, 1)
        high(KC - 1)

    def s_rec_dve(dve):
        link(dve, nc.vector.memset(xpad[:, 0:CONV - 1], 0.0))

        def low(n):
            dve.wait_ge(rhi, n + 1)
            nc.vector.tensor_tensor(rec_l[:, n, :], rec[:, n % 2, :], rec_hi[:, n, :].bitcast(F32), ALU.subtract
                                    ).then_inc(rec_lo, 1)
            dve.wait_ge(rec_lo, n + 1)

        for n in range(KC + 1):
            m = n - 1
            if n < KC:
                dve.wait_ge(xp, n + 1)
                if n >= 2:
                    dve.wait_ge(ga, n - 1)
                x = xconv[:, n % 2, :]
                link(dve, nc.vector.tensor_scalar(x, xpad[:, 0:S], conv_w[:, n, 0:1], conv_b[:, n:n + 1], ALU.mult, ALU.add))
                for j in range(1, CONV):
                    ins = nc.vector.scalar_tensor_tensor(out=x, in0=xpad[:, j:j + S], scalar=conv_w[:, n, j:j + 1], in1=x,
                                                         op0=ALU.mult, op1=ALU.add)
                    if j < CONV - 1:
                        link(dve, ins)
                ins.then_inc(cv, 1)
            if m >= 0:
                dve.wait_ge(th, m + 1)
                link(dve, nc.vector.tensor_scalar(r_g[:], tau[:], 1.0, None, ALU.add))
                link(dve, nc.vector.reciprocal(r_g[:], r_g[:]))
                nc.vector.tensor_tensor(tau[:], tau[:], r_g[:], ALU.mult).then_inc(qq, 1)
                link(dve, nc.vector.tensor_tensor(i_g[:], i_g[:], xconv[:, m % 2, :], ALU.mult))
                if m >= 1:
                    low(m - 1)
                dve.wait_ge(sqr, m + 1)
                link(dve, nc.vector.tensor_tensor(i_g[:], i_g[:], tau[:], ALU.mult))
                h = rec[:, m % 2, :]
                link(dve, nc.vector.tensor_tensor_scan(h, a_g[:], i_g[:], 0.0, ALU.mult, ALU.add))
                dve.wait_ge(gl, m + 1)
                nc.vector.tensor_tensor(h, h, gy[:, m % 2, :], ALU.mult).then_inc(rc, 1)
                dve.wait_ge(rc, m + 1)
        low(KC - 1)

    def s_grec_act(act):
        for n in range(KC):
            split_hi(act, FIRST["s_grec"] + n + RING)
            act.wait_ge(w_used, FIRST["s_grec"] + n + 1)
            nc.scalar.activation(grs[:, n, :], ps[:, n, :], ACT.Sigmoid).then_inc(s_grs, 1)

    mg = at("mg", [2, S], SCR)

    def s_reco_act(act):
        for n in range(KC):
            split_hi(act, FIRST["s_reco"] + n + RING)
            act.wait_ge(merged, n + 1)
            nc.scalar.activation(n_hi[:, n, :], att[:, n, :], ACT.Copy).then_inc(merged_hi, 1)

    def s_reco_dve(dve):
        for n in range(KC + 1):
            if n < KC:
                dve.wait_ge(w_used, FIRST["s_reco"] + n + 1)
                dve.wait_ge(s_grs, n + 1)
                link(dve, nc.vector.tensor_tensor(mg[:, n % 2, :], ps[:, n, :], grs[:, n, :], ALU.mult))
                nc.vector.tensor_tensor(att[:, n, :], att[:, n, :], mg[:, n % 2, :], ALU.add).then_inc(merged, 1)
                dve.wait_ge(merged, n + 1)
            if n >= 1:
                dve.wait_ge(merged_hi, n)
                nc.vector.tensor_tensor(n_lo[:, n - 1, :], att[:, n - 1, :], n_hi[:, n - 1, :].bitcast(F32), ALU.subtract
                                        ).then_inc(merged_lo, 1)

    sp_exp, sp_u_ready = sem("softplus_exp"), sem("softplus_u")
    sp_abs, sp_neg, sp_e, sp_u, sp_l, sp_m, sp_d = (at("sp" + n, [KC], SCR + 13312 + 32 * i) for i, n in enumerate(
        ("_abs", "_neg", "_e", "_u", "_l", "_m", "_d")))

    def softplus_dve(dve):
        lam = lru_s8[:]
        link(dve, nc.vector.tensor_scalar(nsink[:], nsink[:], -1.0, None, ALU.mult))
        link(dve, nc.vector.tensor_scalar(sp_neg[:], lam, -1.0, None, ALU.mult))
        nc.vector.tensor_tensor(sp_abs[:], sp_neg[:], lam, ALU.max).then_inc(setup, 1)
        dve.wait_ge(sp_exp, 1)
        nc.vector.tensor_scalar(sp_u[:], sp_e[:], 1.0, None, ALU.add).then_inc(sp_u_ready, 1)
        dve.wait_ge(sp_u_ready, 1)
        link(dve, nc.vector.tensor_scalar(sp_m[:], sp_u[:], 1.0, None, ALU.is_equal))
        link(dve, nc.vector.scalar_tensor_tensor(out=sp_d[:], in0=sp_u[:], scalar=1.0, in1=sp_m[:], op0=ALU.subtract,
                                                 op1=ALU.add))
        link(dve, nc.vector.reciprocal(sp_d[:], sp_d[:]))
        link(dve, nc.vector.tensor_tensor(sp_d[:], sp_d[:], sp_e[:], ALU.mult))
        link(dve, nc.vector.tensor_tensor(sp_m[:], sp_m[:], sp_e[:], ALU.mult))
        dve.wait_ge(sp_exp, 2)
        link(dve, nc.vector.tensor_tensor(sp_d[:], sp_d[:], sp_l[:], ALU.mult))
        link(dve, nc.vector.tensor_tensor(sp_d[:], sp_d[:], sp_m[:], ALU.add))
        link(dve, nc.vector.scalar_tensor_tensor(out=sp_d[:], in0=sp_neg[:], scalar=0.0, in1=sp_d[:], op0=ALU.max,
                                                 op1=ALU.add))
        link(dve, nc.vector.tensor_scalar(lru_n8[:], sp_d[:], LRU_C, None, ALU.mult))
        link(dve, nc.vector.tensor_scalar(lru_s8[:], sp_d[:], -LRU_C, None, ALU.mult))

    l0_in, l1_in = in_stage(0), in_stage(1)
    for st, name in ((l0_in, "l0_mix_post"), (l1_in, "l1_mix_post")):
        st["h_count"] = 8 * before(name, "_pre")
    MODS_L0, MODS_L1, MODS_S = (MOD_FIRST, 8, cvec), (MOD1, 2, 6, cvec), (MOD2, 3, 9, cvec2)
    l0_ffn = ffn("l0_ffn", 2, (h_hi, h_lo), y, MODS_L1)
    l1_ffn = ffn("l1_ffn", 1, (n_hi, n_lo), y1, MODS_S)
    s_ffn1 = ffn("s_ffn1", 1, (n_hi, n_lo), y1)
    s_ffn2 = ffn("s_ffn2", 1, (n_hi, n_lo), y1)
    for f, name in ((l0_ffn, "l0_ffn_post"), (l1_ffn, "l1_ffn_post"), (s_ffn1, "s0_post"), (s_ffn2, "s2_post")):
        f["h_count"] = 8 * before(name, "_pre")
    LATE = ["mask_in", "rel_in", "lru_wa_in", "lru_wx_in"]

    def stream_x(si, k):
        return xs[si][:, k, :]

    def stream_y(si, k):
        off, n = segs(2)[si]
        return y[:, k, off:off + n]

    def stream_y1(si, k):
        return y1[:, k, :]

    block = ctx.enter_context(nc.Block())

    @block.sync
    def _(sp):
        sp.dma_start(loaded[:], A["consts"]).then_inc(const_landed, 16)
        for c in range(RING):
            load_mod(sp, c)
        sp.dma_start(xl[:], A["x_in"]).then_inc(x_landed, 16)
        sp.dma_start(xc[:], A["ctx_in"]).then_inc(x_landed, 16)
        for c in range(RING):
            load_block(sp, c)
        for c in range(RING, MOD_FIRST):
            load_mod(sp, c)

        def stage(name):
            count = dict(STAGES)[name]
            repeat(sp, FIRST[name] + RING, min(FIRST[name] + count + RING, NBLK), load_block)

        def ffn_stream(f):
            def mods(pair, d):
                if f["mods"]:
                    m0, each, _, _ = f["mods"]
                    for j in range(each):
                        load_mod(sp, m0 + each * pair + j, each * d)

            if f["mods"]:
                sp.wait_ge(w_used, f["c0"] - 7)
            mods(0, 0)
            load_block(sp, f["c0"] + RING)
            load_block(sp, f["c0"] + RING + 1)
            mods(1, 0)

            def step(c, d, group, last):
                g, gd = group
                for j in range(2 if last else 4):
                    if c + RING + j < NBLK:
                        load_block(sp, c + RING + j, d)
                if not last:
                    mods(2 * g + 2, 2 * gd)
                for j in range(2):
                    cj = c + RING + (2 if last else 4) + j
                    if cj < NBLK:
                        load_block(sp, cj, d)
                if not last:
                    mods(2 * g + 3, 2 * gd)

            ffn_groups(sp, f, step)
            if f["mods"]:
                extra = f["mods"][2] - f["mods"][1]
                for j in range(extra):
                    load_mod(sp, f["mods"][0] + f["mods"][1] * (2 * NG) + j)

        for i in range(10):
            for j in range(4 if i < 8 else 0):
                load_mod(sp, MOD_FIRST + 4 * i + j)
            load_block(sp, FIRST["l0_in"] + RING + i)
        load_block(sp, FIRST["l0_pool"] + RING)
        stage("l0_out")
        ffn_stream(l0_ffn)
        stage("l1_in")
        sp.wait_ge(w_used, FIRST["l1_out"])
        sp.dma_start(mask_raw[:], A["mask_in"]).then_inc(late_landed, 16)
        stage("l1_out")
        ffn_stream(l1_ffn)
        ffn_stream(s_ffn1)
        sp.wait_ge(w_used, FIRST["s_in"])
        sp.dma_start(rel[:], A["rel_in"]).then_inc(late_landed, 16)
        stage("s_in")
        stage("s_atto")
        sp.wait_ge(w_used, FIRST["s_atto"] + 1)
        sp.dma_start(lru_wa[:], A["lru_wa_in"]).then_inc(late_landed, 16)
        sp.dma_start(lru_wx[:], A["lru_wx_in"]).then_inc(late_landed, 16)
        for name in ("s_gatt", "s_rec", "s_grec", "s_reco", "s_out"):
            stage(name)
        ffn_stream(s_ffn2)
        sp.wait_ge(x_ready, 8 * (before("s2_post", "_post") + 1))
        sp.dma_start(A["out"], xl[:]).then_inc(sem("out_stored"), 16)
        sp.wait_ge(sem("out_stored"), 16)

    @block.scalar
    def _(act):
        act.wait_ge(const_landed, 16)
        for cv_ in (cvec, cvec2):
            ins = nc.scalar.activation(cv_[:], cv_[:], ACT.Silu)
        ins.then_inc(cact_ready, 1)
        act.wait_ge(setup, 2)
        nc.scalar.activation(sp_e[:], sp_abs[:], ACT.Exp, scale=-1.0).then_inc(sp_exp, 1)
        act.wait_ge(sp_u_ready, 1)
        nc.scalar.activation(sp_l[:], sp_u[:], ACT.Ln).then_inc(sp_exp, 1)
        for c in range(RING):
            split_hi(act, c)
        norm_act(act, "l0_mix_pre", stream_x, lambda eng, si, k: eng.wait_ge(x_landed, 32))
        pre_act(act, "l0_mix_pre", 0, h_hi)
        in_act(act, l0_in)
        pool_act(act, l0_in)
        att_act(act, l0_att)
        out_act(act, "l0_out")
        norm_act(act, "l0_mix_post", stream_y, out_y_ready("l0_out"))
        norm_act(act, "l0_ffn_pre", stream_x, x_done("l0_ffn_pre"))
        pre_act(act, "l0_ffn_pre", 1, h_hi)
        ffn_act(act, l0_ffn)
        norm_act(act, "l0_ffn_post", stream_y, ffn_y_ready(l0_ffn))
        norm_act(act, "l1_mix_pre", stream_x, x_done("l1_mix_pre"))
        pre_act(act, "l1_mix_pre", 0, h_hi)
        in_act(act, l1_in)
        att_act(act, l1_att)
        out_act(act, "l1_out")
        norm_act(act, "l1_mix_post", stream_y1, out_y_ready("l1_out"))
        norm_act(act, "l1_ffn_pre", stream_x, x_done("l1_ffn_pre"))
        pre_act(act, "l1_ffn_pre", 1, n_hi)
        ffn_act(act, l1_ffn)
        norm_act(act, "l1_ffn_post", stream_y1, ffn_y_ready(l1_ffn))
        norm_act(act, "s0_pre", stream_x, x_done("s0_pre"))
        pre_act(act, "s0_pre", 0, n_hi)
        ffn_act(act, s_ffn1)
        norm_act(act, "s0_post", stream_y1, ffn_y_ready(s_ffn1))
        norm_act(act, "s1_pre", stream_x, x_done("s1_pre"))
        pre_act(act, "s1_pre", 1, n_hi)
        s_in_act(act)
        att_act(act, s_att)
        repeat(act, FIRST["s_atto"] + RING, FIRST["s_gatt"] + RING, split_hi)
        s_gatt_act(act)
        s_rec_act(act)
        s_grec_act(act)
        s_reco_act(act)
        out_act(act, "s_out")
        norm_act(act, "s1_post", stream_y1, out_y_ready("s_out"))
        norm_act(act, "s2_pre", stream_x, x_done("s2_pre"))
        pre_act(act, "s2_pre", 2, n_hi)
        ffn_act(act, s_ffn2)
        norm_act(act, "s2_post", stream_y1, ffn_y_ready(s_ffn2))

    @block.vector
    def _(dve):
        dve.wait_ge(const_landed, 16)
        softplus_dve(dve)
        mod_evict(dve, MOD0, MOD_FIRST, MOD0)
        vectors(dve, 0, 0, 0, 1, None).then_inc(modv_ready, 1)
        pre_dve(dve, "l0_mix_pre", 0, h_hi, h_lo)
        in_dve(dve, l0_in)
        pool_dve(dve, l0_in)
        mod_evict(dve, MOD_FIRST, MOD1, MOD0)
        vectors(dve, 0, 0, None, None, 2)
        vectors(dve, 1, 1, 3, 4, 5)
        att_dve(dve, l0_att)
        out_dve(dve, "l0_out", y, 2)
        post_dve(dve, "l0_mix_post", 0, stream_y)
        pre_dve(dve, "l0_ffn_pre", 1, h_hi, h_lo)
        ffn_dve(dve, l0_ffn)
        mod_evict(dve, MOD1, MOD2, MOD1)
        post_dve(dve, "l0_ffn_post", 1, stream_y)
        dve.wait_ge(x_ready, 8 * before("l1_mix_pre", "_post"))
        vectors(dve, 2, 0, 0, 1, 2)
        vectors(dve, 3, 1, 3, 4, 5)
        pre_dve(dve, "l1_mix_pre", 0, h_hi, h_lo)
        in_dve(dve, l1_in)
        dve.wait_ge(late_landed, 16)
        nc.vector.tensor_copy(mask[:], mask_raw[:])
        nc.vector.tensor_copy(ident_r[:], ident[:]).then_inc(sem("mask_ready"), 1)
        att_dve(dve, l1_att)
        out_dve(dve, "l1_out", y1, 1)
        post_dve(dve, "l1_mix_post", 0, stream_y1)
        pre_dve(dve, "l1_ffn_pre", 1, n_hi, n_lo)
        ffn_dve(dve, l1_ffn)
        mod_evict(dve, MOD2, NMOD, MOD2)
        post_dve(dve, "l1_ffn_post", 1, stream_y1)
        dve.wait_ge(x_ready, 8 * before("s0_pre", "_post"))
        for sub, res in enumerate((0.5, 1.0, 0.5)):
            vectors(dve, 4 + sub, sub, 3 * sub, 3 * sub + 1, 3 * sub + 2, res)
        pre_dve(dve, "s0_pre", 0, n_hi, n_lo)
        ffn_dve(dve, s_ffn1)
        post_dve(dve, "s0_post", 0, stream_y1)
        pre_dve(dve, "s1_pre", 1, n_hi, n_lo)
        s_in_dve(dve)
        bias_dve(dve)
        att_dve(dve, s_att)
        s_atto_dve(dve)
        s_gatt_dve(dve)
        s_rec_dve(dve)
        s_reco_dve(dve)
        out_dve(dve, "s_out", y1, 1)
        post_dve(dve, "s1_post", 1, stream_y1)
        pre_dve(dve, "s2_pre", 2, n_hi, n_lo)
        ffn_dve(dve, s_ffn2)
        post_dve(dve, "s2_post", 2, stream_y1)

    @block.gpsimd
    def _(pool):
        nc.gpsimd.memset(ones[:], 1.0)
        nc.gpsimd.memset(eps_col[:], EPS).then_inc(setup, 1)

        def stage(c0, c1):
            repeat(pool, c0 + RING, min(c1 + RING, NBLK), split_lo)

        def ffn_stage(f, pre_name, n):
            pool.wait_ge(n_t, 8 * before(pre_name))
            nc.gpsimd.memset(f["y"][:, :, 0:n], 0.0).then_inc(y_zero, 1)
            stage(f["c0"], f["c0"] + FFN_BLOCKS)

        repeat(pool, 0, RING, split_lo)
        in_pool(pool, l0_in)
        split_lo(pool, FIRST["l0_pool"] + RING)
        att_pool(pool, l0_att, lambda eng: eng.wait_ge(l0_in["mix_lo"], 4))
        stage(FIRST["l0_out"], FIRST["l0_ffn"])
        post_pool(pool, "l0_mix_post")
        ffn_stage(l0_ffn, "l0_ffn_pre", T)
        post_pool(pool, "l0_ffn_post")
        in_pool(pool, l1_in)
        att_pool(pool, l1_att, lambda eng: eng.wait_ge(l1_in["lo"], 10))
        stage(FIRST["l1_out"], FIRST["l1_ffn"])
        post_pool(pool, "l1_mix_post")
        ffn_stage(l1_ffn, "l1_ffn_pre", S)
        post_pool(pool, "l1_ffn_post")
        ffn_stage(s_ffn1, "s0_pre", S)
        post_pool(pool, "s0_post")
        stage(FIRST["s_in"], FIRST["s_atto"])
        att_pool(pool, s_att, lambda eng: eng.wait_ge(s_lo, 12))
        stage(FIRST["s_atto"], FIRST["s_ffn2"])
        post_pool(pool, "s1_post")
        ffn_stage(s_ffn2, "s2_pre", S)
        post_pool(pool, "s2_post")

    @block.tensor
    def _(pe):
        pe.wait_ge(cact_ready, 1)
        for c in range(MOD_FIRST):
            mod_block(pe, c, MOD0, cvec)
        pe.wait_ge(setup, 2)
        norm_pe(pe, "l0_mix_pre")
        in_pe(pe, l0_in, MODS_L0)
        pool_pe(pe, l0_in)

        def l0_free(pe):
            pe.wait_ge(l0_in["mix_lo"], 4)

        att_pe(pe, l0_att, l0_free)
        m_done(pe, l0_att)
        out_pe_two(pe, "l0_out", (h_hi, h_lo))
        pe.wait_ge(sem("l0_out_y"), 5)
        norm_pe(pe, "l0_mix_post")
        norm_pe(pe, "l0_ffn_pre")
        ffn_pe(pe, l0_ffn)
        norm_pe(pe, "l0_ffn_post")
        norm_pe(pe, "l1_mix_pre")
        in_pe(pe, l1_in)

        def l1_free(pe):
            pe.wait_ge(l1_in["out"], 12)
            pe.wait_ge(sem("mask_ready"), 1)

        att_pe(pe, l1_att, l1_free)
        m_done(pe, l1_att)
        out_pe_one(pe, "l1_out", (n_hi, n_lo))
        norm_pe(pe, "l1_mix_post")
        norm_pe(pe, "l1_ffn_pre")
        ffn_pe(pe, l1_ffn)
        norm_pe(pe, "l1_ffn_post")
        norm_pe(pe, "s0_pre")
        ffn_pe(pe, s_ffn1)
        norm_pe(pe, "s0_post")
        norm_pe(pe, "s1_pre")
        s_in_pe(pe)

        def s_free(pe):
            pe.wait_ge(s_lo, 12)
            pe.wait_ge(sem("rel_ready"), 1)

        att_pe(pe, s_att, s_free)
        s_atto_pe(pe)
        eight_pe(pe, "s_gatt", (n_hi, n_lo), lambda i, j: pe.wait_ge(att_done, i * 2 + j // 2 + 1))
        s_rec_pe(pe)

        def grec_free(i, j):
            pe.wait_ge(gl, KC)
            pe.wait_ge(sig, i * (KC - 1) + 1)

        eight_pe(pe, "s_grec", (n_hi, n_lo), grec_free)
        pe.wait_ge(rec_lo, KC)
        eight_pe(pe, "s_reco", (rec_hi, rec_l), lambda i, j: pe.wait_ge(s_grs, i * RING + j + 1))
        pe.wait_ge(merged_lo, KC)
        out_pe_one(pe, "s_out", (n_hi, n_lo))
        norm_pe(pe, "s1_post")
        norm_pe(pe, "s2_pre")
        ffn_pe(pe, s_ffn2)
        norm_pe(pe, "s2_post")


INPUTS = (("x_in", [P, KC, S]), ("ctx_in", [P, KC, C]), ("consts", [P, PACKED]), ("w_stream", [NBLK, P, BLK]),
          ("mod_stream", [NMOD, P, BLK]), ("mask_in", [P, 2, P]), ("rel_in", [P, 8, 2 * P]),
          ("lru_wa_in", [P, KC, P]), ("lru_wx_in", [P, KC, P]))


def kernel(**inputs):
    import concourse.bacc as _bacc
    from concourse.bass_utils import run_bass_kernel_spmd as _run

    a = {k: np.asarray(v) for k, v in inputs.items()}

    def chunks(v):
        v = v.reshape(v.shape[:-1] + (v.shape[-1] // P, P))
        return np.moveaxis(v, -1, 0)

    def tokens(x):
        return np.ascontiguousarray(x.T.reshape(-1, P, x.shape[0]).transpose(1, 0, 2))

    def blocks(w):
        k, n = w.shape
        return w.reshape(k // P, P, n // P, P).transpose(2, 1, 0, 3)

    def heads(*hs):
        return np.concatenate([np.arange(h * HD, (h + 1) * HD) for h in hs])

    stream = np.empty((NBLK, P, 8, P), np.float32)

    def put(name, *parts):
        c = FIRST[name]
        for part in parts:
            stream[c:c + len(part)] = part
            c += len(part)
        assert c == FIRST[name] + dict(STAGES)[name]

    def put_ffn(name, w_in, w_out):
        gate, up = blocks(w_in[:, :FH]), blocks(w_in[:, FH:])
        out = w_out.reshape(NH, 1, P, 8, P)
        order = [gate[0:1], up[0:1]]
        for g in range(NG):
            b = 2 * g + 1
            order += [gate[b:b + 1], up[b:b + 1]]
            if g < NG - 1:
                order += [gate[b + 1:b + 2], up[b + 1:b + 2]]
            order += [out[2 * g], out[b]]
        put(name, *order)

    we, weo, wo, woo = a["we_in"][0], a["we_out"][0], a["wo_in"][0], a["wo_out"][0]
    q0 = np.concatenate([heads(c, c + 4) for c in range(4)])
    put("l0_in", blocks(we[:, 512:640]), blocks(we[:, 640:768]), blocks(we[:, q0]), blocks(we[:, 768:]))
    stream[FIRST["l0_pool"]] = 0.0
    stream[FIRST["l0_pool"], :, 0:4] = a["we_pool"][0].transpose(1, 0, 2)
    put("l0_out", blocks(np.concatenate([weo[q0], weo[512:]])))
    q1 = np.concatenate([heads(8 * (ci % 2) + ci // 2, 8 * (ci % 2) + 4 + ci // 2) for ci in range(8)])
    put("l1_in", blocks(wo[:, 1024:1280]), blocks(wo[:, 1280:1536]), blocks(wo[:, q1]))
    put("l1_out", blocks(woo[q1]))
    put_ffn("l0_ffn", a["w_ffn_in"][0], a["w_ffn_out"][0])
    put_ffn("l1_ffn", a["w_ffn_in"][1], a["w_ffn_out"][1])
    put_ffn("s_ffn1", a["ffn1_w_gu_2"][0], a["ffn1_w_down_2"][0])
    put_ffn("s_ffn2", a["ffn2_w_gu_2"][0], a["ffn2_w_down_2"][0])
    ws = blocks(a["w_in_2"][0])
    put("s_in", ws[0:12])
    xr, yr, ga, gr = ws[12:20], ws[20:28], ws[28:36], ws[36:44]
    atto = blocks(a["w_att_o_2"][0])
    put("s_atto", np.concatenate([atto[0::2], atto[1::2]], axis=2))
    put("s_gatt", ga)
    put("s_rec", np.stack([xr, yr], 1).reshape(16, P, 8, P))
    put("s_grec", gr)
    put("s_reco", blocks(a["w_rec_o_2"][0]))
    put("s_out", blocks(a["w_out_2"][0]))
    mods = np.concatenate([blocks(a["w_mod"][0]), blocks(a["w_mod"][1]), blocks(a["w_ada_2"][0])])

    p = np.arange(P)
    ident = np.eye(P, dtype=np.float32)
    blkones = (p[:, None] // HD == p[None, :] // HD).astype(np.float32)
    freqs = 10000.0 ** (-np.arange(16) / 16)
    t = np.arange(S)
    pos = np.where((p % HD < 32)[:, None], t[None, :] // 64, t[None, :] % 64)
    ang = (pos.astype(np.float32) * freqs[p % 16].astype(np.float32)[:, None]).astype(np.float32)
    cos = np.cos(ang).astype(np.float32)
    sin = (np.sin(ang) * np.where(p % 32 < 16, -1.0, 1.0)[:, None]).astype(np.float32)
    edges = np.ones((4, 2, 8), np.float32)
    for g, w in enumerate(POOL_W):
        for e in range(8):
            edges[g, 0, e] = w / (e + w - w // 2) if e < w // 2 else 1.0
            left = 7 - e
            edges[g, 1, e] = w / (w // 2 + min(left + 1, w - w // 2))
    prev = np.where(p[None, :] >= p[:, None], 0.0, MASKED)
    nxt = np.where(p[None, :] <= p[:, None], 0.0, MASKED)

    def pair(v0, v1):
        return np.stack([chunks(v0), chunks(v1)], axis=-1)

    def rows(v):
        return np.broadcast_to(v.reshape(1, -1), (P, v.size))

    gp = np.stack([a["g_pre_mix"][0], a["g_pre_ffn"][0], a["g_pre_mix"][1], a["g_pre_ffn"][1], *a["norm_pre_2"][0]])
    gq = np.stack([a["g_post_mix"][0], a["g_post_ffn"][0], a["g_post_mix"][1], a["g_post_ffn"][1], *a["norm_post_2"][0]])
    sink = a["wo_sink"][0][[8 * (ci % 2) + 4 * half + ci // 2 for ci in range(8) for half in range(2)]]
    rb = a["rel_bias_2"][0]
    packed = dict(
        ident=ident, blkones=blkones, cos=cos, sin=sin, cvec=pair(a["c"][0], a["c_ctx"]),
        cvec2=pair(a["c_2"][0], a["c_2"][0]),
        bmod=chunks(np.concatenate([a["b_mod"][0], a["b_mod"][1], a["b_ada_2"][0]])), gpre=chunks(gp), gpost=chunks(gq),
        qk_gain=np.stack([np.tile(a["we_q_gain"][0], 2), np.tile(a["we_k_gain"][0], 2)], axis=1),
        pool_scale=chunks(a["we_pool_scale"][0]), edges=rows(edges), nsink=rows(sink), relc=rows(rb[:, 256]),
        conv_w=np.moveaxis(chunks(a["conv_w_2"][0]), 1, 2), conv_b=chunks(a["conv_b_2"][0]),
        lru_ba=chunks(a["lru_ba_2"][0]), lru_bx=chunks(a["lru_bx_2"][0]), lru_s8=chunks(a["lru_lambda_2"][0]))
    consts = np.zeros((P, PACKED), np.float32)
    off = 0
    for name, cols in CONSTS:
        n = int(np.prod(cols))
        consts[:, off:off + n] = packed[name].reshape(P, n)
        off += padded(cols)

    index = np.minimum(256 + p[:, None] - np.arange(2 * P)[None, :], 256)
    rel = np.ascontiguousarray(rb[:, index].transpose(1, 0, 2))

    def diagonal(w):
        out = np.zeros((P, KC, P), np.float32)
        out[0:HD, :, 0:HD] = w[0::2].transpose(1, 0, 2)
        out[HD:P, :, HD:P] = w[1::2].transpose(1, 0, 2)
        return out

    arrays = dict(
        x_in=tokens(a["x"][0]), ctx_in=tokens(a["ctx"][0]), consts=consts, w_stream=stream.reshape(NBLK, P, BLK),
        mod_stream=np.ascontiguousarray(mods).reshape(NMOD, P, BLK),
        mask_in=np.stack([prev, nxt], axis=1).astype(np.float32), rel_in=rel,
        lru_wa_in=diagonal(a["lru_wa_2"][0]), lru_wx_in=diagonal(a["lru_wx_2"][0]))

    nc = _bacc.Bacc("TRN2", target_bir_lowering=False, num_devices=1)
    A = {name: nc.dram_tensor(name, shape, F32, kind="ExternalInput").ap() for name, shape in INPUTS}
    A["out"] = nc.dram_tensor("out", [P, KC, S], F32, kind="ExternalOutput").ap()
    build(nc, A)
    r = _run(nc, [arrays], core_ids=[0])
    out = r.results[0]["out"]
    return np.ascontiguousarray(out.transpose(2, 1, 0).reshape(1, S, D))
```

```python
from contextlib import ExitStack

import numpy as np

import concourse.bass as bass
from concourse import mybir

F32 = mybir.dt.float32
F32R = mybir.dt.float32r
ACT = mybir.ActivationFunctionType
ALU = mybir.AluOpType
AX = mybir.AxisListType

P = 128
D = 1024
KC = D // P
S, C = 512, 256
T = S + C
NQ = S // P
HD = 64
EPS = 1e-6
FH = 2816
NH = FH // P
NG = NH // 2
FFN_BLOCKS = 3 * NH
SCALE = HD ** -0.5
MASKED = -float(2.0 ** 100)
LRU_C = 8.0
CONV = 4
RING = 4
BLK = 8 * P
POOL_W = (2, 4, 8, 16)
PAD = 16
UCOLS = PAD + S + 2 * PAD + C + PAD
ROT = [(i + 16) % 32 for i in range(32)]

STAGES = [("l0_in", 10), ("l0_pool", 1), ("l0_out", 8), ("l0_ffn", FFN_BLOCKS),
          ("l1_in", 12), ("l1_out", 8), ("l1_ffn", FFN_BLOCKS),
          ("s_ffn1", FFN_BLOCKS), ("s_in", 12), ("s_atto", 4), ("s_gatt", 8), ("s_rec", 16),
          ("s_grec", 8), ("s_reco", 8), ("s_out", 8), ("s_ffn2", FFN_BLOCKS)]
FIRST = {}
NBLK = 0
for _name, _count in STAGES:
    FIRST[_name] = NBLK
    NBLK += _count
MOD0, MOD1, MOD2, NMOD = 0, 48, 96, 168
MOD_FIRST, MOD_IN = 16, 26
FIRST_LOADS = 4
MOD_RING = {0: 2, MOD2: 3}
DVE_ADDS = (2, 4, 7)
POOL_ADDS = tuple(k for k in range(KC) if k not in DVE_ADDS)

PASSES = ["l0_mix_pre", "l0_mix_post", "l0_ffn_pre", "l0_ffn_post", "l1_mix_pre", "l1_mix_post",
          "l1_ffn_pre", "l1_ffn_post", "s0_pre", "s0_post", "s1_pre", "s1_post", "s2_pre", "s2_post"]
PASS_SEGS = {p: 2 if p[:2] == "l0" or p == "l1_mix_pre" else 1 for p in PASSES}


CONSTS = [("ident", [P]), ("blkones", [P]), ("cos", [S]), ("sin", [S]),
          ("bmod", [NMOD]),
          ("gpre", [7, KC]), ("gpost", [7, KC]), ("qk_gain", [2]), ("pool_scale", [4]),
          ("edges", [4, 2, 8]),
          ("nsink", [16]),
          ("relc", [8]),
          ("conv_w", [KC, CONV]), ("conv_b", [KC]), ("lru_ba", [KC]), ("lru_bx", [KC]),
          ("lru_s8", [KC])]


def padded(cols):
    return (int(np.prod(cols)) + 7) // 8 * 8


PACKED = sum(padded(c) for _, c in CONSTS)


def segs(n):
    return [(0, S), (S, C)][:n]


def before(name, kind=""):
    return sum(p.endswith(kind) for p in PASSES[:PASSES.index(name)])


def build(nc, A):
    with ExitStack() as ctx:
        write_program(nc, A, ctx)


def write_program(nc, A, ctx):
    sems = {}

    def sem(name):
        if name not in sems:
            sems[name] = ctx.enter_context(nc.semaphore(name))
        return sems[name]

    X = 16512
    MIX = X + KC * S * 4
    XC, Y, HID = MIX, MIX + KC * C * 4, MIX + KC * C * 4 + KC * T * 4
    H = HID + 8 * T * 4
    HSPARE = H + 2 * KC * S * 4
    WHL = H + 2 * KC * T * 4
    RAW = WHL + 2 * RING * BLK * 4
    MODRAW = RAW + RING * BLK * 4
    SCR = MODRAW + RING * BLK * 4
    CONST = SCR + 15360
    cursor = [CONST]

    def at(name, cols, off, dt=F32):
        return nc.alloc_sbuf_tensor_at(name, [P] + cols, dt, offset=off)

    def const(name, cols, dt=F32):
        t = at(name, cols, cursor[0], dt)
        cursor[0] += 4 * padded(cols)
        return t

    xl, xc = at("xl", [KC, S], X), at("xc", [KC, C], XC)
    xs = [xl, xc]
    h_hi, h_lo = at("h_hi", [KC, T], H, F32R), at("h_lo", [KC, T], H + KC * T * 4, F32R)
    n_hi, n_lo = at("n_hi", [KC, S], H, F32R), at("n_lo", [KC, S], H + KC * S * 4, F32R)
    y = at("y", [KC, T], Y)
    y1 = at("y1", [KC, S], Y)
    w_hi, w_lo = at("w_hi", [RING, BLK], WHL, F32R), at("w_lo", [RING, BLK], WHL + RING * BLK * 4, F32R)
    raw = at("raw", [RING, BLK], RAW)
    modraw = at("modraw", [RING, BLK], MODRAW)
    c_rows, c2_row = modraw[:, 2:4, :], modraw[:, 3, :]
    modfirst = at("modfirst", [MOD_FIRST, BLK], Y)

    loaded = const("loaded", [PACKED])
    place = {}
    for name, cols in CONSTS:
        place[name] = sum(padded(c) for _, c in CONSTS[:len(place)])

    def part(name, cols):
        view = loaded[:, place[name]:place[name] + int(np.prod(cols))]
        if len(cols) == 1:
            return view
        names = "abc"[:len(cols)]
        sizes = dict(zip(names, cols))
        return view.rearrange(f"p ({' '.join(names)}) -> p {' '.join(names)}", **sizes)

    (ident, blkones, cos, sin, bmod, gpre, gpost, qk_gain, pool_scale, edges, nsink, relc, conv_w,
     conv_b, lru_ba, lru_bx, lru_s8) = (part(n, c) for n, c in CONSTS)
    ones = const("ones", [P])
    lru_n8 = const("lru_n8", [KC])
    modv_a = [const("modv_l", [72]), const("modv_c", [72])]
    modv_b = [loaded[:, place[n]:place[n] + MOD1] for n in ("bmod", "edges")]
    rms_t = const("rms_t", [T // 32])
    mod_acc = const("mod_acc", [8])
    vec_a = const("vec_a", [3, KC, 2])
    vec_b = const("vec_b", [3, KC, 2])
    vec_g = const("vec_g", [3, KC, 2])
    eps_col = const("eps_col", [1])
    smax, negm, rsum, esink, rinv = (const(n, [4]) for n in ("smax", "negm", "rsum", "esink", "rinv"))
    assert cursor[0] <= nc.sbuf_usable_end, (cursor[0], nc.sbuf_usable_end)

    nsq, tn = at("nsq", [2, T], SCR), at("tn", [2, T], SCR + 8 * T)
    n_rstd = at("n_rstd", [T], SCR + 16 * T)
    dump = at("dump", [BLK], SCR + 8 * T)
    sq, rstd = at("sq", [2, S], SCR), at("rstd", [T], SCR + 4096)
    qn, qraw, tsh = at("qn", [T], SCR + 7168), at("qraw", [T], SCR + 10240), at("tsh", [S], SCR + 13312)
    upad, sA, sB = (at(n, [UCOLS], SCR + 4096 + i * UCOLS * 4) for i, n in enumerate(("upad", "sA", "sB")))
    prob = at("prob", [2, T], SCR)
    qs_hi, qs_lo = at("qs_hi", [2, 2, P], SCR + 6144, F32R), at("qs_lo", [2, 2, P], SCR + 8192, F32R)
    opair, dg = at("opair", [2, P], SCR + 10240), at("dg", [2, P], SCR + 11264)
    pt_hi, pt_lo = at("pt_hi", [2, T], RAW, F32R), at("pt_lo", [2, T], RAW + 8 * T, F32R)

    def mixer_buffers(tag, off, nq, tq, nk, tk, nv, wv):
        out = []
        for n, cols in (("q", [nq, tq]), ("k", [nk, tk]), ("v", [nv, wv])):
            for part in ("hi", "lo"):
                out.append(at(f"{tag}_{n}_{part}", cols, off, F32R))
                off += 4 * int(np.prod(cols))
        return out, off

    l0_qkv, _off = mixer_buffers("l0", Y, 4, T, 1, T, 6, P)
    d_hi, d_lo = at("d_hi", [2, T], _off, F32R), at("d_lo", [2, T], _off + 8 * T, F32R)
    assert _off + 16 * T == H
    l1_qkv, _off = mixer_buffers("l1", XC, 8, S, 2, T, 6, 2 * P)
    assert _off <= H
    s_qkv, _off = mixer_buffers("s", XC, 4, S, 4, S, 4, 4 * P)
    rel = at("rel", [8, 2 * P], _off)
    mask_raw, mask = at("mask_raw", [2, P], HSPARE), at("mask", [2, P], HSPARE + 1024, F32R)
    ident_r = at("ident_r", [P], HSPARE + 2048, F32R)
    o_hi, o_lo = at("o_hi", [4, S], HSPARE, F32R), at("o_lo", [4, S], HSPARE + 16 * S, F32R)

    ps = ctx.enter_context(nc.psum_tensor("ps", [P, 8, 512], F32))
    flat = ps[:].rearrange("p b n -> p (b n)")

    raw_landed = [sem(f"raw_landed{i}") for i in range(RING)]
    hi_ready, lo_ready = sem("hi_ready"), sem("lo_ready")
    w_used = sem("w_used")
    mod_landed = {m: [sem(f"mod{m}_landed{i}") for i in range(n)] for m, n in MOD_RING.items()}
    first_landed = [sem(f"mod_first_landed{i}") for i in range(FIRST_LOADS)]
    mod_ops = sem("mod_ops")
    x_landed, const_landed, late_landed = sem("x_landed"), sem("const_landed"), sem("late_landed")
    setup = sem("setup")
    c_landed, cact_ready = sem("c_landed"), sem("cact_ready")
    mod_copied = sem("mod_copied")
    n_sq, n_ss, n_turn, n_rms = sem("n_sq"), sem("n_ss"), sem("n_turn"), sem("n_rms")
    n_t, n_h, h_ready, y_zero = sem("n_t"), sem("n_h"), sem("h_ready"), sem("y_zero")
    x_pool, x_dve = sem("x_pool"), sem("x_dve")
    dve_chain = sem("dve_chain")
    chain = [0]

    def link(dve, ins):
        chain[0] += 1
        ins.then_inc(dve_chain, 1)
        dve.wait_ge(dve_chain, chain[0])

    def load_block(sp, c, d=0):
        if c >= RING:
            sp.wait_ge(lo_ready, c - RING + 1 + d)
        sp.dma_start(raw[:, c % RING, :], A["w_stream"][bass.ds(c + d, 1)].rearrange("o p n -> (o p) n")
                     ).then_inc(raw_landed[c % RING], 16)

    def split_hi(act, c, d=0):
        if c >= NBLK:
            return
        act.wait_ge(raw_landed[c % RING], 16 * (c // RING + 1) + 4 * d)
        if c >= RING:
            act.wait_ge(w_used, c - RING + 1 + d)
        nc.scalar.activation(w_hi[:, c % RING, :], raw[:, c % RING, :], ACT.Copy).then_inc(hi_ready, 1)

    def split_lo(pool, c, d=0):
        if c >= NBLK:
            return
        pool.wait_ge(hi_ready, c + 1 + d)
        nc.gpsimd.tensor_tensor(w_lo[:, c % RING, :], raw[:, c % RING, :], w_hi[:, c % RING, :].bitcast(F32),
                                ALU.subtract).then_inc(lo_ready, 1)

    def repeat(eng, c0, c1, step):
        turns = (c1 - c0) // RING
        if turns > 1:
            with eng.Fori(0, turns) as i:
                for j in range(RING):
                    step(eng, c0 + j, i * RING)
            c0 += turns * RING
        for c in range(c0, c1):
            step(eng, c)

    def tiles(c):
        s = c % RING
        return [(w_hi[:, s, k * P:(k + 1) * P], w_lo[:, s, k * P:(k + 1) * P]) for k in range(8)]

    def product(w, x, outs, first, last):
        for i, (a, b) in enumerate(((0, 0), (0, 1), (1, 0))):
            for out, off, n in outs:
                mm = nc.tensor.matmul(out, w[a], x[b][:, off:off + n], start=first and i == 0, stop=last and i == 2)
        return mm

    def project(x_hi, x_lo, c, outs):
        for k, w in enumerate(tiles(c)):
            mm = product(w, (x_hi[:, k, :], x_lo[:, k, :]), outs, k == 0, k == 7)
        return mm

    def project_first(pe, x_hi, x_lo, c, outs, h_base, shared=()):
        pe.wait_ge(lo_ready, c + 2)
        for k in range(KC):
            pe.wait_ge(h_ready, h_base + k + 1)
            for b in range(2):
                mm = product(tiles(c + b)[k], (x_hi[:, k, :], x_lo[:, k, :]), outs[b], k == 0, k == 7)
                if k == KC - 1 and (b == 0 or not shared):
                    mm.then_inc(w_used, 1)
        if shared:
            project(x_hi, x_lo, c + 1, shared).then_inc(w_used, 1)

    def mods_of(c):
        if c < MOD2:
            return MOD0, 2 * c, 2
        return MOD2, 2 * MOD2 + c - MOD2, 1

    def load_mod(sp, c, i=0, n=0):
        base, ops, each = mods_of(c)
        ring = MOD_RING[base]
        first = MOD_FIRST if base == MOD0 else MOD2
        if c >= first + ring:
            sp.wait_ge(mod_ops, ops - (ring - 1) * each + i * (each * n))
        sp.dma_start(modraw[:, (c - first) % ring, :],
                     A["mod_stream"][bass.ds(c + i * n, 1)].rearrange("o p n -> (o p) n")
                     ).then_inc(mod_landed[base][(c - first) % ring], 16)

    def mod_block(dve, c, outs, where, i=0, n=0):
        base, ops, each = mods_of(c)
        ring = MOD_RING[base]
        first = MOD_FIRST if base == MOD0 else MOD2
        if c < MOD_FIRST:
            dve.wait_ge(first_landed[c // (MOD_FIRST // FIRST_LOADS)], 16)
            w = modfirst[:, c, :]
        else:
            dve.wait_ge(mod_landed[base][(c - first) % ring], 16 * ((c - first) // ring + 1) + i * (n // ring * 16))
            w = modraw[:, (c - first) % ring, :]
        for m in range(each):
            if c + m > 0:
                dve.wait_ge(mod_ops, ops + m + i * (each * n))
            nc.vector.tensor_tensor_reduce(where, w, c2_row if base else c_rows[:, m, :], 1.0, 0.0, ALU.mult, ALU.add,
                                           outs[m]).then_inc(mod_ops, 1)

    def mod_group(dve, c, count, dst, where, i, n, number):
        base, ops, each = mods_of(c)
        first = MOD1 if c < MOD2 else MOD2
        dve.wait_ge(mod_copied, number)
        for j in range(count):
            mod_block(dve, c + j, [mod_acc[:, m * 4 + j:m * 4 + j + 1] for m in range(each)], where, i, n)
        dve.wait_ge(mod_ops, ops + each * count + i * (each * n))
        for m in range(each):
            ins = nc.vector.tensor_copy(dst[m][:, bass.ds(c - first + i * n, count)], mod_acc[:, m * 4:m * 4 + count])
        ins.then_inc(mod_copied, 1)

    def mod_bias(dve, c0, c1, dst, first):
        base, ops, each = mods_of(c1 - 1)
        dve.wait_ge(mod_ops, ops + each)
        for m in range(each):
            v = dst[m][:, c0 - first:c1 - first]
            ins = nc.vector.tensor_tensor(v, v, bmod[:, c0:c1], ALU.add)
        link(dve, ins)

    def vectors(dve, src, sub, slot, shift, scale, gate, res=1.0):
        for m in range(2 if sub < 4 else 1):
            if scale is not None:
                nc.vector.scalar_tensor_tensor(out=vec_a[:, slot, :, m], in0=src[m][:, scale * KC:scale * KC + KC],
                                               scalar=1.0, in1=gpre[:, sub, :], op0=ALU.add, op1=ALU.mult)
                nc.vector.tensor_copy(vec_b[:, slot, :, m], src[m][:, shift * KC:shift * KC + KC])
            if gate is not None:
                nc.vector.scalar_tensor_tensor(out=vec_g[:, slot, :, m], in0=src[m][:, gate * KC:gate * KC + KC],
                                               scalar=res, in1=gpost[:, sub, :], op0=ALU.mult, op1=ALU.mult)

    def sum_bank(name, si):
        return (4 if name.endswith("_pre") else 0) + si

    def norm_act(act, name, src, ready):
        base = 8 * before(name)
        nseg = PASS_SEGS[name]
        for k in range(KC):
            j = base + k
            ready(act, k)
            if j >= 2:
                act.wait_ge(n_ss, j - 1)
            for si, (off, n) in enumerate(segs(nseg)):
                ins = nc.scalar.activation(nsq[:, j % 2, off:off + n], src(si, k), ACT.Square)
            ins.then_inc(n_sq, 1)
        n = segs(nseg)[-1][0] + segs(nseg)[-1][1]
        act.wait_ge(n_turn, before(name) + 1)
        nc.scalar.activation(rms_t[:, 0:n // 32], squares(n_rstd, n)[:, :, 0], ACT.Sqrt, scale=1.0 / D, bias=eps_col[:, 0:1]
                             ).then_inc(n_rms, 1)

    def squares(t, n):
        return t[:, 0:n].rearrange("p (b c) -> p b c", c=32)

    def turn_sums(banks, t):
        for (off, n), bank in zip(segs(2), banks):
            ins = nc.vector.transpose(t[:, off:off + n], bank[:, 0:n])
        return ins

    def turn_inverse(dve, t, n):
        link(dve, nc.vector.reciprocal(rms_t[:, 0:n // 32], rms_t[:, 0:n // 32]))
        link(dve, nc.vector.transpose(t[:, 0:n], rms_t[:, 0:n // 32].rearrange("p (b o) -> p b o", o=1
                                                                              ).to_broadcast([P, n // 32, 32])))

    def norm_pe(pe, name):
        for k in range(KC):
            j = 8 * before(name) + k
            pe.wait_ge(n_sq, j + 1)
            for si, (off, n) in enumerate(segs(PASS_SEGS[name])):
                mm = nc.tensor.matmul(ps[:, sum_bank(name, si), 0:n], ones[:, :], nsq[:, j % 2, off:off + n],
                                      start=k == 0, stop=k == KC - 1)
            mm.then_inc(n_ss, 1)

    def norm_dve(dve, name):
        nseg = PASS_SEGS[name]
        off, n = segs(nseg)[-1]
        dve.wait_ge(n_ss, 8 * before(name) + KC)
        turn_sums([ps[:, sum_bank(name, si), :] for si in range(nseg)], n_rstd).then_inc(n_turn, 1)
        dve.wait_ge(n_rms, before(name) + 1)
        turn_inverse(dve, n_rstd, off + n)
        return [n_rstd[:, off:off + n] for off, n in segs(nseg)]

    def pre_dve(dve, name, slot, dst_hi, dst_lo):
        tb, hb = 8 * before(name), 8 * before(name, "_pre")
        inv = norm_dve(dve, name)
        for k in range(KC + 1):
            if k < KC:
                for si, (off, n) in enumerate(segs(PASS_SEGS[name])):
                    ins = nc.vector.scalar_tensor_tensor(out=tn[:, k % 2, off:off + n], in0=xs[si][:, k, :],
                                                         scalar=vec_a[:, slot, k, si:si + 1], in1=inv[si],
                                                         op0=ALU.mult, op1=ALU.mult)
                ins.then_inc(n_t, 1)
            if k >= 1:
                j = k - 1
                dve.wait_ge(n_h, hb + j + 1)
                for si, (off, n) in enumerate(segs(PASS_SEGS[name])):
                    ins = nc.vector.scalar_tensor_tensor(out=dst_lo[:, j, off:off + n], in0=tn[:, j % 2, off:off + n],
                                                         scalar=vec_b[:, slot, j, si:si + 1],
                                                         in1=dst_hi[:, j, off:off + n].bitcast(F32),
                                                         op0=ALU.add, op1=ALU.subtract)
                ins.then_inc(h_ready, 1)
                dve.wait_ge(h_ready, hb + j + 1)

    def pre_act(act, name, slot, dst_hi):
        for k in range(KC):
            act.wait_ge(n_t, 8 * before(name) + k + 1)
            for si, (off, n) in enumerate(segs(PASS_SEGS[name])):
                ins = nc.scalar.activation(dst_hi[:, k, off:off + n], tn[:, k % 2, off:off + n], ACT.Identity,
                                           bias=vec_b[:, slot, k, si:si + 1])
            ins.then_inc(n_h, 1)

    def post_dve(dve, name, slot, acc):
        inv = norm_dve(dve, name)
        for k in range(KC):
            for si, (off, n) in enumerate(segs(PASS_SEGS[name])):
                t = acc[:, k, off:off + n]
                ins = nc.vector.scalar_tensor_tensor(out=t, in0=t, scalar=vec_g[:, slot, k, si:si + 1], in1=inv[si],
                                                     op0=ALU.mult, op1=ALU.mult)
            ins.then_inc(n_t, 1)
            if k in DVE_ADDS:
                dve.wait_ge(n_t, 8 * before(name) + k + 1)
                for si, (off, n) in enumerate(segs(PASS_SEGS[name])):
                    ins = nc.vector.tensor_tensor(xs[si][:, k, :], xs[si][:, k, :], acc[:, k, off:off + n], ALU.add)
                ins.then_inc(x_dve, 1)

    def post_pool(pool, name, acc):
        for k in POOL_ADDS:
            pool.wait_ge(n_t, 8 * before(name) + k + 1)
            for si, (off, n) in enumerate(segs(PASS_SEGS[name])):
                ins = nc.gpsimd.tensor_tensor(xs[si][:, k, :], xs[si][:, k, :], acc[:, k, off:off + n], ALU.add)
            ins.then_inc(x_pool, 1)

    def x_chunk(eng, posts, k):
        if k in DVE_ADDS:
            eng.wait_ge(x_dve, len(DVE_ADDS) * (posts - 1) + DVE_ADDS.index(k) + 1)
        else:
            eng.wait_ge(x_pool, len(POOL_ADDS) * (posts - 1) + POOL_ADDS.index(k) + 1)

    def x_done(name):
        return lambda eng, k: x_chunk(eng, before(name, "_post"), k)

    CREDIT = 2

    def ffn_buffers(nseg):
        n = segs(nseg)[-1][0] + segs(nseg)[-1][1]
        tag = f"ffn{nseg}_"
        return dict(hi=at(tag + "hi", [2, n], HID, F32R), lo=at(tag + "lo", [2, n], HID + 8 * n, F32R),
                    silu=at(tag + "silu", [2, n], HID + 16 * n), hid=at(tag + "hid", [2, n], HID + 24 * n))

    FFN_BUFS = {1: ffn_buffers(1), 2: ffn_buffers(2)}

    def ffn(name, nseg, x, acc, post, mods=None):
        return dict(name=name, mods=mods, c0=FIRST[name], segs=segs(nseg), x=x, y=acc, h_base=8 * (before(post, "_pre") - 1), index=[
            "l0_ffn", "l1_ffn", "s_ffn1", "s_ffn2"].index(name), **FFN_BUFS[nseg])

    def gate_bank(buf, si):
        return ps[:, 3 * buf, 0:S] if si == 0 else ps[:, 3 * buf + 2, 0:C]

    def up_bank(buf, si):
        return ps[:, 3 * buf + 1, 0:S] if si == 0 else ps[:, 3 * buf + 2, C:2 * C]

    def out_bank(f, n, si):
        if len(f["segs"]) == 1:
            return ps[:, 5 + n % 2, 0:S]
        return (ps[:, (6, 3)[n % 2], 0:S], ps[:, (5, 4)[n % 2], 0:C])[si]

    def ffn_groups(eng, f, step):
        n0 = f["c0"] + 2
        with eng.Fori(0, (NG - 1) // 2) as i:
            for half in range(2):
                step(n0 + 6 * half, i * 12, (half, i * 2, i), False)
        step(n0 + 6 * (NG - 1), 0, (NG - 1, 0, 0), True)

    def ffn_pe(pe, f):
        hid_ready, out_ready, out_free = (sem(f["name"] + s) for s in ("_hid_ready", "_out_ready", "_out_free"))
        ns = len(f["segs"])

        def in_block(c, d, bank, buf):
            pe.wait_ge(lo_ready, c + 1 + d)
            project(f["x"][0], f["x"][1], c, [(bank(buf, si), off, n) for si, (off, n) in enumerate(f["segs"])]
                    ).then_inc(w_used, 1)

        first = [[(bank(0, si), off, n) for si, (off, n) in enumerate(f["segs"])] for bank in (gate_bank, up_bank)]
        project_first(pe, f["x"][0], f["x"][1], f["c0"], [first[0], first[1][:1]], f["h_base"], first[1][1:])

        def step(c, d, group, last):
            g, gd = group[:2]
            pe.wait_ge(hid_ready, CREDIT + 2 * g + 2 * gd)
            if ns == 2:
                pe.wait_ge(out_free, CREDIT + 8 * g + 8 * gd)
            in_block(c, d, gate_bank, 1)
            in_block(c + 1, d, up_bank, 1)
            if not last:
                pe.wait_ge(hid_ready, CREDIT + 2 * g + 1 + 2 * gd)
                in_block(c + 2, d, gate_bank, 0)
                in_block(c + 3, d, up_bank, 0)
            oa = c + 2 if last else c + 4
            pe.wait_ge(lo_ready, oa + 2 + d)
            pe.wait_ge(hid_ready, CREDIT + 2 * g + 2 + 2 * gd)
            for n in range(KC):
                pe.wait_ge(out_free, CREDIT + 8 * g + n - 1 + 8 * gd)
                outs = [(out_bank(f, n, si), off, w) for si, (off, w) in enumerate(f["segs"])]
                for b in range(2):
                    mm = product(tiles(oa + b)[n], (f["hi"][:, b, :], f["lo"][:, b, :]), outs, b == 0, b == 1)
                if n < KC - 1:
                    mm.then_inc(out_ready, 1)
            mm.then_inc(w_used, 2)

        ffn_groups(pe, f, step)

    def ffn_silu(act, f, c, d, buf):
        act.wait_ge(w_used, c + 2 + d)
        for si, (off, n) in enumerate(f["segs"]):
            nc.scalar.activation(f["silu"][:, buf, off:off + n], gate_bank(buf, si), ACT.Silu
                                 ).then_inc(sem(f["name"] + "_silu"), 1)

    def ffn_hidden_hi(act, f, m, md, out_c, out_d):
        ns = len(f["segs"])
        if out_c is not None:
            act.wait_ge(w_used, out_c + out_d)
        for si, (off, n) in enumerate(f["segs"]):
            act.wait_ge(sem(f["name"] + "_hid"), ns * m + si + 1 + ns * md)
            nc.scalar.activation(f["hi"][:, m % 2, off:off + n], f["hid"][:, m % 2, off:off + n], ACT.Copy
                                 ).then_inc(sem(f["name"] + "_hid_hi"), 1)

    def ffn_act(act, f):
        c0 = f["c0"]
        split_hi(act, c0 + RING)
        split_hi(act, c0 + RING + 1)
        ffn_silu(act, f, c0, 0, 0)
        ffn_hidden_hi(act, f, 0, 0, None, 0)

        def step(c, d, group, last):
            g, gd = group[:2]
            split_hi(act, c + RING, d)
            split_hi(act, c + RING + 1, d)
            ffn_silu(act, f, c, d, 1)
            ffn_hidden_hi(act, f, 2 * g + 1, 2 * gd, c, d)
            split_hi(act, c + RING + 2, d)
            split_hi(act, c + RING + 3, d)
            if not last:
                ffn_silu(act, f, c + 2, d, 0)
                split_hi(act, c + RING + 4, d)
                split_hi(act, c + RING + 5, d)
                ffn_hidden_hi(act, f, 2 * g + 2, 2 * gd, c + 6, d)

        ffn_groups(act, f, step)

    def ffn_mult(dve, f, m, md):
        ns = len(f["segs"])
        for si, (off, n) in enumerate(f["segs"]):
            dve.wait_ge(sem(f["name"] + "_silu"), ns * m + si + 1 + ns * md)
            nc.vector.tensor_tensor(f["hid"][:, m % 2, off:off + n], f["silu"][:, m % 2, off:off + n],
                                    up_bank(m % 2, si), ALU.mult).then_inc(sem(f["name"] + "_hid"), 1)

    def ffn_hidden_lo(dve, f, m, md):
        ns = len(f["segs"])
        for si, (off, n) in enumerate(f["segs"]):
            dve.wait_ge(sem(f["name"] + "_hid_hi"), ns * m + si + 1 + ns * md)
            ins = nc.vector.tensor_tensor(f["lo"][:, m % 2, off:off + n], f["hid"][:, m % 2, off:off + n],
                                          f["hi"][:, m % 2, off:off + n].bitcast(F32), ALU.subtract)
        ins.then_inc(sem(f["name"] + "_hid_ready"), 1)

    def ffn_dve(dve, f):
        out_ready, out_free = sem(f["name"] + "_out_ready"), sem(f["name"] + "_out_free")
        dve.sem_inc(sem(f["name"] + "_hid_ready"), CREDIT)
        dve.sem_inc(out_free, CREDIT)
        ffn_mult(dve, f, 0, 0)
        ffn_hidden_lo(dve, f, 0, 0)
        dve.wait_ge(y_zero, f["index"] + 1)
        if f["mods"]:
            m0, start, each, dst = f["mods"]
            for j in range(start):
                mod_block(dve, m0 + j, [dst[m][:, j:j + 1] for m in range(2)], dump[:])
            done = 0 if f["index"] == 0 else 2 * NG - 1

        def mods(g, part, group):
            if f["mods"]:
                i = group[2]
                mod_group(dve, m0 + start + each * (2 * g + part), each, dst, dump[:], i, 4 * each,
                          done + 2 * g + part + i * 4)

        def step(c, d, group, last):
            g, gd = group[:2]
            ffn_mult(dve, f, 2 * g + 1, 2 * gd)
            ffn_hidden_lo(dve, f, 2 * g + 1, 2 * gd)
            mods(g, 0, group)
            if not last:
                ffn_mult(dve, f, 2 * g + 2, 2 * gd)
            dve.wait_ge(out_free, CREDIT + 8 * g + 8 * gd)
            for n in range(KC):
                if n < KC - 1:
                    dve.wait_ge(out_ready, (KC - 1) * g + n + 1 + (KC - 1) * gd)
                else:
                    dve.wait_ge(w_used, (c + 4 if last else c + 6) + d)
                for si, (off, w) in enumerate(f["segs"]):
                    acc = f["y"][:, n, off:off + w]
                    ins = nc.vector.tensor_tensor(acc, acc, out_bank(f, n, si), ALU.add)
                ins.then_inc(out_free, 1)
            if not last:
                ffn_hidden_lo(dve, f, 2 * g + 2, 2 * gd)
                mods(g, 1, group)

        ffn_groups(dve, f, step)

    def ffn_y_ready(f):
        def ready(eng, k):
            eng.wait_ge(sem(f["name"] + "_out_free"), CREDIT + KC * (NG - 1) + k + 1)
        return ready

    def out_pe_two(pe, name, x):
        for n in range(KC):
            c = FIRST[name] + n
            pe.wait_ge(lo_ready, c + 1)
            if n >= 4:
                pe.wait_ge(sem(name + "_y"), n - 3)
            project(x[0], x[1], c, [(ps[:, 2 * (n % 4) + si, 0:w], off, w) for si, (off, w) in enumerate(segs(2))]
                    ).then_inc(w_used, 1)

    def out_pe_one(pe, name, x):
        c = FIRST[name]
        with pe.Fori(0, KC // RING) as i:
            for j in range(RING):
                pe.wait_ge(lo_ready, c + j + 1 + i * RING)
                project(x[0], x[1], c + j, [(flat[:, bass.ds(512 * j + i * (512 * RING), 512)], 0, S)]
                        ).then_inc(w_used, 1)

    def out_act(act, name):
        repeat(act, FIRST[name] + RING, FIRST[name] + KC + RING, split_hi)

    def out_dve(dve, name, acc, nseg, before_chunk=None):
        for n in range(KC):
            if before_chunk:
                before_chunk(n)
            dve.wait_ge(w_used, FIRST[name] + n + 1)
            for si, (off, w) in enumerate(segs(nseg)):
                src = ps[:, 2 * (n % 4) + si, 0:w] if nseg == 2 else ps[:, n, 0:w]
                ins = nc.vector.tensor_copy(acc[:, n, off:off + w], src)
            ins.then_inc(sem(name + "_y"), 1)

    def out_y_ready(name):
        def ready(eng, k):
            eng.wait_ge(sem(name + "_y"), k + 1)
        return ready

    def pair(i, si, n):
        return ps[:, 2 * (i % 2) + si, 0:n]

    def in_plan(layer):
        q, k, v = ((l0_qkv, l1_qkv)[layer][j:j + 2] for j in (0, 2, 4))
        if layer == 0:
            return ([("qk", k, 0, 1, 2), ("qk", q, 0, 0, 2), ("v", v, 0, None, 2)]
                    + [("qk", q, n, 0, 2) for n in range(1, 4)] + [("u", None, g, None, 2) for g in range(4)])
        return ([("qk", k, n, None, 2) for n in range(2)] + [("wide", v, n, None, 2) for n in range(2)]
                + [("qk", q, n, None, 1) for n in range(8)])

    def in_stage(layer):
        name = f"l{layer}_in"
        return dict(name=name, plan=in_plan(layer), c0=FIRST[name], norm=layer == 0,
                    **{s: sem(f"{name}_{s}") for s in ["out", "v_hi", "v_lo", "sh", "sin", "q", "hi", "lo"] + (
                        ["sq", "ss", "turn", "rms", "qn", "pads", "pool", "d_hi", "d_lo", "mix", "mix_hi", "mix_lo"]
                        if layer == 0 else [])})

    def qk_buf(st, j):
        if st["norm"]:
            return qn, tsh
        return (qraw, tsh) if j % 2 else (qn, sq[:, 0, :])

    def outs_before(plan, i):
        return sum(p[0] != "wide" for p in plan[:i])

    def wide_bank(t):
        return ps[:, 4 + t // 2, (t % 2) * 256:(t % 2 + 1) * 256]

    SS_IN = (4, 5)

    def in_pe(pe, st):
        plan, c0 = st["plan"], st["c0"]
        qk_seen = 0
        pending = None

        def head_sums(j):
            for si, (off, n) in enumerate(segs(2)):
                pe.wait_ge(st["sq"], 2 * j + si + 1)
                nc.tensor.matmul(ps[:, SS_IN[si], 0:n], blkones[:, :], sq[:, si, 0:n], start=True, stop=True
                                 ).then_inc(st["ss"], 1)

        project_first(pe, h_hi, h_lo, c0, [[(pair(i, si, w), off, w) for si, (off, w) in enumerate(segs(2))]
                                           for i in range(2)], st["h_base"])
        for i, (kind, buf, n, gain, ns) in enumerate(plan):
            c = c0 + i
            pe.wait_ge(lo_ready, c + 1)
            if i >= 2 and kind != "wide":
                prev = [p for p in range(i) if plan[p][0] != "wide" and p % 2 == i % 2][-1]
                pe.wait_ge(st["out"], outs_before(plan, prev) + 1)
                if plan[prev][0] == "v":
                    pe.wait_ge(st["v_lo"], 1)
            if kind == "v":
                for t in range(T // P):
                    out = pair(i, t // 4, 512)[:, (t % 4) * P:(t % 4 + 1) * P]
                    for k, w in enumerate(tiles(c)):
                        for m, (a, b) in enumerate(((0, 0), (0, 1), (1, 0))):
                            mm = nc.tensor.matmul(out, (h_hi, h_lo)[a][:, k, t * P:(t + 1) * P], w[b],
                                                  start=k == 0 and m == 0, stop=k == 7 and m == 2)
                mm.then_inc(w_used, 1)
            elif kind == "wide" and n == 1:
                for t in range(T // P):
                    for k in range(KC):
                        cols = slice(k % 4 * 256, (k % 4 + 1) * 256)
                        for m, (a, b) in enumerate(((0, 0), (0, 1), (1, 0))):
                            mm = nc.tensor.matmul(wide_bank(t), (h_hi, h_lo)[a][:, k, t * P:(t + 1) * P],
                                                  (w_hi, w_lo)[b][:, (c - 1 + k // 4) % RING, cols],
                                                  start=k == 0 and m == 0, stop=k == KC - 1 and m == 2)
                mm.then_inc(w_used, 2)
            elif kind != "wide" and i >= 2:
                project(h_hi, h_lo, c, [(pair(i, si, w), off, w) for si, (off, w) in enumerate(segs(ns))]
                        ).then_inc(w_used, 1)
            if pending is not None:
                head_sums(pending)
                pending = None
            if kind == "qk":
                if st["norm"]:
                    pending = qk_seen
                qk_seen += 1

    def in_act(act, st):
        plan, c0 = st["plan"], st["c0"]
        j = 0
        pending = None

        def head_rms(j):
            act.wait_ge(st["turn"], j + 1)
            nc.scalar.activation(rms_t[:], squares(rstd, T)[:, :, 0], ACT.Sqrt, scale=1.0 / HD, bias=eps_col[:, 0:1]
                                 ).then_inc(st["rms"], 1)

        def qk_hi(j, buf, n, ns):
            act.wait_ge(st["q"], j + 1)
            w = segs(ns)[-1][0] + segs(ns)[-1][1]
            nc.scalar.activation(buf[0][:, n, 0:w], qk_buf(st, j)[0][:, 0:w], ACT.Copy).then_inc(st["hi"], 1)

        def pool_hi(g):
            act.wait_ge(st["pool"], g + 1)
            if g >= 2:
                act.wait_ge(st["mix"], g - 1)
            s = (sA, sB)[g % 2]
            nc.scalar.activation(d_hi[:, g % 2, 0:S], s[:, PAD:PAD + S], ACT.Copy)
            nc.scalar.activation(d_hi[:, g % 2, S:T], s[:, S + 3 * PAD:S + 3 * PAD + C], ACT.Copy
                                 ).then_inc(st["d_hi"], 1)

        for i, (kind, buf, n, gain, ns) in enumerate(plan):
            split_hi(act, c0 + i + RING)
            act.wait_ge(w_used, c0 + i + 1)
            if pending is not None and st["norm"]:
                head_rms(pending[0])
            if kind == "qk":
                if st["norm"]:
                    for si, (off, w) in enumerate(segs(2)):
                        if j >= 1:
                            act.wait_ge(st["ss"], 2 * j - 1 + si)
                        nc.scalar.activation(sq[:, si, 0:w], pair(i, si, w), ACT.Square).then_inc(st["sq"], 1)
                dst = qraw if st["norm"] else qk_buf(st, j)[0]
                if st["norm"] and j >= 1:
                    act.wait_ge(st["qn"], j)
                if not st["norm"] and j >= 2:
                    act.wait_ge(st["lo"], j - 1)
                for si, (off, w) in enumerate(segs(ns)):
                    ins = nc.scalar.activation(dst[:, off:off + w], pair(i, si, w), ACT.Copy)
                ins.then_inc(st["out"], 1)
            elif kind == "v":
                for t0, t1, si in ((0, 4, 0), (4, 6, 1)):
                    ins = nc.scalar.activation(buf[0][:, t0:t1, n * P:(n + 1) * P],
                                               pair(i, si, (t1 - t0) * P).rearrange("p (t c) -> p t c", c=P), ACT.Copy)
                ins.then_inc(st["out"], 1)
            elif kind == "wide" and n == 1:
                for t in range(0, T // P, 2):
                    nc.scalar.activation(buf[0][:, t:t + 2, :], ps[:, 4 + t // 2, :].rearrange("p (t c) -> p t c", t=2),
                                         ACT.Copy).then_inc(st["v_hi"], 1)
            if pending is not None:
                qk_hi(*pending)
                pending = None
            if kind == "u":
                if n >= 1:
                    pool_hi(n - 1)
                else:
                    act.wait_ge(st["lo"], j)
                act.wait_ge(st["pads"], 1)
                nc.scalar.activation(upad[:, PAD:PAD + S], pair(i, 0, S), ACT.Copy)
                nc.scalar.activation(upad[:, S + 3 * PAD:S + 3 * PAD + C], pair(i, 1, C), ACT.Copy
                                     ).then_inc(st["out"], 1)
            if kind == "qk":
                pending = (j, buf, n, ns)
                j += 1
        if pending is not None:
            qk_hi(*pending)
        if st["norm"]:
            pool_hi(3)

    def in_dve(dve, st):
        plan = st["plan"]
        j = 0
        for i, (kind, buf, n, gain, ns) in enumerate(plan):
            if kind == "wide" and n == 1:
                for t in range(0, T // P, 2):
                    dve.wait_ge(st["v_hi"], t // 2 + 1)
                    nc.vector.tensor_tensor(buf[1][:, t:t + 2, :], ps[:, 4 + t // 2, :].rearrange("p (t c) -> p t c", t=2),
                                            buf[0][:, t:t + 2, :].bitcast(F32), ALU.subtract).then_inc(st["v_lo"], 1)
            if kind == "v":
                dve.wait_ge(st["out"], outs_before(plan, i) + 1)
                for t0, t1, si in ((0, 4, 0), (4, 6, 1)):
                    cols = slice(n * P, (n + 1) * P)
                    ins = nc.vector.tensor_tensor(buf[1][:, t0:t1, cols],
                                                  pair(i, si, (t1 - t0) * P).rearrange("p (t c) -> p t c", c=P),
                                                  buf[0][:, t0:t1, cols].bitcast(F32), ALU.subtract)
                ins.then_inc(st["v_lo"], 1)
            if kind == "qk":
                w = segs(ns)[-1][0] + segs(ns)[-1][1]
                q, sh = qk_buf(st, j)
                if st["norm"]:
                    dve.wait_ge(st["ss"], 2 * j + 2)
                    turn_sums([ps[:, b, :] for b in SS_IN], rstd).then_inc(st["turn"], 1)
                    dve.wait_ge(st["rms"], j + 1)
                    turn_inverse(dve, rstd, T)
                    dve.wait_ge(st["out"], outs_before(plan, i) + 1)
                    nc.vector.scalar_tensor_tensor(out=q[:, 0:w], in0=qraw[:, 0:w], scalar=qk_gain[:, gain:gain + 1],
                                                   in1=rstd[:, 0:w], op0=ALU.mult, op1=ALU.mult).then_inc(st["qn"], 1)
                    dve.wait_ge(st["qn"], j + 1)
                else:
                    dve.wait_ge(st["out"], outs_before(plan, i) + 1)
                nc.vector.stream_shuffle(sh[:, 0:S], q[:, 0:S], ROT).then_inc(st["sh"], 1)
                dve.wait_ge(st["sh"], j + 1)
                link(dve, nc.vector.tensor_tensor(q[:, 0:S], q[:, 0:S], cos[:, :], ALU.mult))
                dve.wait_ge(st["sin"], j + 1)
                nc.vector.tensor_tensor(q[:, 0:S], q[:, 0:S], sh[:, 0:S], ALU.add).then_inc(st["q"], 1)
                dve.wait_ge(st["hi"], j + 1)
                nc.vector.tensor_tensor(buf[1][:, n, 0:w], q[:, 0:w], buf[0][:, n, 0:w].bitcast(F32), ALU.subtract
                                        ).then_inc(st["lo"], 1)
                dve.wait_ge(st["lo"], j + 1)
                j += 1
            if kind == "u":
                pool_mean(dve, st, n, i)
            if st["norm"]:
                c = MOD_FIRST + i
                mod_block(dve, c, [modv_a[m][:, c:c + 1] for m in range(2)], flat[:, 6 * 512:8 * 512])

    def pool_mean(dve, st, g, i):
        dve.wait_ge(st["out"], i + 1)
        src, lo, hi = upad, 0, UCOLS
        for level in range(g + 1):
            dst = (sA, sB)[level % 2]
            back, ahead = (1, 0) if level == 0 else (2 ** (level - 1), 2 ** (level - 1))
            lo, hi = lo + back, hi - ahead
            link(dve, nc.vector.tensor_tensor(dst[:, lo:hi], src[:, lo - back:hi - back], src[:, lo + ahead:hi + ahead],
                                              ALU.add))
            src = dst
        for first, n in ((PAD, S), (S + 3 * PAD, C)):
            for e, at_ in ((0, first), (1, first + n - 8)):
                ins = nc.vector.tensor_tensor(src[:, at_:at_ + 8], src[:, at_:at_ + 8], edges[:, g, e, :], ALU.mult)
        link(dve, ins)
        nc.vector.scalar_tensor_tensor(out=src[:, PAD:UCOLS - PAD], in0=src[:, PAD:UCOLS - PAD],
                                       scalar=1.0 / POOL_W[g], in1=upad[:, PAD:UCOLS - PAD], op0=ALU.mult,
                                       op1=ALU.subtract).then_inc(st["pool"], 1)
        dve.wait_ge(st["d_hi"], g + 1)
        nc.vector.tensor_tensor(d_lo[:, g % 2, 0:S], src[:, PAD:PAD + S], d_hi[:, g % 2, 0:S].bitcast(F32), ALU.subtract)
        nc.vector.tensor_tensor(d_lo[:, g % 2, S:T], src[:, S + 3 * PAD:S + 3 * PAD + C],
                                d_hi[:, g % 2, S:T].bitcast(F32), ALU.subtract).then_inc(st["d_lo"], 1)
        dve.wait_ge(st["d_lo"], g + 1)

    def in_pool(pool, st):
        j = 0
        for i, (kind, buf, n, gain, ns) in enumerate(st["plan"]):
            split_lo(pool, st["c0"] + i + RING)
            if kind == "qk":
                q, sh = qk_buf(st, j)
                pool.wait_ge(st["sh"], j + 1)
                nc.gpsimd.tensor_tensor(sh[:, 0:S], sh[:, 0:S], sin[:, :], ALU.mult).then_inc(st["sin"], 1)
                j += 1
            if kind == "u" and n == 0:
                pool.wait_ge(st["lo"], j)
                for k, (a, b) in enumerate(((0, PAD), (PAD + S, S + 3 * PAD), (UCOLS - PAD, UCOLS))):
                    ins = nc.gpsimd.memset(upad[:, a:b], 0.0)
                ins.then_inc(st["pads"], 1)

    def pool_pe(pe, st):
        c = FIRST["l0_pool"]
        pe.wait_ge(lo_ready, c + 1)
        for g in range(4):
            i = len(st["plan"]) + g
            pe.wait_ge(st["d_lo"], g + 1)
            pe.wait_ge(st["out"], i - 1) if g < 2 else pe.wait_ge(st["mix_lo"], g - 1)
            mm = product(tiles(c)[g], (d_hi[:, g % 2, :], d_lo[:, g % 2, :]),
                         [(pair(i, si, w), off, w) for si, (off, w) in enumerate(segs(2))], True, True)
            mm.then_inc(st["mix"] if g < 3 else w_used, 1)

    def pool_out_ready(eng, st, g):
        if g < 3:
            eng.wait_ge(st["mix"], g + 1)
        else:
            eng.wait_ge(w_used, FIRST["l0_pool"] + 1)

    def pool_act(act, st):
        for g in range(4):
            pool_out_ready(act, st, g)
            for si, (off, w) in enumerate(segs(2)):
                ins = nc.scalar.activation(h_hi[:, 4 + g, off:off + w], pair(len(st["plan"]) + g, si, w), ACT.Copy,
                                           scale=pool_scale[:, g:g + 1])
            ins.then_inc(st["mix_hi"], 1)
        split_hi(act, FIRST["l0_pool"] + RING)

    def pool_dve(dve, st):
        for g in range(4):
            dve.wait_ge(st["mix_hi"], g + 1)
            for si, (off, w) in enumerate(segs(2)):
                ins = nc.vector.scalar_tensor_tensor(out=h_lo[:, 4 + g, off:off + w],
                                                     in0=pair(len(st["plan"]) + g, si, w),
                                                     scalar=pool_scale[:, g:g + 1],
                                                     in1=h_hi[:, 4 + g, off:off + w].bitcast(F32),
                                                     op0=ALU.mult, op1=ALU.subtract)
            ins.then_inc(st["mix_lo"], 1)

    def attention(name, units, q, k, v, out, scale, qchunk, kchunk, vcol, outchunk, next_block, extra=None, sink=None,
                  unroll=False):
        groups = []
        for x in units:
            nb = len(x[4])
            groups.append([(0, (nb + 1) // 2), ((nb + 1) // 2, nb)] if nb > 1 else [(0, 1)])
        cum = [0]
        for g in groups:
            cum.append(cum[-1] + len(g))
        return dict(name=name, units=units, q=q, k=k, v=v, out=out, scale=scale, qchunk=qchunk, kchunk=kchunk,
                    vcol=vcol, outchunk=outchunk, extra=extra, sink=sink, groups=groups, cum=cum, nu=len(units), next=next_block, unroll=unroll, d_steps=3 if sink else 2,
                    **{"s_" + s: sem(f"{name}_{s}") for s in (
                        "staged", "qk", "negm", "p", "diag", "t", "hi", "lo", "pv", "o", "m_hi", "m_lo")})

    ATT_ITERS = 4

    def att_loop(eng, a, body):
        body(0, True, False)
        if a["unroll"]:
            for c in range(1, ATT_ITERS - 1):
                body(c, False, False)
        else:
            with eng.Fori(0, ATT_ITERS - 2) as i:
                body(i + 1, False, False)
        body(ATT_ITERS - 1, False, True)

    def ahead(a, c, u, last):
        if u + 2 < a["nu"]:
            return c, u + 2
        return None if last else (c + 1, u + 2 - a["nu"])

    def behind(a, c, u, first, n, size):
        if u >= n:
            return c, u - n
        return None if first else (c - 1, size + u - n)

    def score(u, col, n):
        return flat[:, (u % 2) * 1024 + col:(u % 2) * 1024 + col + n]

    def att_pe(pe, a, free):
        nu, cum = a["nu"], a["cum"]

        def qk(c, u):
            qt, half, _, keys, _, tag = a["units"][u]
            if half == 0:
                pe.wait_ge(a["s_staged"], c * (nu // 2) + qt + 1)
            more = a["extra"](c, a["units"][u]) if a["extra"] else []
            kc = a["kchunk"](c, a["units"][u])
            for col, kcol, w in keys:
                added = [m for m in more if col <= m[0] < col + w]
                for i, (x, z) in enumerate(((0, 0), (0, 1), (1, 0))):
                    mm = nc.tensor.matmul(score(u, col, w), (qs_hi, qs_lo)[x][:, qt % 2, half, :],
                                          a["k"][z][:, kc, kcol:kcol + w], start=i == 0, stop=i == 2 and not added)
                for j, (mcol, mw, lhs, rhs) in enumerate(added):
                    mm = nc.tensor.matmul(score(u, mcol, mw), lhs, rhs, start=False, stop=j == len(added) - 1)
            mm.then_inc(a["s_qk"], 1)

        def qk_next(c, u, n):
            pe.wait_ge(a["s_p"], c * nu + u + 1)
            qk(*n)

        def turn(c, u, first):
            pe.wait_ge(a["s_diag"], a["d_steps"] * (c * nu + u + 1))
            for g, (b0, b1) in enumerate(a["groups"][u]):
                if not (first and u == 0):
                    pe.wait_ge(a["s_lo"], c * cum[-1] + cum[u] - len(a["groups"][u - 1]) + min(g + 1, len(a["groups"][u - 1])))
                for b in range(b0, b1):
                    mm = nc.tensor.matmul(ps[:, 4 + g, (b - b0) * P:(b - b0 + 1) * P], prob[:, u % 2, b * P:(b + 1) * P],
                                          dg[:, u % 2, :], start=True, stop=True)
                mm.then_inc(a["s_t"], 1)

        def values(c, u, first):
            x = a["units"][u]
            if not (first and u < 2):
                pe.wait_ge(a["s_o"], c * nu + u - 1)
            nb = len(x[4])
            for g, (b0, b1) in enumerate(a["groups"][u]):
                pe.wait_ge(a["s_lo"], c * cum[-1] + cum[u] + g + 1)
                for b in range(b0, b1):
                    for i, (z, p) in enumerate(((0, 0), (0, 1), (1, 0))):
                        mm = nc.tensor.matmul(ps[0:HD, 6 + u % 2, 0:P], a["v"][z][:, x[4][b], a["vcol"](c, x)],
                                              (pt_hi, pt_lo)[p][:, u % 2, b * P:(b + 1) * P], start=b == 0 and i == 0,
                                              stop=b == nb - 1 and i == 2)
            mm.then_inc(a["s_pv"], 1)

        def body(c, first, last):
            for u in range(nu):
                n = ahead(a, c, u, last)
                if n:
                    qk_next(c, u, n)
                turn(c, u, first)
                n = behind(a, c, u, first, 1, nu)
                if n:
                    values(*n, first)
            if last:
                values(c, nu - 1, False)

        free(pe)
        qk(0, 0)
        qk(0, 1)
        att_loop(pe, a, body)

    def att_act(act, a):
        nu, cum = a["nu"], a["cum"]

        def exps(c, u):
            act.wait_ge(a["s_negm"], 2 * (c * nu + u + 1))
            x = a["units"][u]
            w = P * len(x[4])
            e = u % 4
            ins = nc.scalar.activation(prob[:, u % 2, 0:w], score(u, 0, w), ACT.Exp, scale=a["scale"],
                                       bias=negm[:, e:e + 1], accum_out=rsum[:, e:e + 1])
            if a["sink"]:
                ins = nc.scalar.activation(esink[:, e:e + 1], nsink[:, a["sink"](c, x)], ACT.Exp, scale=-1.0,
                                           bias=negm[:, e:e + 1])
            ins.then_inc(a["s_p"], 1)

        def out(c, u):
            p, half = u // 2, a["units"][u][1]
            act.wait_ge(a["s_pv"], c * nu + u + 1)
            if half == 0 and not (first_pair(c) and p < 2):
                act.wait_ge(a["s_m_lo"], c * (nu // 2) + p - 1)
            nc.scalar.activation(opair[half * HD:(half + 1) * HD, p % 2, :], ps[0:HD, 6 + u % 2, 0:P], ACT.Copy
                                 ).then_inc(a["s_o"], 1)
            if half == 1:
                act.wait_ge(a["s_o"], c * nu + u + 1)
                x = a["units"][u]
                nc.scalar.activation(a["out"][0][:, a["outchunk"](c, x), x[2]:x[2] + P], opair[:, p % 2, :], ACT.Copy
                                     ).then_inc(a["s_m_hi"], 1)

        def first_pair(c):
            return isinstance(c, int) and c == 0

        def body(c, first, last):
            for u in range(nu):
                if not (first and u < 2):
                    act.wait_ge(a["s_pv"], c * nu + u - 1)
                for g, (b0, b1) in enumerate(a["groups"][u]):
                    act.wait_ge(a["s_t"], c * cum[-1] + cum[u] + g + 1)
                    nc.scalar.activation(pt_hi[:, u % 2, b0 * P:b1 * P], ps[:, 4 + g, 0:(b1 - b0) * P], ACT.Copy
                                         ).then_inc(a["s_hi"], 1)
                n = ahead(a, c, u, last)
                if n:
                    exps(*n)
                n = behind(a, c, u, first, 1, nu)
                if n:
                    out(*n)
            if last:
                out(c, nu - 1)

        exps(0, 0)
        exps(0, 1)
        act.wait_ge(lo_ready, a["next"] + RING)
        att_loop(act, a, body)

    def att_dve(dve, a):
        nu, cum = a["nu"], a["cum"]

        def row_max(c, u):
            dve.wait_ge(a["s_qk"], c * nu + u + 1)
            x = a["units"][u]
            e = u % 4
            nc.vector.reduce_max(smax[:, e:e + 1], score(u, 0, P * len(x[4])), AX.X).then_inc(a["s_negm"], 1)
            dve.wait_ge(a["s_negm"], 2 * (c * nu + u) + 1)
            if a["sink"]:
                ins = nc.vector.tensor_scalar(negm[:, e:e + 1], smax[:, e:e + 1], -a["scale"], nsink[:, a["sink"](c, x)],
                                              ALU.mult, ALU.min)
            else:
                ins = nc.vector.tensor_scalar(negm[:, e:e + 1], smax[:, e:e + 1], -a["scale"], None, ALU.mult)
            ins.then_inc(a["s_negm"], 1)

        def low(c, u, g):
            b0, b1 = a["groups"][u][g]
            dve.wait_ge(a["s_hi"], c * cum[-1] + cum[u] + g + 1)
            nc.vector.tensor_tensor(pt_lo[:, u % 2, b0 * P:b1 * P], ps[:, 4 + g, 0:(b1 - b0) * P],
                                    pt_hi[:, u % 2, b0 * P:b1 * P].bitcast(F32), ALU.subtract).then_inc(a["s_lo"], 1)

        def diagonal(c, u):
            e, done = u % 4, a["d_steps"] * (c * nu + u)
            dve.wait_ge(a["s_p"], c * nu + u + 1)
            if a["sink"]:
                nc.vector.tensor_tensor(rsum[:, e:e + 1], rsum[:, e:e + 1], esink[:, e:e + 1], ALU.add
                                        ).then_inc(a["s_diag"], 1)
                dve.wait_ge(a["s_diag"], done + 1)
            nc.vector.reciprocal(rinv[:, e:e + 1], rsum[:, e:e + 1]).then_inc(a["s_diag"], 1)
            dve.wait_ge(a["s_diag"], done + a["d_steps"] - 1)
            nc.vector.tensor_scalar(dg[:, u % 2, :], ident, rinv[:, e:e + 1], None, ALU.mult).then_inc(a["s_diag"], 1)

        def m_lo(c, p):
            dve.wait_ge(a["s_m_hi"], c * (nu // 2) + p + 1)
            x = a["units"][2 * p]
            n = a["outchunk"](c, x)
            nc.vector.tensor_tensor(a["out"][1][:, n, x[2]:x[2] + P], opair[:, p % 2, :],
                                    a["out"][0][:, n, x[2]:x[2] + P].bitcast(F32), ALU.subtract).then_inc(a["s_m_lo"], 1)

        def body(c, first, last):
            for u in range(nu):
                if u + 1 < nu:
                    diagonal(c, u + 1)
                elif not last:
                    diagonal(c + 1, 0)
                n = ahead(a, c, u, last)
                if n:
                    row_max(*n)
                for g in range(len(a["groups"][u])):
                    low(c, u, g)
                n = behind(a, c, (u - 1) // 2, first, 1, nu // 2) if u % 2 else None
                if n:
                    m_lo(*n)
            if last:
                m_lo(c, nu // 2 - 1)

        row_max(0, 0)
        row_max(0, 1)
        diagonal(0, 0)
        att_loop(dve, a, body)

    def att_pool(pool, a, ready):
        nt = a["nu"] // 2
        halves = [blkones[:, h * HD:h * HD + 1].to_broadcast([P, P]) for h in range(2)]
        ready(pool)
        def body(c, first, last):
            for qt in range(nt):
                x = a["units"][2 * qt]
                if not (first and qt < 2):
                    pool.wait_ge(a["s_qk"], c * 2 * nt + 2 * qt - 2)
                n = a["qchunk"](c, x)
                for t, src in ((qs_hi, a["q"][0]), (qs_lo, a["q"][1])):
                    for half in range(2):
                        ins = nc.gpsimd.tensor_tensor(t[:, qt % 2, half, :], src[:, n, x[2]:x[2] + P].bitcast(F32),
                                                      halves[half], ALU.mult)
                ins.then_inc(a["s_staged"], 1)

        att_loop(pool, a, body)

    def m_done(eng, a):
        eng.wait_ge(a["s_m_lo"], ATT_ITERS * a["nu"] // 2)

    l0_att = attention(
        "l0_att",
        [(t, half, t * P, [(0, 0, S), (S, S, C)] if t < NQ else [(0, S, C)], list(range(6)) if t < NQ else [4, 5], None)
         for t in range(T // P) for half in range(2)],
        l0_qkv[0:2], l0_qkv[2:4], l0_qkv[4:6], (h_hi, h_lo), SCALE, lambda c, x: c, lambda c, x: 0,
        lambda c, x: slice(x[1] * HD, (x[1] + 1) * HD), lambda c, x: c, FIRST["l0_out"])

    def l1_units():
        units = []
        for kc in range(2):
            for t in range(NQ):
                b0, b1 = max(t - 1, 0), min(t + 2, NQ)
                w = (b1 - b0) * P
                keys = [(0, S, C), (C, b0 * P, min(w, C))] + ([(2 * C, b0 * P + C, w - C)] if w > C else [])
                for half in range(2):
                    units.append((kc * NQ + t, half, t * P, keys, [4, 5] + list(range(b0, b1)), (kc, t, b0, b1)))
        return units

    def l1_extra(c, x):
        kc, t, b0, b1 = x[5]
        return [(C + (b - b0) * P, P, ident_r[:, :], mask[:, 0 if b < t else 1, :]) for b in range(b0, b1) if b != t]

    l1_att = attention(
        "l1_att", l1_units(), l1_qkv[0:2], l1_qkv[2:4], l1_qkv[4:6], (n_hi, n_lo), SCALE,
        lambda c, x: c * 2 + x[5][0], lambda c, x: x[5][0],
        lambda c, x: slice((2 * x[5][0] + x[1]) * HD, (2 * x[5][0] + x[1] + 1) * HD), lambda c, x: c * 2 + x[5][0],
        FIRST["l1_out"], extra=l1_extra, sink=lambda c, x: bass.ds(c * 4 + 2 * x[5][0] + x[1], 1))

    def s_extra(c, x):
        t = x[0]
        head = c * 2 + x[1]
        if t == 0:
            return [(0, P, ident[:, :], rel[:, head, P:2 * P])]
        return [((t - 1) * P, 2 * P, ident[:, :], rel[:, head, :])]

    s_att = attention(
        "s_att", [(t, half, t * P, [(0, 0, (t + 1) * P)], list(range(t + 1)), None) for t in range(NQ) for half in range(2)],
        s_qkv[0:2], s_qkv[2:4], s_qkv[4:6], (o_hi, o_lo), 1.0, lambda c, x: c, lambda c, x: c,
        lambda c, x: slice(c * P + x[1] * HD, c * P + (x[1] + 1) * HD), lambda c, x: c, FIRST["s_atto"],
        extra=s_extra, unroll=True)

    s_hi, s_lo = sem("s_in_hi"), sem("s_in_lo")
    att_done, gated, rec_lo = sem("s_att_done"), sem("s_gated"), sem("s_rec_lo")
    s_sig, s_grs, merged, merged_hi, merged_lo = (sem(n) for n in (
        "s_sig", "s_grs", "s_merged", "s_merged_hi", "s_merged_lo"))

    def bank_of(j, i):
        return flat[:, bass.ds(512 * j + i * (512 * RING), 512)]

    def s_in_pe(pe):
        c0 = FIRST["s_in"]
        project_first(pe, n_hi, n_lo, c0, [[(ps[:, i, :], 0, S)] for i in range(2)], 8 * before("s1_pre", "_pre"))
        for i in range(2, 8):
            pe.wait_ge(lo_ready, c0 + i + 1)
            if i >= 4:
                pe.wait_ge(s_lo, i - 3)
            project(n_hi, n_lo, c0 + i, [(ps[:, i % 4, :], 0, S)]).then_inc(w_used, 1)
        for i in range(4):
            c = c0 + 8 + i
            pe.wait_ge(lo_ready, c + 1)
            for t in range(NQ):
                for k in range(2):
                    for m, (a, b) in enumerate(((0, 0), (0, 1), (1, 0))):
                        mm = nc.tensor.matmul(ps[:, 4 + t, :], (n_hi, n_lo)[a][:, 2 * i + k, t * P:(t + 1) * P],
                                              (w_hi, w_lo)[b][:, c % RING, k * S:(k + 1) * S],
                                              start=i == 0 and k == 0 and m == 0, stop=i == 3 and k == 1 and m == 2)
            mm.then_inc(w_used, 1)

    def s_in_out(i, part):
        if i < 8:
            return s_qkv[2 * (i // 4) + part][:, i % 4, :], ps[:, i % 4, :]
        return s_qkv[4 + part][:, i - 8, :], ps[:, i - 4, :]

    def s_in_act(act):
        c0 = FIRST["s_in"]
        for i in range(12):
            split_hi(act, c0 + i + RING)
            if i < 8:
                act.wait_ge(w_used, c0 + i + 1)
                dst, bank = s_in_out(i, 0)
                nc.scalar.activation(dst, bank, ACT.Copy, scale=SCALE if i < 4 else 1.0).then_inc(s_hi, 1)
        act.wait_ge(w_used, c0 + 12)
        for i in range(8, 12):
            dst, bank = s_in_out(i, 0)
            nc.scalar.activation(dst, bank, ACT.Copy).then_inc(s_hi, 1)

    def s_in_dve(dve):
        for i in range(12):
            dve.wait_ge(s_hi, i + 1)
            hi, bank = s_in_out(i, 0)
            lo, _ = s_in_out(i, 1)
            nc.vector.scalar_tensor_tensor(out=lo, in0=bank, scalar=SCALE if i < 4 else 1.0, in1=hi.bitcast(F32),
                                           op0=ALU.mult, op1=ALU.subtract).then_inc(s_lo, 1)

    def bias_dve(dve):
        dve.wait_ge(late_landed, 16 * (LATE.index("rel_in") + 1))
        for h in range(8):
            ins = nc.vector.tensor_scalar(rel[:, h, :], rel[:, h, :], relc[:, h:h + 1], None, ALU.subtract)
        link(dve, ins)
        nc.vector.memset(rel[0:HD, :, P + HD:2 * P], -1e30).then_inc(sem("rel_ready"), 1)

    LRU = MODRAW
    lru_wa, lru_wx = at("lru_wa_sb", [KC, P], LRU), at("lru_wx_sb", [KC, P], LRU + KC * P * 4)
    _lru = LRU + 2 * KC * P * 4
    xpad = at("xpad", [S + 8], _lru)
    xconv, gy, rec = (at(n, [2, S], _lru + 4 * (S + 8) + 8 * S * i) for i, n in enumerate(("xconv", "gy", "rec")))
    r_g, i_g, a_g, tau = (at(n, [S], _lru + 4 * (S + 8) + 24 * S + 4 * S * i) for i, n in enumerate(("r_g", "i_g", "a_g", "tau")))
    assert _lru + 4 * (S + 8) + 40 * S <= SCR + 15360
    att = at("att", [KC, S], MIX)
    rec_hi, rec_l = at("rec_hi", [KC, S], MIX + 4 * KC * S, F32R), at("rec_lo", [KC, S], MIX + 8 * KC * S, F32R)
    grs = at("grs", [KC, S], HSPARE)
    sg = at("sg", [2, S], SCR + 8192)
    xp, cv, ga, sig, ex, th, qq, sqr, uu, rc, rhi, gl = (sem("lru_" + n) for n in (
        "xpad", "conv", "gates", "sigmoid", "a", "tanh", "ratio", "sqrt", "u", "rec", "hi", "gelu"))

    def s_atto_pe(pe):
        c0 = FIRST["s_atto"]
        m_done(pe, s_att)
        for b in range(4):
            pe.wait_ge(lo_ready, c0 + b + 1)
            for j in range(2):
                for k in range(4):
                    mm = product(tiles(c0 + b)[4 * j + k], (o_hi[:, k, :], o_lo[:, k, :]), [(ps[:, 2 * b + j, :], 0, S)],
                                 k == 0, k == 3)
            mm.then_inc(w_used, 1)

    def s_atto_dve(dve):
        for b in range(4):
            dve.wait_ge(w_used, FIRST["s_atto"] + b + 1)
            nc.vector.tensor_copy(att[:, 2 * b:2 * b + 2, :], ps[:, 2 * b:2 * b + 2, :]).then_inc(att_done, 1)

    def eight_pe(pe, name, x, free):
        c = FIRST[name]
        with pe.Fori(0, KC // RING) as i:
            for j in range(RING):
                pe.wait_ge(lo_ready, c + j + 1 + i * RING)
                free(i, j)
                project(x[0], x[1], c + j, [(bank_of(j, i), 0, S)]).then_inc(w_used, 1)

    def s_gatt_act(act):
        for n in range(KC):
            split_hi(act, FIRST["s_gatt"] + n + RING)
            act.wait_ge(w_used, FIRST["s_gatt"] + n + 1)
            if n >= 2:
                act.wait_ge(gated, n - 1)
            nc.scalar.activation(sg[:, n % 2, :], ps[:, n, :], ACT.Sigmoid).then_inc(s_sig, 1)

    def s_gatt_dve(dve):
        dve.wait_ge(att_done, 4)
        for n in range(KC):
            dve.wait_ge(s_sig, n + 1)
            nc.vector.tensor_tensor(att[:, n, :], att[:, n, :], sg[:, n % 2, :], ALU.mult).then_inc(gated, 1)

    def s_rec_pe(pe):
        c0 = FIRST["s_rec"]
        pe.wait_ge(late_landed, 16 * (LATE.index("lru_wx_in") + 1))

        def block(c, bank, waits):
            pe.wait_ge(lo_ready, c + 1)
            pe.wait_ge(*waits)
            project(n_hi, n_lo, c, [(ps[:, bank, :], 0, S)]).then_inc(w_used, 1)

        def gates(n):
            pe.wait_ge(cv, n + 1)
            if n >= 2:
                pe.wait_ge(sig, n - 1)
            nc.tensor.matmul(ps[:, 4 + n % 2, :], lru_wa[:, n, :], xconv[:, n % 2, :], start=True, stop=True)
            nc.tensor.matmul(ps[:, 6 + n % 2, :], lru_wx[:, n, :], xconv[:, n % 2, :], start=True, stop=True
                             ).then_inc(ga, 1)

        for n in range(KC):
            block(c0 + 2 * n, n % 2, (xp, n - 1) if n >= 2 else (s_sig, n + 1))
            if n >= 1:
                if n == 1:
                    pe.wait_ge(s_sig, KC)
                gates(n - 1)
            block(c0 + 2 * n + 1, 2 + n % 2, (gl, n - 1) if n >= 2 else (s_sig, 3 + n))
        gates(KC - 1)

    def s_rec_act(act):
        c0 = FIRST["s_rec"]

        def high(n):
            act.wait_ge(rc, n + 1)
            nc.scalar.activation(rec_hi[:, n, :], rec[:, n % 2, :], ACT.Copy).then_inc(rhi, 1)

        for n in range(KC + 1):
            m = n - 1
            if n < KC:
                split_hi(act, c0 + 2 * n + RING)
                act.wait_ge(w_used, c0 + 2 * n + 1)
                if n >= 1:
                    act.wait_ge(cv, n)
                nc.scalar.activation(xpad[:, CONV - 1:CONV - 1 + S], ps[:, n % 2, :], ACT.Copy).then_inc(xp, 1)
            if m >= 0:
                act.wait_ge(ga, m + 1)
                if m >= 1:
                    act.wait_ge(rc, m)
                nc.scalar.activation(r_g[:], ps[:, 4 + m % 2, :], ACT.Sigmoid, bias=lru_ba[:, m:m + 1])
                nc.scalar.activation(i_g[:], ps[:, 6 + m % 2, :], ACT.Sigmoid, bias=lru_bx[:, m:m + 1]
                                     ).then_inc(sig, 1)
                act.wait_ge(sig, m + 1)
                nc.scalar.activation(a_g[:], r_g[:], ACT.Exp, scale=lru_s8[:, m:m + 1]).then_inc(ex, 1)
                nc.scalar.activation(tau[:], r_g[:], ACT.Tanh, scale=lru_n8[:, m:m + 1]).then_inc(th, 1)
            if n < KC:
                split_hi(act, c0 + 2 * n + 1 + RING)
                act.wait_ge(w_used, c0 + 2 * n + 2)
                if n >= 2:
                    act.wait_ge(rc, n - 1)
                nc.scalar.activation(gy[:, n % 2, :], ps[:, 2 + n % 2, :], ACT.Gelu_apprx_tanh).then_inc(gl, 1)
            if m >= 1:
                high(m - 1)
            if m >= 0:
                act.wait_ge(qq, m + 1)
                nc.scalar.activation(tau[:], tau[:], ACT.Sqrt, scale=2.0).then_inc(sqr, 1)
        high(KC - 1)

    def s_rec_dve(dve):
        link(dve, nc.vector.memset(xpad[:, 0:CONV - 1], 0.0))

        def low(n):
            dve.wait_ge(rhi, n + 1)
            nc.vector.tensor_tensor(rec_l[:, n, :], rec[:, n % 2, :], rec_hi[:, n, :].bitcast(F32), ALU.subtract
                                    ).then_inc(rec_lo, 1)
            dve.wait_ge(rec_lo, n + 1)

        for n in range(KC + 1):
            m = n - 1
            if n < KC:
                dve.wait_ge(xp, n + 1)
                if n >= 2:
                    dve.wait_ge(ga, n - 1)
                x = xconv[:, n % 2, :]
                link(dve, nc.vector.tensor_scalar(x, xpad[:, 0:S], conv_w[:, n, 0:1], conv_b[:, n:n + 1], ALU.mult, ALU.add))
                for j in range(1, CONV):
                    ins = nc.vector.scalar_tensor_tensor(out=x, in0=xpad[:, j:j + S], scalar=conv_w[:, n, j:j + 1], in1=x,
                                                         op0=ALU.mult, op1=ALU.add)
                    if j < CONV - 1:
                        link(dve, ins)
                ins.then_inc(cv, 1)
            if m >= 0:
                dve.wait_ge(th, m + 1)
                link(dve, nc.vector.tensor_scalar(r_g[:], tau[:], 1.0, None, ALU.add))
                link(dve, nc.vector.reciprocal(r_g[:], r_g[:]))
                nc.vector.tensor_tensor(tau[:], tau[:], r_g[:], ALU.mult).then_inc(qq, 1)
                link(dve, nc.vector.tensor_tensor(i_g[:], i_g[:], xconv[:, m % 2, :], ALU.mult))
                if m >= 1:
                    low(m - 1)
                dve.wait_ge(sqr, m + 1)
                link(dve, nc.vector.tensor_tensor(i_g[:], i_g[:], tau[:], ALU.mult))
                h = rec[:, m % 2, :]
                link(dve, nc.vector.tensor_tensor_scan(h, a_g[:], i_g[:], 0.0, ALU.mult, ALU.add))
                dve.wait_ge(gl, m + 1)
                nc.vector.tensor_tensor(h, h, gy[:, m % 2, :], ALU.mult).then_inc(rc, 1)
                dve.wait_ge(rc, m + 1)
        low(KC - 1)

    def s_grec_act(act):
        for n in range(KC):
            split_hi(act, FIRST["s_grec"] + n + RING)
            act.wait_ge(w_used, FIRST["s_grec"] + n + 1)
            nc.scalar.activation(grs[:, n, :], ps[:, n, :], ACT.Sigmoid).then_inc(s_grs, 1)

    mg = at("mg", [2, S], SCR)

    def s_reco_act(act):
        for n in range(KC):
            split_hi(act, FIRST["s_reco"] + n + RING)
            act.wait_ge(merged, n + 1)
            nc.scalar.activation(n_hi[:, n, :], att[:, n, :], ACT.Copy).then_inc(merged_hi, 1)

    def s_reco_dve(dve):
        for n in range(KC + 1):
            if n < KC:
                dve.wait_ge(w_used, FIRST["s_reco"] + n + 1)
                dve.wait_ge(s_grs, n + 1)
                link(dve, nc.vector.tensor_tensor(mg[:, n % 2, :], ps[:, n, :], grs[:, n, :], ALU.mult))
                nc.vector.tensor_tensor(att[:, n, :], att[:, n, :], mg[:, n % 2, :], ALU.add).then_inc(merged, 1)
                dve.wait_ge(merged, n + 1)
            if n >= 1:
                dve.wait_ge(merged_hi, n)
                nc.vector.tensor_tensor(n_lo[:, n - 1, :], att[:, n - 1, :], n_hi[:, n - 1, :].bitcast(F32), ALU.subtract
                                        ).then_inc(merged_lo, 1)

    sp_exp, sp_u_ready = sem("softplus_exp"), sem("softplus_u")
    sp_abs, sp_neg, sp_e, sp_u, sp_l, sp_m, sp_d = (at("sp" + n, [KC], SCR + 8 * T + 32 * i) for i, n in enumerate(
        ("_abs", "_neg", "_e", "_u", "_l", "_m", "_d")))

    def softplus_dve(dve):
        lam = lru_s8[:]
        link(dve, nc.vector.tensor_scalar(nsink[:], nsink[:], -1.0, None, ALU.mult))
        link(dve, nc.vector.tensor_scalar(sp_neg[:], lam, -1.0, None, ALU.mult))
        nc.vector.tensor_tensor(sp_abs[:], sp_neg[:], lam, ALU.max).then_inc(setup, 1)
        dve.wait_ge(sp_exp, 1)
        nc.vector.tensor_scalar(sp_u[:], sp_e[:], 1.0, None, ALU.add).then_inc(sp_u_ready, 1)
        dve.wait_ge(sp_u_ready, 1)
        link(dve, nc.vector.tensor_scalar(sp_m[:], sp_u[:], 1.0, None, ALU.is_equal))
        link(dve, nc.vector.scalar_tensor_tensor(out=sp_d[:], in0=sp_u[:], scalar=1.0, in1=sp_m[:], op0=ALU.subtract,
                                                 op1=ALU.add))
        link(dve, nc.vector.reciprocal(sp_d[:], sp_d[:]))
        link(dve, nc.vector.tensor_tensor(sp_d[:], sp_d[:], sp_e[:], ALU.mult))
        link(dve, nc.vector.tensor_tensor(sp_m[:], sp_m[:], sp_e[:], ALU.mult))
        dve.wait_ge(sp_exp, 2)
        link(dve, nc.vector.tensor_tensor(sp_d[:], sp_d[:], sp_l[:], ALU.mult))
        link(dve, nc.vector.tensor_tensor(sp_d[:], sp_d[:], sp_m[:], ALU.add))
        link(dve, nc.vector.scalar_tensor_tensor(out=sp_d[:], in0=sp_neg[:], scalar=0.0, in1=sp_d[:], op0=ALU.max,
                                                 op1=ALU.add))
        link(dve, nc.vector.tensor_scalar(lru_n8[:], sp_d[:], LRU_C, None, ALU.mult))
        link(dve, nc.vector.tensor_scalar(lru_s8[:], sp_d[:], -LRU_C, None, ALU.mult))

    l0_in, l1_in = in_stage(0), in_stage(1)
    for st, name in ((l0_in, "l0_mix_pre"), (l1_in, "l1_mix_pre")):
        st["h_base"] = 8 * before(name, "_pre")
    l0_ffn = ffn("l0_ffn", 2, (h_hi, h_lo), y, "l0_ffn_post", (MOD1, 6, 2, modv_b))
    l1_ffn = ffn("l1_ffn", 1, (n_hi, n_lo), y1, "l1_ffn_post", (MOD2, 9, 3, modv_a))
    OUT_MODS = [3] * 6 + [2] * 2
    s_ffn1 = ffn("s_ffn1", 1, (n_hi, n_lo), y1, "s0_post")
    s_ffn2 = ffn("s_ffn2", 1, (n_hi, n_lo), y1, "s2_post")
    out_stored = sem("out_stored")
    LATE = ["mask_in", "rel_in", "lru_wa_in", "lru_wx_in"]

    def stream_x(si, k):
        return xs[si][:, k, :]

    def stream_y(si, k):
        off, n = segs(2)[si]
        return y[:, k, off:off + n]

    def stream_y1(si, k):
        return y1[:, k, :]

    block = ctx.enter_context(nc.Block())

    @block.sync
    def _(sp):
        sp.dma_start(loaded[:], A["consts"]).then_inc(const_landed, 16)

        def first_mods(i):
            n = MOD_FIRST // FIRST_LOADS
            sp.dma_start(modfirst[:, i * n:(i + 1) * n, :], A["mod_stream"][i * n:(i + 1) * n].rearrange("c p n -> p c n")
                         ).then_inc(first_landed[i], 16)

        sp.dma_start(c_rows, A["c_rows"]).then_inc(c_landed, 16)
        first_mods(0)
        sp.dma_start(xl[:], A["x_in"]).then_inc(x_landed, 16)
        sp.dma_start(xc[:], A["ctx_in"]).then_inc(x_landed, 16)
        for i in range(1, FIRST_LOADS):
            first_mods(i)
        for c in range(RING):
            load_block(sp, c)

        def attention_stream(a):
            sp.wait_ge(a["s_pv"], ATT_ITERS * a["nu"])

        def stage(name):
            count = dict(STAGES)[name]
            repeat(sp, FIRST[name] + RING, min(FIRST[name] + count + RING, NBLK), load_block)

        def ffn_stream(f):
            m0, start, each, _ = f["mods"]

            def mods(g, part, i):
                for j in range(each):
                    load_mod(sp, m0 + start + each * (2 * g + part) + j, i, 4 * each)

            load_block(sp, f["c0"] + RING)
            load_block(sp, f["c0"] + RING + 1)
            for j in range(start):
                load_mod(sp, m0 + j)

            def step(c, d, group, last):
                g, _, i = group
                load_block(sp, c + RING, d)
                load_block(sp, c + RING + 1, d)
                mods(g, 0, i)
                load_block(sp, c + RING + 2, d)
                load_block(sp, c + RING + 3, d)
                if not last:
                    mods(g, 1, i)
                    load_block(sp, c + RING + 4, d)
                    load_block(sp, c + RING + 5, d)

            ffn_groups(sp, f, step)

        load_mod(sp, MOD_FIRST)
        for i in range(10):
            load_block(sp, FIRST["l0_in"] + RING + i)
            load_mod(sp, MOD_FIRST + 1 + i)
        stage("l0_pool")
        attention_stream(l0_att)
        c = MOD_IN + 1
        for n in range(KC):
            load_block(sp, FIRST["l0_out"] + RING + n)
            for _ in range(OUT_MODS[n] if n < KC - 1 else OUT_MODS[n] - 1):
                load_mod(sp, c)
                c += 1
        ffn_stream(l0_ffn)
        stage("l1_in")
        sp.wait_ge(w_used, FIRST["l1_out"])
        sp.dma_start(mask_raw[:], A["mask_in"]).then_inc(late_landed, 16)
        sp.wait_ge(mod_ops, 2 * MOD2)
        sp.dma_start(c2_row, A["c2_row"]).then_inc(c_landed, 16)
        attention_stream(l1_att)
        stage("l1_out")
        ffn_stream(l1_ffn)
        stage("s_ffn1")
        sp.wait_ge(w_used, FIRST["s_in"])
        sp.dma_start(rel[:], A["rel_in"]).then_inc(late_landed, 16)
        sp.dma_start(lru_wa[:], A["lru_wa_in"]).then_inc(late_landed, 16)
        sp.dma_start(lru_wx[:], A["lru_wx_in"]).then_inc(late_landed, 16)
        stage("s_in")
        attention_stream(s_att)
        for name in ("s_atto", "s_gatt", "s_rec", "s_grec", "s_reco", "s_out", "s_ffn2"):
            stage(name)
        for k in range(KC):
            x_chunk(sp, before("s2_post", "_post") + 1, k)
            sp.dma_start(A["out"][:, k, :], xl[:, k, :]).then_inc(out_stored, 16)
        sp.wait_ge(out_stored, 16 * KC)

    @block.scalar
    def _(act):
        act.wait_ge(const_landed, 16)
        act.wait_ge(c_landed, 16)
        nc.scalar.activation(c_rows, c_rows, ACT.Silu).then_inc(cact_ready, 1)
        act.wait_ge(setup, 2)
        nc.scalar.activation(sp_e[:], sp_abs[:], ACT.Exp, scale=-1.0).then_inc(sp_exp, 1)
        act.wait_ge(sp_u_ready, 1)
        nc.scalar.activation(sp_l[:], sp_u[:], ACT.Ln).then_inc(sp_exp, 1)
        norm_act(act, "l0_mix_pre", stream_x, lambda eng, k: eng.wait_ge(x_landed, 32))
        for c in range(RING):
            split_hi(act, c)
        pre_act(act, "l0_mix_pre", 0, h_hi)
        in_act(act, l0_in)
        pool_act(act, l0_in)
        att_act(act, l0_att)
        out_act(act, "l0_out")
        norm_act(act, "l0_mix_post", stream_y, out_y_ready("l0_out"))
        norm_act(act, "l0_ffn_pre", stream_x, x_done("l0_ffn_pre"))
        pre_act(act, "l0_ffn_pre", 1, h_hi)
        ffn_act(act, l0_ffn)
        norm_act(act, "l0_ffn_post", stream_y, ffn_y_ready(l0_ffn))
        norm_act(act, "l1_mix_pre", stream_x, x_done("l1_mix_pre"))
        pre_act(act, "l1_mix_pre", 0, h_hi)
        in_act(act, l1_in)
        act.wait_ge(c_landed, 32)
        nc.scalar.activation(c2_row, c2_row, ACT.Silu).then_inc(cact_ready, 1)
        att_act(act, l1_att)
        out_act(act, "l1_out")
        norm_act(act, "l1_mix_post", stream_y1, out_y_ready("l1_out"))
        norm_act(act, "l1_ffn_pre", stream_x, x_done("l1_ffn_pre"))
        pre_act(act, "l1_ffn_pre", 1, n_hi)
        ffn_act(act, l1_ffn)
        norm_act(act, "l1_ffn_post", stream_y1, ffn_y_ready(l1_ffn))
        norm_act(act, "s0_pre", stream_x, x_done("s0_pre"))
        pre_act(act, "s0_pre", 0, n_hi)
        ffn_act(act, s_ffn1)
        norm_act(act, "s0_post", stream_y1, ffn_y_ready(s_ffn1))
        norm_act(act, "s1_pre", stream_x, x_done("s1_pre"))
        pre_act(act, "s1_pre", 1, n_hi)
        s_in_act(act)
        att_act(act, s_att)
        repeat(act, FIRST["s_atto"] + RING, FIRST["s_gatt"] + RING, split_hi)
        s_gatt_act(act)
        s_rec_act(act)
        s_grec_act(act)
        s_reco_act(act)
        out_act(act, "s_out")
        norm_act(act, "s1_post", stream_y1, out_y_ready("s_out"))
        norm_act(act, "s2_pre", stream_x, x_done("s2_pre"))
        pre_act(act, "s2_pre", 2, n_hi)
        ffn_act(act, s_ffn2)
        norm_act(act, "s2_post", stream_y1, ffn_y_ready(s_ffn2))

    @block.vector
    def _(dve):
        dve.wait_ge(const_landed, 16)
        softplus_dve(dve)
        dve.wait_ge(cact_ready, 1)
        for c in range(MOD_FIRST):
            mod_block(dve, c, [modv_a[m][:, c:c + 1] for m in range(2)], flat[:, 6 * 512:8 * 512])
        mod_bias(dve, MOD0, MOD_FIRST, modv_a, MOD0)
        vectors(dve, modv_a, 0, 0, 0, 1, None)
        pre_dve(dve, "l0_mix_pre", 0, h_hi, h_lo)
        in_dve(dve, l0_in)
        pool_dve(dve, l0_in)
        att_dve(dve, l0_att)

        def out_mods(n):
            for j in range(OUT_MODS[n]):
                c = MOD_IN + sum(OUT_MODS[:n]) + j
                mod_block(dve, c, [modv_a[m][:, c:c + 1] for m in range(2)], dump[:])

        out_dve(dve, "l0_out", y, 2, out_mods)
        mod_bias(dve, MOD_FIRST, MOD1, modv_a, MOD0)
        vectors(dve, modv_a, 0, 0, None, None, 2)
        vectors(dve, modv_a, 1, 1, 3, 4, 5)
        post_dve(dve, "l0_mix_post", 0, y)
        pre_dve(dve, "l0_ffn_pre", 1, h_hi, h_lo)
        ffn_dve(dve, l0_ffn)
        post_dve(dve, "l0_ffn_post", 1, y)
        dve.wait_ge(n_t, 8 * before("l1_mix_pre"))
        dve.wait_ge(mod_copied, 2 * NG - 1)
        mod_bias(dve, MOD1, MOD2, modv_b, MOD1)
        vectors(dve, modv_b, 2, 0, 0, 1, 2)
        vectors(dve, modv_b, 3, 1, 3, 4, 5)
        pre_dve(dve, "l1_mix_pre", 0, h_hi, h_lo)
        in_dve(dve, l1_in)
        dve.wait_ge(late_landed, 16)
        nc.vector.tensor_copy(mask[:], mask_raw[:])
        nc.vector.tensor_copy(ident_r[:], ident[:]).then_inc(sem("mask_ready"), 1)
        att_dve(dve, l1_att)
        out_dve(dve, "l1_out", y1, 1)
        post_dve(dve, "l1_mix_post", 0, y1)
        pre_dve(dve, "l1_ffn_pre", 1, n_hi, n_lo)
        dve.wait_ge(cact_ready, 2)
        ffn_dve(dve, l1_ffn)
        post_dve(dve, "l1_ffn_post", 1, y1)
        dve.wait_ge(n_t, 8 * before("s0_pre"))
        dve.wait_ge(mod_copied, 2 * (2 * NG - 1))
        mod_bias(dve, MOD2, NMOD, modv_a, MOD2)
        for sub, res in enumerate((0.5, 1.0, 0.5)):
            vectors(dve, modv_a, 4 + sub, sub, 3 * sub, 3 * sub + 1, 3 * sub + 2, res)
        pre_dve(dve, "s0_pre", 0, n_hi, n_lo)
        ffn_dve(dve, s_ffn1)
        post_dve(dve, "s0_post", 0, y1)
        pre_dve(dve, "s1_pre", 1, n_hi, n_lo)
        s_in_dve(dve)
        bias_dve(dve)
        att_dve(dve, s_att)
        s_atto_dve(dve)
        s_gatt_dve(dve)
        s_rec_dve(dve)
        s_reco_dve(dve)
        out_dve(dve, "s_out", y1, 1)
        post_dve(dve, "s1_post", 1, y1)
        pre_dve(dve, "s2_pre", 2, n_hi, n_lo)
        ffn_dve(dve, s_ffn2)
        post_dve(dve, "s2_post", 2, y1)

    @block.gpsimd
    def _(pool):
        nc.gpsimd.memset(ones[:], 1.0)
        nc.gpsimd.memset(eps_col[:], EPS).then_inc(setup, 1)

        def stage(c0, c1):
            repeat(pool, c0 + RING, min(c1 + RING, NBLK), split_lo)

        def ffn_stage(f, pre_name, n):
            x_chunk(pool, before(pre_name, "_post"), DVE_ADDS[-1])
            x_chunk(pool, before(pre_name, "_post"), POOL_ADDS[-1])
            nc.gpsimd.memset(f["y"][:, :, 0:n], 0.0).then_inc(y_zero, 1)
            stage(f["c0"], f["c0"] + FFN_BLOCKS)

        repeat(pool, 0, RING, split_lo)
        in_pool(pool, l0_in)
        split_lo(pool, FIRST["l0_pool"] + RING)
        att_pool(pool, l0_att, lambda eng: eng.wait_ge(l0_in["mix_lo"], 4))
        stage(FIRST["l0_out"], FIRST["l0_ffn"])
        post_pool(pool, "l0_mix_post", y)
        ffn_stage(l0_ffn, "l0_ffn_pre", T)
        post_pool(pool, "l0_ffn_post", y)
        in_pool(pool, l1_in)
        att_pool(pool, l1_att, lambda eng: eng.wait_ge(l1_in["lo"], 10))
        stage(FIRST["l1_out"], FIRST["l1_ffn"])
        post_pool(pool, "l1_mix_post", y1)
        ffn_stage(l1_ffn, "l1_ffn_pre", S)
        post_pool(pool, "l1_ffn_post", y1)
        ffn_stage(s_ffn1, "s0_pre", S)
        post_pool(pool, "s0_post", y1)
        stage(FIRST["s_in"], FIRST["s_atto"])
        att_pool(pool, s_att, lambda eng: eng.wait_ge(s_lo, 12))
        stage(FIRST["s_atto"], FIRST["s_ffn2"])
        post_pool(pool, "s1_post", y1)
        ffn_stage(s_ffn2, "s2_pre", S)
        post_pool(pool, "s2_post", y1)

    @block.tensor
    def _(pe):
        pe.wait_ge(setup, 2)
        norm_pe(pe, "l0_mix_pre")
        in_pe(pe, l0_in)
        pool_pe(pe, l0_in)

        def l0_free(pe):
            pe.wait_ge(l0_in["mix_lo"], 4)

        att_pe(pe, l0_att, l0_free)
        m_done(pe, l0_att)
        out_pe_two(pe, "l0_out", (h_hi, h_lo))
        pe.wait_ge(sem("l0_out_y"), 5)
        norm_pe(pe, "l0_mix_post")
        norm_pe(pe, "l0_ffn_pre")
        ffn_pe(pe, l0_ffn)
        norm_pe(pe, "l0_ffn_post")
        norm_pe(pe, "l1_mix_pre")
        in_pe(pe, l1_in)

        def l1_free(pe):
            pe.wait_ge(l1_in["out"], 10)
            pe.wait_ge(l1_in["v_lo"], 3)
            pe.wait_ge(sem("mask_ready"), 1)

        att_pe(pe, l1_att, l1_free)
        m_done(pe, l1_att)
        out_pe_one(pe, "l1_out", (n_hi, n_lo))
        norm_pe(pe, "l1_mix_post")
        norm_pe(pe, "l1_ffn_pre")
        ffn_pe(pe, l1_ffn)
        norm_pe(pe, "l1_ffn_post")
        norm_pe(pe, "s0_pre")
        ffn_pe(pe, s_ffn1)
        norm_pe(pe, "s0_post")
        norm_pe(pe, "s1_pre")
        s_in_pe(pe)

        def s_free(pe):
            pe.wait_ge(s_lo, 12)
            pe.wait_ge(sem("rel_ready"), 1)

        att_pe(pe, s_att, s_free)
        s_atto_pe(pe)
        eight_pe(pe, "s_gatt", (n_hi, n_lo), lambda i, j: pe.wait_ge(att_done, i * 2 + j // 2 + 1))
        s_rec_pe(pe)

        def grec_free(i, j):
            pe.wait_ge(gl, KC)
            pe.wait_ge(sig, i * (KC - 1) + 1)

        eight_pe(pe, "s_grec", (n_hi, n_lo), grec_free)
        pe.wait_ge(rec_lo, KC)
        eight_pe(pe, "s_reco", (rec_hi, rec_l), lambda i, j: pe.wait_ge(s_grs, i * RING + j + 1))
        pe.wait_ge(merged_lo, KC)
        out_pe_one(pe, "s_out", (n_hi, n_lo))
        norm_pe(pe, "s1_post")
        norm_pe(pe, "s2_pre")
        ffn_pe(pe, s_ffn2)
        norm_pe(pe, "s2_post")


INPUTS = (("x_in", [P, KC, S]), ("ctx_in", [P, KC, C]), ("consts", [P, PACKED]), ("c_rows", [P, 2, D]), ("c2_row", [P, D]), ("w_stream", [NBLK, P, BLK]),
          ("mod_stream", [NMOD, P, BLK]), ("mask_in", [P, 2, P]), ("rel_in", [P, 8, 2 * P]),
          ("lru_wa_in", [P, KC, P]), ("lru_wx_in", [P, KC, P]))


def kernel(**inputs):
    import concourse.bacc as _bacc
    from concourse.bass_utils import run_bass_kernel_spmd as _run

    a = {k: np.asarray(v) for k, v in inputs.items()}

    def chunks(v):
        v = v.reshape(v.shape[:-1] + (v.shape[-1] // P, P))
        return np.moveaxis(v, -1, 0)

    def tokens(x):
        return np.ascontiguousarray(x.T.reshape(-1, P, x.shape[0]).transpose(1, 0, 2))

    def blocks(w):
        k, n = w.shape
        return w.reshape(k // P, P, n // P, P).transpose(2, 1, 0, 3)

    def wide(w):
        n = w.shape[1]
        return w.reshape(n // P, BLK // n, P, n).transpose(0, 2, 1, 3).reshape(n // P, P, 8, P)

    def heads(*hs):
        return np.concatenate([np.arange(h * HD, (h + 1) * HD) for h in hs])

    stream = np.empty((NBLK, P, 8, P), np.float32)

    def put(name, *parts):
        c = FIRST[name]
        for part in parts:
            stream[c:c + len(part)] = part
            c += len(part)
        assert c == FIRST[name] + dict(STAGES)[name]

    def put_ffn(name, w_in, w_out):
        gate, up = blocks(w_in[:, :FH]), blocks(w_in[:, FH:])
        out = w_out.reshape(NH, 1, P, 8, P)
        order = [gate[0:1], up[0:1]]
        for g in range(NG):
            b = 2 * g + 1
            order += [gate[b:b + 1], up[b:b + 1]]
            if g < NG - 1:
                order += [gate[b + 1:b + 2], up[b + 1:b + 2]]
            order += [out[2 * g], out[b]]
        put(name, *order)

    we, weo, wo, woo = a["we_in"][0], a["we_out"][0], a["wo_in"][0], a["wo_out"][0]
    q0 = np.concatenate([heads(c, c + 4) for c in range(4)])
    put("l0_in", blocks(we[:, 512:640]), blocks(we[:, q0[:P]]), blocks(we[:, 640:768]), blocks(we[:, q0[P:]]),
        blocks(we[:, 768:]))
    stream[FIRST["l0_pool"]] = 0.0
    stream[FIRST["l0_pool"], :, 0:4] = a["we_pool"][0].transpose(1, 0, 2)
    put("l0_out", blocks(np.concatenate([weo[q0], weo[512:]])))
    q1 = np.concatenate([heads(8 * (ci % 2) + ci // 2, 8 * (ci % 2) + 4 + ci // 2) for ci in range(8)])
    put("l1_in", blocks(wo[:, 1024:1280]), wide(wo[:, 1280:1536]), blocks(wo[:, q1]))
    put("l1_out", blocks(woo[q1]))
    put_ffn("l0_ffn", a["w_ffn_in"][0], a["w_ffn_out"][0])
    put_ffn("l1_ffn", a["w_ffn_in"][1], a["w_ffn_out"][1])
    put_ffn("s_ffn1", a["ffn1_w_gu_2"][0], a["ffn1_w_down_2"][0])
    put_ffn("s_ffn2", a["ffn2_w_gu_2"][0], a["ffn2_w_down_2"][0])
    ws = blocks(a["w_in_2"][0])
    put("s_in", ws[0:8], wide(a["w_in_2"][0][:, 1024:1536]))
    xr, yr, ga, gr = ws[12:20], ws[20:28], ws[28:36], ws[36:44]
    atto = blocks(a["w_att_o_2"][0])
    put("s_atto", np.concatenate([atto[0::2], atto[1::2]], axis=2))
    put("s_gatt", ga)
    put("s_rec", np.stack([xr, yr], 1).reshape(16, P, 8, P))
    put("s_grec", gr)
    put("s_reco", blocks(a["w_rec_o_2"][0]))
    put("s_out", blocks(a["w_out_2"][0]))
    mods = np.concatenate([a["w_mod"][0].T, a["w_mod"][1].T, a["w_ada_2"][0].T])

    p = np.arange(P)
    ident = np.eye(P, dtype=np.float32)
    blkones = (p[:, None] // HD == p[None, :] // HD).astype(np.float32)
    freqs = 10000.0 ** (-np.arange(16) / 16)
    t = np.arange(S)
    pos = np.where((p % HD < 32)[:, None], t[None, :] // 64, t[None, :] % 64)
    ang = (pos.astype(np.float32) * freqs[p % 16].astype(np.float32)[:, None]).astype(np.float32)
    cos = np.cos(ang).astype(np.float32)
    sin = (np.sin(ang) * np.where(p % 32 < 16, -1.0, 1.0)[:, None]).astype(np.float32)
    edges = np.ones((4, 2, 8), np.float32)
    for g, w in enumerate(POOL_W):
        for e in range(8):
            edges[g, 0, e] = w / (e + w - w // 2) if e < w // 2 else 1.0
            left = 7 - e
            edges[g, 1, e] = w / (w // 2 + min(left + 1, w - w // 2))
    prev = np.where(p[None, :] >= p[:, None], 0.0, MASKED)
    nxt = np.where(p[None, :] <= p[:, None], 0.0, MASKED)

    def rows(v):
        return np.broadcast_to(v.reshape(1, -1), (P, v.size))

    gp = np.stack([a["g_pre_mix"][0], a["g_pre_ffn"][0], a["g_pre_mix"][1], a["g_pre_ffn"][1], *a["norm_pre_2"][0]])
    gq = np.stack([a["g_post_mix"][0], a["g_post_ffn"][0], a["g_post_mix"][1], a["g_post_ffn"][1], *a["norm_post_2"][0]])
    sink = a["wo_sink"][0][[8 * (ci % 2) + 4 * half + ci // 2 for ci in range(8) for half in range(2)]]
    rb = a["rel_bias_2"][0]
    packed = dict(
        ident=ident, blkones=blkones, cos=cos, sin=sin,
        bmod=chunks(np.concatenate([a["b_mod"][0], a["b_mod"][1], a["b_ada_2"][0]])), gpre=chunks(gp), gpost=chunks(gq),
        qk_gain=np.stack([np.tile(a["we_q_gain"][0], 2), np.tile(a["we_k_gain"][0], 2)], axis=1),
        pool_scale=chunks(a["we_pool_scale"][0]), edges=rows(edges), nsink=rows(sink), relc=rows(rb[:, 256]),
        conv_w=np.moveaxis(chunks(a["conv_w_2"][0]), 1, 2), conv_b=chunks(a["conv_b_2"][0]),
        lru_ba=chunks(a["lru_ba_2"][0]), lru_bx=chunks(a["lru_bx_2"][0]), lru_s8=chunks(a["lru_lambda_2"][0]))
    consts = np.zeros((P, PACKED), np.float32)
    off = 0
    for name, cols in CONSTS:
        n = int(np.prod(cols))
        consts[:, off:off + n] = packed[name].reshape(P, n)
        off += padded(cols)

    index = np.minimum(256 + p[:, None] - np.arange(2 * P)[None, :], 256)
    rel = np.ascontiguousarray(rb[:, index].transpose(1, 0, 2))

    def diagonal(w):
        out = np.zeros((P, KC, P), np.float32)
        out[0:HD, :, 0:HD] = w[0::2].transpose(1, 0, 2)
        out[HD:P, :, HD:P] = w[1::2].transpose(1, 0, 2)
        return out

    c_rows = np.stack([rows(a["c"][0]), rows(a["c_ctx"])], axis=1)
    arrays = dict(c_rows=c_rows, c2_row=np.ascontiguousarray(rows(a["c_2"][0])),
        
        x_in=tokens(a["x"][0]), ctx_in=tokens(a["ctx"][0]), consts=consts, w_stream=stream.reshape(NBLK, P, BLK),
        mod_stream=mods.reshape(NMOD, P, BLK),
        mask_in=np.stack([prev, nxt], axis=1).astype(np.float32), rel_in=rel,
        lru_wa_in=diagonal(a["lru_wa_2"][0]), lru_wx_in=diagonal(a["lru_wx_2"][0]))

    nc = _bacc.Bacc("TRN2", target_bir_lowering=False, num_devices=1)
    A = {name: nc.dram_tensor(name, shape, F32, kind="ExternalInput").ap() for name, shape in INPUTS}
    A["out"] = nc.dram_tensor("out", [P, KC, S], F32, kind="ExternalOutput").ap()
    build(nc, A)
    r = _run(nc, [arrays], core_ids=[0])
    out = r.results[0]["out"]
    return np.ascontiguousarray(out.transpose(2, 1, 0).reshape(1, S, D))
```

```python
from contextlib import ExitStack

import numpy as np

import concourse.bass as bass
from concourse import mybir

F32 = mybir.dt.float32
F32R = mybir.dt.float32r
ACT = mybir.ActivationFunctionType
ALU = mybir.AluOpType
AX = mybir.AxisListType

P = 128
D = 1024
KC = D // P
S, C = 512, 256
T = S + C
NQ = S // P
HD = 64
EPS = 1e-6
FH = 2816
NH = FH // P
NG = NH // 2
FFN_BLOCKS = 3 * NH
SCALE = HD ** -0.5
MASKED = -float(2.0 ** 100)
LRU_C = 8.0
CONV = 4
RING = 4
BLK = 8 * P
POOL_W = (2, 4, 8, 16)
PAD = 16
UCOLS = PAD + S + 2 * PAD + C + PAD
ROT = [(i + 16) % 32 for i in range(32)]

STAGES = [("l0_in", 10), ("l0_pool", 1), ("l0_out", 8), ("l0_ffn", FFN_BLOCKS),
          ("l1_in", 12), ("l1_out", 8), ("l1_ffn", FFN_BLOCKS),
          ("s_ffn1", FFN_BLOCKS), ("s_in", 12), ("s_atto", 4), ("s_gatt", 8), ("s_rec", 16),
          ("s_grec", 8), ("s_reco", 8), ("s_out", 8), ("s_ffn2", FFN_BLOCKS)]
FIRST = {}
NBLK = 0
for _name, _count in STAGES:
    FIRST[_name] = NBLK
    NBLK += _count
MOD0, MOD1, MOD2, NMOD = 0, 48, 96, 168
MOD_FIRST, MOD_IN, MOD_OUT, MOD_TAIL, MOD_LATE, MOD_LAST = 16, 22, 42, 88, 98, 138
SCALES_AHEAD, FIRST_AHEAD = 2, 2
FIRST_SEMS = 4
MOD_RING = 2
DVE_ADDS = (0, 3, 5, 7)
POOL_ADDS = tuple(k for k in range(KC) if k not in DVE_ADDS)

PASSES = ["l0_mix_pre", "l0_mix_post", "l0_ffn_pre", "l0_ffn_post", "l1_mix_pre", "l1_mix_post",
          "l1_ffn_pre", "l1_ffn_post", "s0_pre", "s0_post", "s1_pre", "s1_post", "s2_pre", "s2_post"]
PASS_SEGS = {p: 2 if p[:2] == "l0" or p == "l1_mix_pre" else 1 for p in PASSES}


CONSTS = [("ident", [P]), ("blkones", [P]), ("cos", [S]), ("sin", [S]),
          ("bmod", [NMOD]),
          ("gpre", [7, KC]), ("gpost", [7, KC]), ("qk_gain", [2]), ("pool_scale", [4]),
          ("edges", [4, 2, 8]),
          ("nsink", [16]),
          ("relc", [8]),
          ("conv_w", [KC, CONV]), ("conv_b", [KC]), ("lru_ba", [KC]), ("lru_bx", [KC]),
          ("lru_s8", [KC])]


def padded(cols):
    return (int(np.prod(cols)) + 7) // 8 * 8


PACKED = sum(padded(c) for _, c in CONSTS)


def segs(n):
    return [(0, S), (S, C)][:n]


def before(name, kind=""):
    return sum(p.endswith(kind) for p in PASSES[:PASSES.index(name)])


def build(nc, A):
    with ExitStack() as ctx:
        write_program(nc, A, ctx)


def write_program(nc, A, ctx):
    sems = {}

    def sem(name):
        if name not in sems:
            sems[name] = ctx.enter_context(nc.semaphore(name))
        return sems[name]

    X = 16512
    MIX = X + KC * S * 4
    XC, Y, HID = MIX, MIX + KC * C * 4, MIX + KC * C * 4 + KC * T * 4
    H = HID + 8 * T * 4
    HSPARE = H + 2 * KC * S * 4
    WHL = H + 2 * KC * T * 4
    RAW = WHL + 2 * RING * BLK * 4
    MODRAW = RAW + RING * BLK * 4
    SCR = MODRAW + RING * BLK * 4
    CONST = SCR + 15360
    cursor = [CONST]

    def at(name, cols, off, dt=F32):
        return nc.alloc_sbuf_tensor_at(name, [P] + cols, dt, offset=off)

    def const(name, cols, dt=F32):
        t = at(name, cols, cursor[0], dt)
        cursor[0] += 4 * padded(cols)
        return t

    xl, xc = at("xl", [KC, S], X), at("xc", [KC, C], XC)
    xs = [xl, xc]
    h_hi, h_lo = at("h_hi", [KC, T], H, F32R), at("h_lo", [KC, T], H + KC * T * 4, F32R)
    n_hi, n_lo = at("n_hi", [KC, S], H, F32R), at("n_lo", [KC, S], H + KC * S * 4, F32R)
    y = at("y", [KC, T], Y)
    y1 = at("y1", [KC, S], Y)
    w_hi, w_lo = at("w_hi", [RING, BLK], WHL, F32R), at("w_lo", [RING, BLK], WHL + RING * BLK * 4, F32R)
    raw = at("raw", [RING, BLK], RAW)
    modraw = at("modraw", [RING, BLK], MODRAW)
    c_rows, c2_row = modraw[:, 2:4, :], modraw[:, 3, :]
    c_line = nc.alloc_sbuf_tensor_at("c_line", [1, 2, D], F32, offset=RAW + 2 * BLK * 4)
    mod_pairs = [at("mod_pair0", [2, BLK], WHL + 2 * BLK * 4), modraw[:, 0:2, :]] + [
        at(f"mod_pair{k}", [2, BLK], Y + (k - 2) * 2 * BLK * 4) for k in range(2, KC)]

    loaded = const("loaded", [PACKED])
    place = {}
    for name, cols in CONSTS:
        place[name] = sum(padded(c) for _, c in CONSTS[:len(place)])

    def part(name, cols):
        view = loaded[:, place[name]:place[name] + int(np.prod(cols))]
        if len(cols) == 1:
            return view
        names = "abc"[:len(cols)]
        sizes = dict(zip(names, cols))
        return view.rearrange(f"p ({' '.join(names)}) -> p {' '.join(names)}", **sizes)

    (ident, blkones, cos, sin, bmod, gpre, gpost, qk_gain, pool_scale, edges, nsink, relc, conv_w,
     conv_b, lru_ba, lru_bx, lru_s8) = (part(n, c) for n, c in CONSTS)
    ones = const("ones", [P])
    lru_n8 = const("lru_n8", [KC])
    modv_a = [const("modv_l", [72]), const("modv_c", [72])]
    modv_b = [loaded[:, place[n]:place[n] + MOD1] for n in ("bmod", "edges")]
    c_cols = const("c_cols", [KC, 2])
    rms_t = const("rms_t", [T // 32])
    mod_acc = const("mod_acc", [8])
    vec_a = const("vec_a", [3, KC, 2])
    vec_b = const("vec_b", [3, KC, 2])
    vec_g = const("vec_g", [3, KC, 2])
    eps_col = const("eps_col", [1])
    smax, negm, rsum, esink, rinv = (const(n, [4]) for n in ("smax", "negm", "rsum", "esink", "rinv"))
    assert cursor[0] <= nc.sbuf_usable_end, (cursor[0], nc.sbuf_usable_end)

    nsq, tn = at("nsq", [2, T], SCR), at("tn", [2, T], SCR + 8 * T)
    n_rstd = at("n_rstd", [T], SCR + 16 * T)
    dump = at("dump", [BLK], SCR + 8 * T)
    sq, rstd = at("sq", [2, S], SCR), at("rstd", [T], SCR + 4096)
    qn, qraw, tsh = at("qn", [T], SCR + 7168), at("qraw", [T], SCR + 10240), at("tsh", [S], SCR + 13312)
    upad, sA, sB = (at(n, [UCOLS], SCR + 4096 + i * UCOLS * 4) for i, n in enumerate(("upad", "sA", "sB")))
    prob = at("prob", [2, T], SCR)
    qs_hi, qs_lo = at("qs_hi", [2, 2, P], SCR + 6144, F32R), at("qs_lo", [2, 2, P], SCR + 8192, F32R)
    opair, dg = at("opair", [2, P], SCR + 10240), at("dg", [2, P], SCR + 11264)
    dump_att = at("dump_att", [BLK], RAW + 16 * T)
    pt_hi, pt_lo = at("pt_hi", [2, T], RAW, F32R), at("pt_lo", [2, T], RAW + 8 * T, F32R)

    def mixer_buffers(tag, off, nq, tq, nk, tk, nv, wv):
        out = []
        for n, cols in (("q", [nq, tq]), ("k", [nk, tk]), ("v", [nv, wv])):
            for part in ("hi", "lo"):
                out.append(at(f"{tag}_{n}_{part}", cols, off, F32R))
                off += 4 * int(np.prod(cols))
        return out, off

    l0_qkv, _off = mixer_buffers("l0", Y, 4, T, 1, T, 6, P)
    d_hi, d_lo = at("d_hi", [2, T], _off, F32R), at("d_lo", [2, T], _off + 8 * T, F32R)
    assert _off + 16 * T == H
    l1_qkv, _off = mixer_buffers("l1", XC, 8, S, 2, T, 6, 2 * P)
    assert _off <= H
    s_qkv, _off = mixer_buffers("s", XC, 4, S, 4, S, 4, 4 * P)
    rel = at("rel", [8, 2 * P], _off)
    mask_raw, mask = at("mask_raw", [2, P], HSPARE), at("mask", [2, P], HSPARE + 1024, F32R)
    ident_r = at("ident_r", [P], HSPARE + 2048, F32R)
    o_hi, o_lo = at("o_hi", [4, S], HSPARE, F32R), at("o_lo", [4, S], HSPARE + 16 * S, F32R)

    ps = ctx.enter_context(nc.psum_tensor("ps", [P, 8, 512], F32))
    flat = ps[:].rearrange("p b n -> p (b n)")

    raw_landed = [sem(f"raw_landed{i}") for i in range(RING)]
    hi_ready, lo_ready = sem("hi_ready"), sem("lo_ready")
    w_used = sem("w_used")
    mod_landed = [sem(f"mod_landed{i}") for i in range(MOD_RING)]
    first_landed = [sem(f"mod_first_landed{k}") for k in range(FIRST_SEMS)]
    first_mods = sem("first_mods")
    mod_ops = sem("mod_ops")
    x_landed, const_landed, late_landed = sem("x_landed"), sem("const_landed"), sem("late_landed")
    setup = sem("setup")
    c_landed, cact_ready = sem("c_landed"), sem("cact_ready")
    mod_copied = sem("mod_copied")
    n_sq, n_ss, n_turn, n_rms = sem("n_sq"), sem("n_ss"), sem("n_turn"), sem("n_rms")
    n_t, n_h, h_ready, y_zero = sem("n_t"), sem("n_h"), sem("h_ready"), sem("y_zero")
    x_pool, x_dve = sem("x_pool"), sem("x_dve")
    dve_chain = sem("dve_chain")
    chain = [0]

    def link(dve, ins):
        chain[0] += 1
        ins.then_inc(dve_chain, 1)
        dve.wait_ge(dve_chain, chain[0])

    def load_block(sp, c, d=0):
        if c >= RING:
            sp.wait_ge(lo_ready, c - RING + 1 + d)
        sp.dma_start(raw[:, c % RING, :], A["w_stream"][bass.ds(c + d, 1)].rearrange("o p n -> (o p) n")
                     ).then_inc(raw_landed[c % RING], 16)

    def split_hi(act, c, d=0):
        if c >= NBLK:
            return
        act.wait_ge(raw_landed[c % RING], 16 * (c // RING + 1) + 4 * d)
        if c >= RING:
            act.wait_ge(w_used, c - RING + 1 + d)
        nc.scalar.activation(w_hi[:, c % RING, :], raw[:, c % RING, :], ACT.Copy).then_inc(hi_ready, 1)

    def split_lo(pool, c, d=0):
        if c >= NBLK:
            return
        pool.wait_ge(hi_ready, c + 1 + d)
        nc.gpsimd.tensor_tensor(w_lo[:, c % RING, :], raw[:, c % RING, :], w_hi[:, c % RING, :].bitcast(F32),
                                ALU.subtract).then_inc(lo_ready, 1)

    def repeat(eng, c0, c1, step):
        turns = (c1 - c0) // RING
        if turns > 1:
            with eng.Fori(0, turns) as i:
                for j in range(RING):
                    step(eng, c0 + j, i * RING)
            c0 += turns * RING
        for c in range(c0, c1):
            step(eng, c)

    def tiles(c):
        s = c % RING
        return [(w_hi[:, s, k * P:(k + 1) * P], w_lo[:, s, k * P:(k + 1) * P]) for k in range(8)]

    def product(w, x, outs, first, last):
        for i, (a, b) in enumerate(((0, 0), (0, 1), (1, 0))):
            for out, off, n in outs:
                mm = nc.tensor.matmul(out, w[a], x[b][:, off:off + n], start=first and i == 0, stop=last and i == 2)
        return mm

    def project(x_hi, x_lo, c, outs):
        for k, w in enumerate(tiles(c)):
            mm = product(w, (x_hi[:, k, :], x_lo[:, k, :]), outs, k == 0, k == 7)
        return mm

    def project_first(pe, x_hi, x_lo, c, outs, h_base, shared=(), beside=None):
        pe.wait_ge(lo_ready, c + 2)
        for k in range(KC):
            pe.wait_ge(h_ready, h_base + k + 1)
            for b in range(2):
                mm = product(tiles(c + b)[k], (x_hi[:, k, :], x_lo[:, k, :]), outs[b], k == 0, k == 7)
                if k == KC - 1 and (b == 0 or not shared):
                    mm.then_inc(w_used, 1)
            if beside:
                beside(k)
        if shared:
            project(x_hi, x_lo, c + 1, shared).then_inc(w_used, 1)

    def mods_of(c):
        tail = 2 * (KC + MOD_TAIL - MOD_FIRST)
        return (tail - 2 * (MOD_TAIL - c), 2) if c < MOD_TAIL else (tail + c - MOD_TAIL, 1)

    def load_mod(sp, c, i=0, n=0):
        ops, each = mods_of(c)
        slot, turn = (c - MOD_FIRST) % MOD_RING, (c - MOD_FIRST) // MOD_RING
        if turn > 0:
            sp.wait_ge(mod_ops, ops - (MOD_RING - 1) * each + i * (each * n))
        sp.dma_start(modraw[:, slot, :], A["mod_stream"][bass.ds(c - MOD_FIRST + i * n, 1)].rearrange("o p n -> (o p) n")
                     ).then_inc(mod_landed[slot], 16)

    def mod_block(dve, c, outs, where, i=0, n=0):
        ops, each = mods_of(c)
        slot, turn = (c - MOD_FIRST) % MOD_RING, (c - MOD_FIRST) // MOD_RING
        dve.wait_ge(mod_landed[slot], 16 * (turn + 1) + i * (n // MOD_RING * 16))
        for m in range(each):
            dve.wait_ge(mod_ops, ops + m + i * (each * n))
            nc.vector.tensor_tensor_reduce(where, modraw[:, slot, :], c_rows[:, m, :] if c < MOD2 else c2_row, 1.0, 0.0,
                                           ALU.mult, ALU.add, outs[m]).then_inc(mod_ops, 1)

    def first_there(eng, k):
        eng.wait_ge(first_landed[k % FIRST_SEMS], 16 * (k // FIRST_SEMS + 1))

    def first_mods_pe(pe, k):
        first_there(pe, k)
        for j in range(KC):
            mm = nc.tensor.matmul(ps[:, 4 + k % 2, 0:2], mod_pairs[k][:, 0, j * P:(j + 1) * P], c_cols[:, j, :],
                                  start=j == 0, stop=j == KC - 1)
        mm.then_inc(first_mods, 1)

    def first_scale(dve, k):
        first_there(dve, k)
        for m in range(2):
            if k + m > 0:
                dve.wait_ge(mod_ops, 2 * k + m)
            nc.vector.tensor_tensor_reduce(flat[:, 6 * 512:8 * 512], mod_pairs[k][:, 1, :], c_rows[:, m, :], 1.0, 0.0,
                                           ALU.mult, ALU.add, modv_a[0][:, 2 * k + m:2 * k + m + 1]).then_inc(mod_ops, 1)

    def first_vectors(dve, k):
        dve.wait_ge(first_mods, k + 1)
        nc.vector.tensor_scalar(vec_b[:, 0, k, :], ps[:, 4 + k % 2, 0:2], bmod[:, k:k + 1], None, ALU.add)
        dve.wait_ge(mod_ops, 2 * k + 2)
        link(dve, nc.vector.tensor_scalar(vec_a[:, 0, k, :], modv_a[0][:, 2 * k:2 * k + 2], bmod[:, KC + k:KC + k + 1], 1.0, ALU.add, ALU.add))
        link(dve, nc.vector.tensor_scalar(vec_a[:, 0, k, :], vec_a[:, 0, k, :], gpre[:, 0, k:k + 1], None, ALU.mult))

    def mod_group(dve, c, count, dst, where, i, n, number):
        ops, each = mods_of(c)
        first = MOD1 if c < MOD2 else MOD2
        dve.wait_ge(mod_copied, number)
        for j in range(count):
            mod_block(dve, c + j, [mod_acc[:, m * 4 + j:m * 4 + j + 1] for m in range(each)], where, i, n)
        dve.wait_ge(mod_ops, ops + each * count + i * (each * n))
        for m in range(each):
            ins = nc.vector.tensor_copy(dst[m][:, bass.ds(c - first + i * n, count)], mod_acc[:, m * 4:m * 4 + count])
        ins.then_inc(mod_copied, 1)

    def mod_bias(dve, c0, c1, dst, first):
        ops, each = mods_of(c1 - 1)
        dve.wait_ge(mod_ops, ops + each)
        for m in range(each):
            v = dst[m][:, c0 - first:c1 - first]
            ins = nc.vector.tensor_tensor(v, v, bmod[:, c0:c1], ALU.add)
        link(dve, ins)

    def vectors(dve, src, sub, slot, shift, scale, gate, res=1.0, nseg=2):
        for m in range(nseg):
            if scale is not None:
                nc.vector.scalar_tensor_tensor(out=vec_a[:, slot, :, m], in0=src[m][:, scale * KC:scale * KC + KC],
                                               scalar=1.0, in1=gpre[:, sub, :], op0=ALU.add, op1=ALU.mult)
                nc.vector.tensor_copy(vec_b[:, slot, :, m], src[m][:, shift * KC:shift * KC + KC])
            if gate is not None:
                nc.vector.scalar_tensor_tensor(out=vec_g[:, slot, :, m], in0=src[m][:, gate * KC:gate * KC + KC],
                                               scalar=res, in1=gpost[:, sub, :], op0=ALU.mult, op1=ALU.mult)

    def sum_bank(name, si):
        if name == "l0_mix_post":
            return 6 + si
        return (4 if name.endswith("_pre") else 0) + si

    def norm_square(act, name, src, ready, k):
        j = 8 * before(name) + k
        ready(act, k)
        if j >= 2:
            act.wait_ge(n_ss, j - 1)
        for si, (off, n) in enumerate(segs(PASS_SEGS[name])):
            ins = nc.scalar.activation(nsq[:, j % 2, off:off + n], src(si, k), ACT.Square)
        ins.then_inc(n_sq, 1)

    def norm_root(act, name):
        off, n = segs(PASS_SEGS[name])[-1]
        act.wait_ge(n_turn, before(name) + 1)
        nc.scalar.activation(rms_t[:, 0:(off + n) // 32], squares(n_rstd, off + n)[:, :, 0], ACT.Sqrt, scale=1.0 / D,
                             bias=eps_col[:, 0:1]).then_inc(n_rms, 1)

    def norm_act(act, name, src, ready, before_root=None):
        for k in range(KC):
            norm_square(act, name, src, ready, k)
        if before_root:
            before_root(act)
        norm_root(act, name)

    def squares(t, n):
        return t[:, 0:n].rearrange("p (b c) -> p b c", c=32)

    def turn_sums(banks, t):
        for (off, n), bank in zip(segs(2), banks):
            ins = nc.vector.transpose(t[:, off:off + n], bank[:, 0:n])
        return ins

    def turn_inverse(dve, t, n):
        link(dve, nc.vector.reciprocal(rms_t[:, 0:n // 32], rms_t[:, 0:n // 32]))
        link(dve, nc.vector.transpose(t[:, 0:n], rms_t[:, 0:n // 32].rearrange("p (b o) -> p b o", o=1
                                                                              ).to_broadcast([P, n // 32, 32])))

    def norm_pe(pe, name, chunks=range(KC)):
        for k in chunks:
            j = 8 * before(name) + k
            pe.wait_ge(n_sq, j + 1)
            for si, (off, n) in enumerate(segs(PASS_SEGS[name])):
                mm = nc.tensor.matmul(ps[:, sum_bank(name, si), 0:n], ones[:, :], nsq[:, j % 2, off:off + n],
                                      start=k == 0, stop=k == KC - 1)
            mm.then_inc(n_ss, 1)

    SUMS_BEHIND = 3

    def sums_behind(pe, name, n):
        if n >= SUMS_BEHIND:
            norm_pe(pe, name, [n - SUMS_BEHIND])

    def norm_dve(dve, name):
        nseg = PASS_SEGS[name]
        off, n = segs(nseg)[-1]
        dve.wait_ge(n_ss, 8 * before(name) + KC)
        turn_sums([ps[:, sum_bank(name, si), :] for si in range(nseg)], n_rstd).then_inc(n_turn, 1)
        dve.wait_ge(n_rms, before(name) + 1)
        turn_inverse(dve, n_rstd, off + n)
        return [n_rstd[:, off:off + n] for off, n in segs(nseg)]

    def pre_dve(dve, name, slot, dst_hi, dst_lo, first=False):
        tb, hb = 8 * before(name), 8 * before(name, "_pre")
        inv = norm_dve(dve, name)

        def scaled(k):
            for si, (off, n) in enumerate(segs(PASS_SEGS[name])):
                ins = nc.vector.scalar_tensor_tensor(out=tn[:, k % 2, off:off + n], in0=xs[si][:, k, :],
                                                     scalar=vec_a[:, slot, k, si:si + 1], in1=inv[si],
                                                     op0=ALU.mult, op1=ALU.mult)
            ins.then_inc(n_t, 1)

        def low(j):
            dve.wait_ge(n_h, hb + j + 1)
            for si, (off, n) in enumerate(segs(PASS_SEGS[name])):
                ins = nc.vector.scalar_tensor_tensor(out=dst_lo[:, j, off:off + n], in0=tn[:, j % 2, off:off + n],
                                                     scalar=vec_b[:, slot, j, si:si + 1],
                                                     in1=dst_hi[:, j, off:off + n].bitcast(F32),
                                                     op0=ALU.add, op1=ALU.subtract)
            ins.then_inc(h_ready, 1)
            dve.wait_ge(h_ready, hb + j + 1)

        if first:
            for k in range(KC):
                first_vectors(dve, k)
                scaled(k)
                if k + SCALES_AHEAD < KC:
                    first_scale(dve, k + SCALES_AHEAD)
                low(k)
            return
        for k in range(KC):
            scaled(k)
            if k >= 1:
                low(k - 1)
        low(KC - 1)

    def pre_act(act, name, slot, dst_hi):
        for k in range(KC):
            act.wait_ge(n_t, 8 * before(name) + k + 1)
            for si, (off, n) in enumerate(segs(PASS_SEGS[name])):
                ins = nc.scalar.activation(dst_hi[:, k, off:off + n], tn[:, k % 2, off:off + n], ACT.Identity,
                                           bias=vec_b[:, slot, k, si:si + 1])
            ins.then_inc(n_h, 1)

    def post_dve(dve, name, slot, acc):
        inv = norm_dve(dve, name)
        for k in range(KC):
            for si, (off, n) in enumerate(segs(PASS_SEGS[name])):
                t = acc[:, k, off:off + n]
                ins = nc.vector.scalar_tensor_tensor(out=t, in0=t, scalar=vec_g[:, slot, k, si:si + 1], in1=inv[si],
                                                     op0=ALU.mult, op1=ALU.mult)
            ins.then_inc(n_t, 1)
            if k in DVE_ADDS:
                dve.wait_ge(n_t, 8 * before(name) + k + 1)
                for si, (off, n) in enumerate(segs(PASS_SEGS[name])):
                    ins = nc.vector.tensor_tensor(xs[si][:, k, :], xs[si][:, k, :], acc[:, k, off:off + n], ALU.add)
                ins.then_inc(x_dve, 1)

    def post_pool(pool, name, acc):
        for k in POOL_ADDS:
            pool.wait_ge(n_t, 8 * before(name) + k + 1)
            for si, (off, n) in enumerate(segs(PASS_SEGS[name])):
                ins = nc.gpsimd.tensor_tensor(xs[si][:, k, :], xs[si][:, k, :], acc[:, k, off:off + n], ALU.add)
            ins.then_inc(x_pool, 1)

    def x_chunk(eng, posts, k):
        if k in DVE_ADDS:
            eng.wait_ge(x_dve, len(DVE_ADDS) * (posts - 1) + DVE_ADDS.index(k) + 1)
        else:
            eng.wait_ge(x_pool, len(POOL_ADDS) * (posts - 1) + POOL_ADDS.index(k) + 1)

    def x_done(name):
        return lambda eng, k: x_chunk(eng, before(name, "_post"), k)

    CREDIT = 2

    def ffn_buffers(nseg):
        n = segs(nseg)[-1][0] + segs(nseg)[-1][1]
        tag = f"ffn{nseg}_"
        return dict(hi=at(tag + "hi", [2, n], HID, F32R), lo=at(tag + "lo", [2, n], HID + 8 * n, F32R),
                    silu=at(tag + "silu", [2, n], HID + 16 * n), hid=at(tag + "hid", [2, n], HID + 24 * n))

    FFN_BUFS = {1: ffn_buffers(1), 2: ffn_buffers(2)}

    def ffn(name, nseg, x, acc, post, mods=None):
        return dict(name=name, mods=mods, post=post, c0=FIRST[name], segs=segs(nseg), x=x, y=acc, h_base=8 * (before(post, "_pre") - 1), index=[
            "l0_ffn", "l1_ffn", "s_ffn1", "s_ffn2"].index(name), **FFN_BUFS[nseg])

    def gate_bank(buf, si):
        return ps[:, 3 * buf, 0:S] if si == 0 else ps[:, 3 * buf + 2, 0:C]

    def up_bank(buf, si):
        return ps[:, 3 * buf + 1, 0:S] if si == 0 else ps[:, 3 * buf + 2, C:2 * C]

    FILL = {1: 4, 2: 2}

    def out_bank(f, n, si, last):
        if len(f["segs"]) == 1:
            return ps[:, (5, 6, 2, 7)[n % 4] if last else 5 + n % 2, 0:S]
        if last and n < 2:
            return (ps[:, (6, 0)[n], 0:S], ps[:, (7, 1)[n], 0:C])[si]
        return (ps[:, (3, 6)[n % 2], 0:S], ps[:, (4, 7)[n % 2], 0:C])[si]

    def ffn_groups(eng, f, step):
        n0 = f["c0"] + 2
        with eng.Fori(0, (NG - 1) // 2) as i:
            for half in range(2):
                step(n0 + 6 * half, i * 12, (half, i * 2, i), False)
        step(n0 + 6 * (NG - 1), 0, (NG - 1, 0, 0), True)

    def ffn_pe(pe, f):
        hid_ready, out_ready, out_free = (sem(f["name"] + s) for s in ("_hid_ready", "_out_ready", "_out_free"))
        ns = len(f["segs"])

        def in_block(c, d, bank, buf):
            pe.wait_ge(lo_ready, c + 1 + d)
            project(f["x"][0], f["x"][1], c, [(bank(buf, si), off, n) for si, (off, n) in enumerate(f["segs"])]
                    ).then_inc(w_used, 1)

        first = [[(bank(0, si), off, n) for si, (off, n) in enumerate(f["segs"])] for bank in (gate_bank, up_bank)]
        project_first(pe, f["x"][0], f["x"][1], f["c0"], [first[0], first[1][:1]], f["h_base"], first[1][1:])

        def step(c, d, group, last):
            g, gd = group[:2]
            pe.wait_ge(hid_ready, CREDIT + 2 * g + 2 * gd)
            if ns == 2:
                pe.wait_ge(out_free, CREDIT + 8 * g - 1 + 8 * gd)
            in_block(c, d, gate_bank, 1)
            in_block(c + 1, d, up_bank, 1)
            if not last:
                pe.wait_ge(hid_ready, CREDIT + 2 * g + 1 + 2 * gd)
                in_block(c + 2, d, gate_bank, 0)
                in_block(c + 3, d, up_bank, 0)
            oa = c + 2 if last else c + 4
            pe.wait_ge(lo_ready, oa + 2 + d)

            def halves(n, bs):
                for b in bs:
                    mm = product(tiles(oa + b)[n], (f["hi"][:, b, :], f["lo"][:, b, :]),
                                 [(out_bank(f, n, si, last), off, w) for si, (off, w) in enumerate(f["segs"])], b == 0, b == 1)
                return mm

            fill = FILL[ns] if last else 0
            if last:
                pe.wait_ge(hid_ready, CREDIT + 2 * g + 1 + 2 * gd)
                pe.wait_ge(out_free, CREDIT + 8 * g + 8 * gd)
                for n in range(fill):
                    halves(n, [0])
            pe.wait_ge(hid_ready, CREDIT + 2 * g + 2 + 2 * gd)
            for n in range(KC):
                if n >= fill:
                    pe.wait_ge(out_free, CREDIT + 8 * g + n - 1 + 8 * gd)
                mm = halves(n, [1] if n < fill else [0, 1])
                if last:
                    sums_behind(pe, f["post"], n)
                if n < KC - 1:
                    mm.then_inc(out_ready, 1)
            mm.then_inc(w_used, 2)

        ffn_groups(pe, f, step)

    def ffn_silu(act, f, c, d, buf):
        for si, (off, n) in enumerate(f["segs"]):
            act.wait_ge(w_used, c + 1 + si + d)
            nc.scalar.activation(f["silu"][:, buf, off:off + n], gate_bank(buf, si), ACT.Silu
                                 ).then_inc(sem(f["name"] + "_silu"), 1)

    def ffn_hidden_hi(act, f, m, md, out_c, out_d):
        ns = len(f["segs"])
        if out_c is not None:
            act.wait_ge(w_used, out_c + out_d)
        for si, (off, n) in enumerate(f["segs"]):
            act.wait_ge(sem(f["name"] + "_hid"), ns * m + si + 1 + ns * md)
            nc.scalar.activation(f["hi"][:, m % 2, off:off + n], f["hid"][:, m % 2, off:off + n], ACT.Copy
                                 ).then_inc(sem(f["name"] + "_hid_hi"), 1)

    def ffn_act(act, f):
        c0 = f["c0"]
        split_hi(act, c0 + RING)
        ffn_silu(act, f, c0, 0, 0)
        split_hi(act, c0 + RING + 1)
        ffn_hidden_hi(act, f, 0, 0, None, 0)

        def step(c, d, group, last):
            g, gd = group[:2]
            split_hi(act, c + RING, d)
            ffn_silu(act, f, c, d, 1)
            split_hi(act, c + RING + 1, d)
            ffn_hidden_hi(act, f, 2 * g + 1, 2 * gd, c, d)
            if not last:
                split_hi(act, c + RING + 2, d)
                ffn_silu(act, f, c + 2, d, 0)
                split_hi(act, c + RING + 3, d)
                split_hi(act, c + RING + 4, d)
                split_hi(act, c + RING + 5, d)
                ffn_hidden_hi(act, f, 2 * g + 2, 2 * gd, c + 6, d)

        ffn_groups(act, f, step)

    def ffn_last_blocks(f):
        def split(act):
            for c in range(f["c0"] + FFN_BLOCKS - 2, f["c0"] + FFN_BLOCKS):
                split_hi(act, c + RING)
        return split

    def ffn_mult(dve, f, m, md, c, d):
        ns = len(f["segs"])
        dve.wait_ge(w_used, c + 2 + d)
        for si, (off, n) in enumerate(f["segs"]):
            dve.wait_ge(sem(f["name"] + "_silu"), ns * m + si + 1 + ns * md)
            nc.vector.tensor_tensor(f["hid"][:, m % 2, off:off + n], f["silu"][:, m % 2, off:off + n],
                                    up_bank(m % 2, si), ALU.mult).then_inc(sem(f["name"] + "_hid"), 1)

    def ffn_hidden_lo(dve, f, m, md):
        ns = len(f["segs"])
        for si, (off, n) in enumerate(f["segs"]):
            dve.wait_ge(sem(f["name"] + "_hid_hi"), ns * m + si + 1 + ns * md)
            ins = nc.vector.tensor_tensor(f["lo"][:, m % 2, off:off + n], f["hid"][:, m % 2, off:off + n],
                                          f["hi"][:, m % 2, off:off + n].bitcast(F32), ALU.subtract)
        ins.then_inc(sem(f["name"] + "_hid_ready"), 1)

    def ffn_dve(dve, f):
        out_ready, out_free = sem(f["name"] + "_out_ready"), sem(f["name"] + "_out_free")
        dve.sem_inc(sem(f["name"] + "_hid_ready"), CREDIT)
        dve.sem_inc(out_free, CREDIT)
        ffn_mult(dve, f, 0, 0, f["c0"], 0)
        ffn_hidden_lo(dve, f, 0, 0)
        dve.wait_ge(y_zero, f["index"] + 1)
        if f["mods"]:
            start, start_dst, m0, each, dst = f["mods"]
            for c in start:
                mod_block(dve, c, [start_dst[m][:, c:c + 1] for m in range(2)], dump[:])
            done = 2 * (NG - 1) * f["index"]

        def mods(g, part, group):
            if f["mods"]:
                i = group[2]
                mod_group(dve, m0 + sum(each) * g + part * each[0], each[part], dst, dump[:], i, 2 * sum(each),
                          done + 2 * g + part + i * 4)

        def step(c, d, group, last):
            g, gd = group[:2]
            ffn_mult(dve, f, 2 * g + 1, 2 * gd, c, d)
            ffn_hidden_lo(dve, f, 2 * g + 1, 2 * gd)
            if not last:
                mods(g, 0, group)
                ffn_mult(dve, f, 2 * g + 2, 2 * gd, c + 2, d)
            dve.wait_ge(out_free, CREDIT + 8 * g + 8 * gd)
            for n in range(KC):
                if n < KC - 1:
                    dve.wait_ge(out_ready, (KC - 1) * g + n + 1 + (KC - 1) * gd)
                else:
                    dve.wait_ge(w_used, (c + 4 if last else c + 6) + d)
                for si, (off, w) in enumerate(f["segs"]):
                    acc = f["y"][:, n, off:off + w]
                    ins = nc.vector.tensor_tensor(acc, acc, out_bank(f, n, si, last), ALU.add)
                ins.then_inc(out_free, 1)
            if not last:
                ffn_hidden_lo(dve, f, 2 * g + 2, 2 * gd)
                mods(g, 1, group)

        ffn_groups(dve, f, step)

    def ffn_y_ready(f):
        def ready(eng, k):
            eng.wait_ge(sem(f["name"] + "_out_free"), CREDIT + KC * (NG - 1) + k + 1)
        return ready

    def out_bank_of(n, si, nseg):
        return ps[:, n, :] if nseg == 1 else ps[:, 2 * (n % 3) + si, 0:segs(2)[si][1]]

    def out_pe(pe, name, x, post):
        nseg = PASS_SEGS[post]
        for n in range(KC):
            pe.wait_ge(lo_ready, FIRST[name] + n + 1)
            if nseg == 2 and n >= 3:
                pe.wait_ge(sem(name + "_y"), n - 2)
            project(x[0], x[1], FIRST[name] + n, [(out_bank_of(n, si, nseg), off, w) for si, (off, w) in enumerate(segs(nseg))]
                    ).then_inc(w_used, 1)
            sums_behind(pe, post, n)
        norm_pe(pe, post, range(KC - SUMS_BEHIND, KC))

    def out_act(act, name, post, src):
        for n in range(KC):
            split_hi(act, FIRST[name] + n + RING)
            if n >= 1:
                norm_square(act, post, src, out_y_ready(name), n - 1)
        norm_square(act, post, src, out_y_ready(name), KC - 1)
        norm_root(act, post)

    def out_dve(dve, name, acc, nseg, before_chunk=None):
        for n in range(KC):
            if before_chunk:
                before_chunk(n)
            dve.wait_ge(w_used, FIRST[name] + n + 1)
            for si, (off, w) in enumerate(segs(nseg)):
                ins = nc.vector.tensor_copy(acc[:, n, off:off + w], out_bank_of(n, si, nseg))
            ins.then_inc(sem(name + "_y"), 1)

    def out_y_ready(name):
        def ready(eng, k):
            eng.wait_ge(sem(name + "_y"), k + 1)
        return ready

    def pair(i, si, n):
        return ps[:, 2 * (i % 2) + si, 0:n]

    def in_plan(layer):
        q, k, v = ((l0_qkv, l1_qkv)[layer][j:j + 2] for j in (0, 2, 4))
        if layer == 0:
            return ([("qk", k, 0, 1, 2), ("qk", q, 0, 0, 2), ("v", v, 0, None, 2)]
                    + [("qk", q, n, 0, 2) for n in range(1, 4)] + [("u", None, n, None, 2) for n in range(4)])
        return ([("qk", k, n, None, 2) for n in range(2)] + [("wide", v, n, None, 2) for n in range(2)]
                + [("qk", q, n, None, 1) for n in range(8)])

    def in_stage(layer):
        name = f"l{layer}_in"
        return dict(name=name, plan=in_plan(layer), c0=FIRST[name], norm=layer == 0, beside=None,
                    **{s: sem(f"{name}_{s}") for s in ["out", "v_hi", "v_lo", "sh", "sin", "q", "hi", "lo"] + (
                        ["sq", "ss", "turn", "rms", "qn", "pads", "pool", "d_hi", "d_lo", "mix", "mix_hi", "mix_lo"]
                        if layer == 0 else [])})

    def qk_buf(st, j):
        if st["norm"]:
            return qn, tsh
        return (qraw, tsh) if j % 2 else (qn, sq[:, 0, :])

    def outs_before(plan, i):
        return sum(p[0] != "wide" for p in plan[:i])

    def wide_bank(t):
        return ps[:, 4 + t // 2, (t % 2) * 256:(t % 2 + 1) * 256]

    SS_IN = (4, 5)

    def pool_group(n):
        return 3 - n

    def in_pe(pe, st):
        plan, c0 = st["plan"], st["c0"]
        qk_seen = 0
        pending = None

        def head_sums(j):
            for si, (off, n) in enumerate(segs(2)):
                pe.wait_ge(st["sq"], 2 * j + si + 1)
                nc.tensor.matmul(ps[:, SS_IN[si], 0:n], blkones[:, :], sq[:, si, 0:n], start=True, stop=True
                                 ).then_inc(st["ss"], 1)

        project_first(pe, h_hi, h_lo, c0, [[(pair(i, si, w), off, w) for si, (off, w) in enumerate(segs(2))]
                                           for i in range(2)], st["h_base"], beside=st["beside"])
        for i, (kind, buf, n, gain, ns) in enumerate(plan):
            c = c0 + i
            pe.wait_ge(lo_ready, c + 1)
            if i >= 2 and kind != "wide":
                prev = [p for p in range(i) if plan[p][0] != "wide" and p % 2 == i % 2][-1]
                pe.wait_ge(st["out"], outs_before(plan, prev) + 1)
                if plan[prev][0] == "v":
                    pe.wait_ge(st["v_lo"], 1)
            if kind == "v":
                for t in range(T // P):
                    out = pair(i, t // 4, 512)[:, (t % 4) * P:(t % 4 + 1) * P]
                    for k, w in enumerate(tiles(c)):
                        for m, (a, b) in enumerate(((0, 0), (0, 1), (1, 0))):
                            mm = nc.tensor.matmul(out, (h_hi, h_lo)[a][:, k, t * P:(t + 1) * P], w[b],
                                                  start=k == 0 and m == 0, stop=k == 7 and m == 2)
                mm.then_inc(w_used, 1)
            elif kind == "wide" and n == 1:
                for t in range(T // P):
                    for k in range(KC):
                        cols = slice(k % 4 * 256, (k % 4 + 1) * 256)
                        for m, (a, b) in enumerate(((0, 0), (0, 1), (1, 0))):
                            mm = nc.tensor.matmul(wide_bank(t), (h_hi, h_lo)[a][:, k, t * P:(t + 1) * P],
                                                  (w_hi, w_lo)[b][:, (c - 1 + k // 4) % RING, cols],
                                                  start=k == 0 and m == 0, stop=k == KC - 1 and m == 2)
                mm.then_inc(w_used, 2)
            elif kind != "wide" and i >= 2:
                project(h_hi, h_lo, c, [(pair(i, si, w), off, w) for si, (off, w) in enumerate(segs(ns))]
                        ).then_inc(w_used, 1)
            if pending is not None:
                head_sums(pending)
                pending = None
            if kind == "qk":
                if st["norm"]:
                    pending = qk_seen
                qk_seen += 1

    def in_act(act, st):
        plan, c0 = st["plan"], st["c0"]
        j = 0
        pending = None

        def head_rms(j):
            act.wait_ge(st["turn"], j + 1)
            nc.scalar.activation(rms_t[:], squares(rstd, T)[:, :, 0], ACT.Sqrt, scale=1.0 / HD, bias=eps_col[:, 0:1]
                                 ).then_inc(st["rms"], 1)

        def qk_hi(j, buf, n, ns):
            act.wait_ge(st["q"], j + 1)
            w = segs(ns)[-1][0] + segs(ns)[-1][1]
            nc.scalar.activation(buf[0][:, n, 0:w], qk_buf(st, j)[0][:, 0:w], ACT.Copy).then_inc(st["hi"], 1)

        def pool_hi(n):
            act.wait_ge(st["pool"], n + 1)
            if n >= 2:
                act.wait_ge(st["mix"], n - 1)
            s = (sA, sB)[pool_group(n) % 2]
            nc.scalar.activation(d_hi[:, n % 2, 0:S], s[:, PAD:PAD + S], ACT.Copy)
            nc.scalar.activation(d_hi[:, n % 2, S:T], s[:, S + 3 * PAD:S + 3 * PAD + C], ACT.Copy
                                 ).then_inc(st["d_hi"], 1)

        for i, (kind, buf, n, gain, ns) in enumerate(plan):
            split_hi(act, c0 + i + RING)
            act.wait_ge(w_used, c0 + i + 1)
            if pending is not None and st["norm"]:
                head_rms(pending[0])
            if kind == "qk":
                if st["norm"]:
                    for si, (off, w) in enumerate(segs(2)):
                        if j >= 1:
                            act.wait_ge(st["ss"], 2 * j - 1 + si)
                        nc.scalar.activation(sq[:, si, 0:w], pair(i, si, w), ACT.Square).then_inc(st["sq"], 1)
                dst = qraw if st["norm"] else qk_buf(st, j)[0]
                if st["norm"] and j >= 1:
                    act.wait_ge(st["qn"], j)
                if not st["norm"] and j >= 2:
                    act.wait_ge(st["lo"], j - 1)
                for si, (off, w) in enumerate(segs(ns)):
                    ins = nc.scalar.activation(dst[:, off:off + w], pair(i, si, w), ACT.Copy)
                ins.then_inc(st["out"], 1)
            elif kind == "v":
                for t0, t1, si in ((0, 4, 0), (4, 6, 1)):
                    ins = nc.scalar.activation(buf[0][:, t0:t1, n * P:(n + 1) * P],
                                               pair(i, si, (t1 - t0) * P).rearrange("p (t c) -> p t c", c=P), ACT.Copy)
                ins.then_inc(st["out"], 1)
            elif kind == "wide" and n == 1:
                for t in range(0, T // P, 2):
                    nc.scalar.activation(buf[0][:, t:t + 2, :], ps[:, 4 + t // 2, :].rearrange("p (t c) -> p t c", t=2),
                                         ACT.Copy).then_inc(st["v_hi"], 1)
            if pending is not None:
                qk_hi(*pending)
                pending = None
            if kind == "u":
                if n >= 1:
                    pool_hi(n - 1)
                else:
                    act.wait_ge(st["lo"], j)
                act.wait_ge(st["pads"], 1)
                nc.scalar.activation(upad[:, PAD:PAD + S], pair(i, 0, S), ACT.Copy)
                nc.scalar.activation(upad[:, S + 3 * PAD:S + 3 * PAD + C], pair(i, 1, C), ACT.Copy
                                     ).then_inc(st["out"], 1)
            if kind == "qk":
                pending = (j, buf, n, ns)
                j += 1
        if pending is not None:
            qk_hi(*pending)
        if st["norm"]:
            pool_hi(3)

    def in_dve(dve, st):
        plan = st["plan"]
        j = 0
        for i, (kind, buf, n, gain, ns) in enumerate(plan):
            if kind == "wide" and n == 1:
                for t in range(0, T // P, 2):
                    dve.wait_ge(st["v_hi"], t // 2 + 1)
                    nc.vector.tensor_tensor(buf[1][:, t:t + 2, :], ps[:, 4 + t // 2, :].rearrange("p (t c) -> p t c", t=2),
                                            buf[0][:, t:t + 2, :].bitcast(F32), ALU.subtract).then_inc(st["v_lo"], 1)
            if kind == "v":
                dve.wait_ge(st["out"], outs_before(plan, i) + 1)
                for t0, t1, si in ((0, 4, 0), (4, 6, 1)):
                    cols = slice(n * P, (n + 1) * P)
                    ins = nc.vector.tensor_tensor(buf[1][:, t0:t1, cols],
                                                  pair(i, si, (t1 - t0) * P).rearrange("p (t c) -> p t c", c=P),
                                                  buf[0][:, t0:t1, cols].bitcast(F32), ALU.subtract)
                ins.then_inc(st["v_lo"], 1)
            if kind == "qk":
                w = segs(ns)[-1][0] + segs(ns)[-1][1]
                q, sh = qk_buf(st, j)
                if st["norm"]:
                    dve.wait_ge(st["ss"], 2 * j + 2)
                    turn_sums([ps[:, b, :] for b in SS_IN], rstd).then_inc(st["turn"], 1)
                    dve.wait_ge(st["rms"], j + 1)
                    turn_inverse(dve, rstd, T)
                    dve.wait_ge(st["out"], outs_before(plan, i) + 1)
                    nc.vector.scalar_tensor_tensor(out=q[:, 0:w], in0=qraw[:, 0:w], scalar=qk_gain[:, gain:gain + 1],
                                                   in1=rstd[:, 0:w], op0=ALU.mult, op1=ALU.mult).then_inc(st["qn"], 1)
                    dve.wait_ge(st["qn"], j + 1)
                else:
                    dve.wait_ge(st["out"], outs_before(plan, i) + 1)
                nc.vector.stream_shuffle(sh[:, 0:S], q[:, 0:S], ROT).then_inc(st["sh"], 1)
                dve.wait_ge(st["sh"], j + 1)
                link(dve, nc.vector.tensor_tensor(q[:, 0:S], q[:, 0:S], cos[:, :], ALU.mult))
                dve.wait_ge(st["sin"], j + 1)
                nc.vector.tensor_tensor(q[:, 0:S], q[:, 0:S], sh[:, 0:S], ALU.add).then_inc(st["q"], 1)
                dve.wait_ge(st["hi"], j + 1)
                nc.vector.tensor_tensor(buf[1][:, n, 0:w], q[:, 0:w], buf[0][:, n, 0:w].bitcast(F32), ALU.subtract
                                        ).then_inc(st["lo"], 1)
                dve.wait_ge(st["lo"], j + 1)
                j += 1
            if kind == "u":
                pool_mean(dve, st, n, i)

    def pool_mean(dve, st, j, i):
        g = pool_group(j)
        dve.wait_ge(st["out"], i + 1)
        src, lo, hi = upad, 0, UCOLS
        for level in range(g + 1):
            dst = (sA, sB)[level % 2]
            back, ahead = (1, 0) if level == 0 else (2 ** (level - 1), 2 ** (level - 1))
            lo, hi = lo + back, hi - ahead
            link(dve, nc.vector.tensor_tensor(dst[:, lo:hi], src[:, lo - back:hi - back], src[:, lo + ahead:hi + ahead],
                                              ALU.add))
            src = dst
        for first, n in ((PAD, S), (S + 3 * PAD, C)):
            for e, at_ in ((0, first), (1, first + n - 8)):
                ins = nc.vector.tensor_tensor(src[:, at_:at_ + 8], src[:, at_:at_ + 8], edges[:, g, e, :], ALU.mult)
        link(dve, ins)
        nc.vector.scalar_tensor_tensor(out=src[:, PAD:UCOLS - PAD], in0=src[:, PAD:UCOLS - PAD],
                                       scalar=1.0 / POOL_W[g], in1=upad[:, PAD:UCOLS - PAD], op0=ALU.mult,
                                       op1=ALU.subtract).then_inc(st["pool"], 1)
        dve.wait_ge(st["d_hi"], j + 1)
        nc.vector.tensor_tensor(d_lo[:, j % 2, 0:S], src[:, PAD:PAD + S], d_hi[:, j % 2, 0:S].bitcast(F32), ALU.subtract)
        nc.vector.tensor_tensor(d_lo[:, j % 2, S:T], src[:, S + 3 * PAD:S + 3 * PAD + C],
                                d_hi[:, j % 2, S:T].bitcast(F32), ALU.subtract).then_inc(st["d_lo"], 1)
        dve.wait_ge(st["d_lo"], j + 1)

    def in_pool(pool, st):
        j = 0
        for i, (kind, buf, n, gain, ns) in enumerate(st["plan"]):
            split_lo(pool, st["c0"] + i + RING)
            if kind == "qk":
                q, sh = qk_buf(st, j)
                pool.wait_ge(st["sh"], j + 1)
                nc.gpsimd.tensor_tensor(sh[:, 0:S], sh[:, 0:S], sin[:, :], ALU.mult).then_inc(st["sin"], 1)
                j += 1
            if kind == "u" and n == 0:
                pool.wait_ge(st["lo"], j)
                for k, (a, b) in enumerate(((0, PAD), (PAD + S, S + 3 * PAD), (UCOLS - PAD, UCOLS))):
                    ins = nc.gpsimd.memset(upad[:, a:b], 0.0)
                ins.then_inc(st["pads"], 1)

    def pool_pe(pe, st):
        c = FIRST["l0_pool"]
        pe.wait_ge(lo_ready, c + 1)
        for n in range(4):
            i = len(st["plan"]) + n
            pe.wait_ge(st["d_lo"], n + 1)
            pe.wait_ge(st["out"], i - 1) if n < 2 else pe.wait_ge(st["mix_lo"], n - 1)
            mm = product(tiles(c)[pool_group(n)], (d_hi[:, n % 2, :], d_lo[:, n % 2, :]),
                         [(pair(i, si, w), off, w) for si, (off, w) in enumerate(segs(2))], True, True)
            mm.then_inc(st["mix"] if n < 3 else w_used, 1)

    def pool_out_ready(eng, st, n):
        if n < 3:
            eng.wait_ge(st["mix"], n + 1)
        else:
            eng.wait_ge(w_used, FIRST["l0_pool"] + 1)

    def pool_act(act, st):
        for n in range(4):
            g = pool_group(n)
            pool_out_ready(act, st, n)
            for si, (off, w) in enumerate(segs(2)):
                ins = nc.scalar.activation(h_hi[:, 4 + g, off:off + w], pair(len(st["plan"]) + n, si, w), ACT.Copy,
                                           scale=pool_scale[:, g:g + 1])
            ins.then_inc(st["mix_hi"], 1)
        split_hi(act, FIRST["l0_pool"] + RING)

    def pool_dve(dve, st):
        for n in range(4):
            g = pool_group(n)
            dve.wait_ge(st["mix_hi"], n + 1)
            for si, (off, w) in enumerate(segs(2)):
                ins = nc.vector.scalar_tensor_tensor(out=h_lo[:, 4 + g, off:off + w],
                                                     in0=pair(len(st["plan"]) + n, si, w),
                                                     scalar=pool_scale[:, g:g + 1],
                                                     in1=h_hi[:, 4 + g, off:off + w].bitcast(F32),
                                                     op0=ALU.mult, op1=ALU.subtract)
            ins.then_inc(st["mix_lo"], 1)

    def attention(name, units, q, k, v, out, scale, qchunk, kchunk, vcol, outchunk, next_block, extra=None, sink=None,
                  unroll=False):
        groups = []
        for x in units:
            nb = len(x[4])
            groups.append([(0, (nb + 1) // 2), ((nb + 1) // 2, nb)] if nb > 1 else [(0, 1)])
        cum = [0]
        for g in groups:
            cum.append(cum[-1] + len(g))
        return dict(name=name, units=units, q=q, k=k, v=v, out=out, scale=scale, qchunk=qchunk, kchunk=kchunk,
                    vcol=vcol, outchunk=outchunk, extra=extra, sink=sink, groups=groups, cum=cum, nu=len(units), next=next_block, unroll=unroll, d_steps=3 if sink else 2,
                    **{"s_" + s: sem(f"{name}_{s}") for s in (
                        "staged", "qk", "negm", "p", "diag", "t", "hi", "lo", "pv", "o", "m_hi", "m_lo")})

    ATT_ITERS = 4

    def att_loop(eng, a, body):
        body(0, True, False)
        if a["unroll"]:
            for c in range(1, ATT_ITERS - 1):
                body(c, False, False)
        else:
            with eng.Fori(0, ATT_ITERS - 2) as i:
                body(i + 1, False, False)
        body(ATT_ITERS - 1, False, True)

    def ahead(a, c, u, last):
        if u + 2 < a["nu"]:
            return c, u + 2
        return None if last else (c + 1, u + 2 - a["nu"])

    def behind(a, c, u, first, n, size):
        if u >= n:
            return c, u - n
        return None if first else (c - 1, size + u - n)

    def score(u, col, n):
        return flat[:, (u % 2) * 1024 + col:(u % 2) * 1024 + col + n]

    def att_pe(pe, a, free):
        nu, cum = a["nu"], a["cum"]

        def qk(c, u):
            qt, half, _, keys, _, tag = a["units"][u]
            if half == 0:
                pe.wait_ge(a["s_staged"], c * (nu // 2) + qt + 1)
            more = a["extra"](c, a["units"][u]) if a["extra"] else []
            kc = a["kchunk"](c, a["units"][u])
            for col, kcol, w in keys:
                added = [m for m in more if col <= m[0] < col + w]
                for i, (x, z) in enumerate(((0, 0), (0, 1), (1, 0))):
                    mm = nc.tensor.matmul(score(u, col, w), (qs_hi, qs_lo)[x][:, qt % 2, half, :],
                                          a["k"][z][:, kc, kcol:kcol + w], start=i == 0, stop=i == 2 and not added)
                for j, (mcol, mw, lhs, rhs) in enumerate(added):
                    mm = nc.tensor.matmul(score(u, mcol, mw), lhs, rhs, start=False, stop=j == len(added) - 1)
            mm.then_inc(a["s_qk"], 1)

        def qk_next(c, u, n):
            pe.wait_ge(a["s_p"], c * nu + u + 1)
            qk(*n)

        def turn(c, u, first):
            pe.wait_ge(a["s_diag"], a["d_steps"] * (c * nu + u + 1))
            for g, (b0, b1) in enumerate(a["groups"][u]):
                if not (first and u == 0):
                    pe.wait_ge(a["s_lo"], c * cum[-1] + cum[u] - len(a["groups"][u - 1]) + min(g + 1, len(a["groups"][u - 1])))
                for b in range(b0, b1):
                    mm = nc.tensor.matmul(ps[:, 4 + g, (b - b0) * P:(b - b0 + 1) * P], prob[:, u % 2, b * P:(b + 1) * P],
                                          dg[:, u % 2, :], start=True, stop=True)
                mm.then_inc(a["s_t"], 1)

        def values(c, u, first):
            x = a["units"][u]
            if not (first and u < 2):
                pe.wait_ge(a["s_o"], c * nu + u - 1)
            nb = len(x[4])
            for g, (b0, b1) in enumerate(a["groups"][u]):
                pe.wait_ge(a["s_lo"], c * cum[-1] + cum[u] + g + 1)
                for b in range(b0, b1):
                    for i, (z, p) in enumerate(((0, 0), (0, 1), (1, 0))):
                        mm = nc.tensor.matmul(ps[0:HD, 6 + u % 2, 0:P], a["v"][z][:, x[4][b], a["vcol"](c, x)],
                                              (pt_hi, pt_lo)[p][:, u % 2, b * P:(b + 1) * P], start=b == 0 and i == 0,
                                              stop=b == nb - 1 and i == 2)
            mm.then_inc(a["s_pv"], 1)

        def body(c, first, last):
            for u in range(nu):
                n = ahead(a, c, u, last)
                if n:
                    qk_next(c, u, n)
                turn(c, u, first)
                n = behind(a, c, u, first, 1, nu)
                if n:
                    values(*n, first)
            if last:
                values(c, nu - 1, False)

        free(pe)
        qk(0, 0)
        qk(0, 1)
        att_loop(pe, a, body)

    def att_act(act, a):
        nu, cum = a["nu"], a["cum"]

        def exps(c, u):
            act.wait_ge(a["s_negm"], 2 * (c * nu + u + 1))
            x = a["units"][u]
            w = P * len(x[4])
            e = u % 4
            ins = nc.scalar.activation(prob[:, u % 2, 0:w], score(u, 0, w), ACT.Exp, scale=a["scale"],
                                       bias=negm[:, e:e + 1], accum_out=rsum[:, e:e + 1])
            if a["sink"]:
                ins = nc.scalar.activation(esink[:, e:e + 1], nsink[:, a["sink"](c, x)], ACT.Exp, scale=-1.0,
                                           bias=negm[:, e:e + 1])
            ins.then_inc(a["s_p"], 1)

        def out(c, u):
            p, half = u // 2, a["units"][u][1]
            act.wait_ge(a["s_pv"], c * nu + u + 1)
            if half == 0 and not (first_pair(c) and p < 2):
                act.wait_ge(a["s_m_lo"], c * (nu // 2) + p - 1)
            nc.scalar.activation(opair[half * HD:(half + 1) * HD, p % 2, :], ps[0:HD, 6 + u % 2, 0:P], ACT.Copy
                                 ).then_inc(a["s_o"], 1)
            if half == 1:
                act.wait_ge(a["s_o"], c * nu + u + 1)
                x = a["units"][u]
                nc.scalar.activation(a["out"][0][:, a["outchunk"](c, x), x[2]:x[2] + P], opair[:, p % 2, :], ACT.Copy
                                     ).then_inc(a["s_m_hi"], 1)

        def first_pair(c):
            return isinstance(c, int) and c == 0

        def body(c, first, last):
            for u in range(nu):
                if not (first and u < 2):
                    act.wait_ge(a["s_pv"], c * nu + u - 1)
                for g, (b0, b1) in enumerate(a["groups"][u]):
                    act.wait_ge(a["s_t"], c * cum[-1] + cum[u] + g + 1)
                    nc.scalar.activation(pt_hi[:, u % 2, b0 * P:b1 * P], ps[:, 4 + g, 0:(b1 - b0) * P], ACT.Copy
                                         ).then_inc(a["s_hi"], 1)
                n = ahead(a, c, u, last)
                if n:
                    exps(*n)
                n = behind(a, c, u, first, 1, nu)
                if n:
                    out(*n)
            if last:
                out(c, nu - 1)

        exps(0, 0)
        exps(0, 1)
        act.wait_ge(lo_ready, a["next"] + RING)
        att_loop(act, a, body)

    def att_dve(dve, a, beside=None):
        nu, cum = a["nu"], a["cum"]

        def row_max(c, u):
            dve.wait_ge(a["s_qk"], c * nu + u + 1)
            x = a["units"][u]
            e = u % 4
            nc.vector.reduce_max(smax[:, e:e + 1], score(u, 0, P * len(x[4])), AX.X).then_inc(a["s_negm"], 1)
            dve.wait_ge(a["s_negm"], 2 * (c * nu + u) + 1)
            if a["sink"]:
                ins = nc.vector.tensor_scalar(negm[:, e:e + 1], smax[:, e:e + 1], -a["scale"], nsink[:, a["sink"](c, x)],
                                              ALU.mult, ALU.min)
            else:
                ins = nc.vector.tensor_scalar(negm[:, e:e + 1], smax[:, e:e + 1], -a["scale"], None, ALU.mult)
            ins.then_inc(a["s_negm"], 1)

        def low(c, u, g):
            b0, b1 = a["groups"][u][g]
            dve.wait_ge(a["s_hi"], c * cum[-1] + cum[u] + g + 1)
            nc.vector.tensor_tensor(pt_lo[:, u % 2, b0 * P:b1 * P], ps[:, 4 + g, 0:(b1 - b0) * P],
                                    pt_hi[:, u % 2, b0 * P:b1 * P].bitcast(F32), ALU.subtract).then_inc(a["s_lo"], 1)

        def diagonal(c, u):
            e, done = u % 4, a["d_steps"] * (c * nu + u)
            dve.wait_ge(a["s_p"], c * nu + u + 1)
            if a["sink"]:
                nc.vector.tensor_tensor(rsum[:, e:e + 1], rsum[:, e:e + 1], esink[:, e:e + 1], ALU.add
                                        ).then_inc(a["s_diag"], 1)
                dve.wait_ge(a["s_diag"], done + 1)
            nc.vector.reciprocal(rinv[:, e:e + 1], rsum[:, e:e + 1]).then_inc(a["s_diag"], 1)
            dve.wait_ge(a["s_diag"], done + a["d_steps"] - 1)
            nc.vector.tensor_scalar(dg[:, u % 2, :], ident, rinv[:, e:e + 1], None, ALU.mult).then_inc(a["s_diag"], 1)

        def m_lo(c, p):
            dve.wait_ge(a["s_m_hi"], c * (nu // 2) + p + 1)
            x = a["units"][2 * p]
            n = a["outchunk"](c, x)
            nc.vector.tensor_tensor(a["out"][1][:, n, x[2]:x[2] + P], opair[:, p % 2, :],
                                    a["out"][0][:, n, x[2]:x[2] + P].bitcast(F32), ALU.subtract).then_inc(a["s_m_lo"], 1)

        def body(c, first, last):
            for u in range(nu):
                if u + 1 < nu:
                    diagonal(c, u + 1)
                elif not last:
                    diagonal(c + 1, 0)
                n = ahead(a, c, u, last)
                if n:
                    row_max(*n)
                for g in range(len(a["groups"][u])):
                    low(c, u, g)
                if beside and (first or last):
                    beside(c, u)
                n = behind(a, c, (u - 1) // 2, first, 1, nu // 2) if u % 2 else None
                if n:
                    m_lo(*n)
            if last:
                m_lo(c, nu // 2 - 1)

        row_max(0, 0)
        row_max(0, 1)
        diagonal(0, 0)
        att_loop(dve, a, body)

    def att_pool(pool, a, ready):
        nt = a["nu"] // 2
        halves = [blkones[:, h * HD:h * HD + 1].to_broadcast([P, P]) for h in range(2)]
        ready(pool)
        def body(c, first, last):
            for qt in range(nt):
                x = a["units"][2 * qt]
                if not (first and qt < 2):
                    pool.wait_ge(a["s_qk"], c * 2 * nt + 2 * qt - 2)
                n = a["qchunk"](c, x)
                for t, src in ((qs_hi, a["q"][0]), (qs_lo, a["q"][1])):
                    for half in range(2):
                        ins = nc.gpsimd.tensor_tensor(t[:, qt % 2, half, :], src[:, n, x[2]:x[2] + P].bitcast(F32),
                                                      halves[half], ALU.mult)
                ins.then_inc(a["s_staged"], 1)

        att_loop(pool, a, body)

    def m_done(eng, a):
        eng.wait_ge(a["s_m_lo"], ATT_ITERS * a["nu"] // 2)

    l0_att = attention(
        "l0_att",
        [(t, half, t * P, [(0, 0, S), (S, S, C)] if t < NQ else [(0, S, C)], list(range(6)) if t < NQ else [4, 5], None)
         for t in range(T // P) for half in range(2)],
        l0_qkv[0:2], l0_qkv[2:4], l0_qkv[4:6], (h_hi, h_lo), SCALE, lambda c, x: c, lambda c, x: 0,
        lambda c, x: slice(x[1] * HD, (x[1] + 1) * HD), lambda c, x: c, FIRST["l0_out"])

    def l1_units():
        units = []
        for kc in range(2):
            for t in range(NQ):
                b0, b1 = max(t - 1, 0), min(t + 2, NQ)
                w = (b1 - b0) * P
                keys = [(0, S, C), (C, b0 * P, min(w, C))] + ([(2 * C, b0 * P + C, w - C)] if w > C else [])
                for half in range(2):
                    units.append((kc * NQ + t, half, t * P, keys, [4, 5] + list(range(b0, b1)), (kc, t, b0, b1)))
        return units

    def l1_extra(c, x):
        kc, t, b0, b1 = x[5]
        return [(C + (b - b0) * P, P, ident_r[:, :], mask[:, 0 if b < t else 1, :]) for b in range(b0, b1) if b != t]

    l1_att = attention(
        "l1_att", l1_units(), l1_qkv[0:2], l1_qkv[2:4], l1_qkv[4:6], (n_hi, n_lo), SCALE,
        lambda c, x: c * 2 + x[5][0], lambda c, x: x[5][0],
        lambda c, x: slice((2 * x[5][0] + x[1]) * HD, (2 * x[5][0] + x[1] + 1) * HD), lambda c, x: c * 2 + x[5][0],
        FIRST["l1_out"], extra=l1_extra, sink=lambda c, x: bass.ds(c * 4 + 2 * x[5][0] + x[1], 1))

    def s_extra(c, x):
        t = x[0]
        head = c * 2 + x[1]
        if t == 0:
            return [(0, P, ident[:, :], rel[:, head, P:2 * P])]
        return [((t - 1) * P, 2 * P, ident[:, :], rel[:, head, :])]

    s_att = attention(
        "s_att", [(t, half, t * P, [(0, 0, (t + 1) * P)], list(range(t + 1)), None) for t in range(NQ) for half in range(2)],
        s_qkv[0:2], s_qkv[2:4], s_qkv[4:6], (o_hi, o_lo), 1.0, lambda c, x: c, lambda c, x: c,
        lambda c, x: slice(c * P + x[1] * HD, c * P + (x[1] + 1) * HD), lambda c, x: c, FIRST["s_atto"],
        extra=s_extra, unroll=True)

    s_hi, s_lo = sem("s_in_hi"), sem("s_in_lo")
    att_done, gated, rec_lo = sem("s_att_done"), sem("s_gated"), sem("s_rec_lo")
    s_sig, s_grs, merged, merged_hi, merged_lo = (sem(n) for n in (
        "s_sig", "s_grs", "s_merged", "s_merged_hi", "s_merged_lo"))

    def bank_of(j, i):
        return flat[:, bass.ds(512 * j + i * (512 * RING), 512)]

    def s_in_pe(pe):
        c0 = FIRST["s_in"]
        project_first(pe, n_hi, n_lo, c0, [[(ps[:, i, :], 0, S)] for i in range(2)], 8 * before("s1_pre", "_pre"))
        for i in range(2, 8):
            pe.wait_ge(lo_ready, c0 + i + 1)
            if i >= 4:
                pe.wait_ge(s_lo, i - 3)
            project(n_hi, n_lo, c0 + i, [(ps[:, i % 4, :], 0, S)]).then_inc(w_used, 1)
        for i in range(4):
            c = c0 + 8 + i
            pe.wait_ge(lo_ready, c + 1)
            for t in range(NQ):
                for k in range(2):
                    for m, (a, b) in enumerate(((0, 0), (0, 1), (1, 0))):
                        mm = nc.tensor.matmul(ps[:, 4 + t, :], (n_hi, n_lo)[a][:, 2 * i + k, t * P:(t + 1) * P],
                                              (w_hi, w_lo)[b][:, c % RING, k * S:(k + 1) * S],
                                              start=i == 0 and k == 0 and m == 0, stop=i == 3 and k == 1 and m == 2)
            mm.then_inc(w_used, 1)

    def s_in_out(i, part):
        if i < 8:
            return s_qkv[2 * (i // 4) + part][:, i % 4, :], ps[:, i % 4, :]
        return s_qkv[4 + part][:, i - 8, :], ps[:, i - 4, :]

    def s_in_act(act):
        c0 = FIRST["s_in"]
        for i in range(12):
            split_hi(act, c0 + i + RING)
            if i < 8:
                act.wait_ge(w_used, c0 + i + 1)
                dst, bank = s_in_out(i, 0)
                nc.scalar.activation(dst, bank, ACT.Copy, scale=SCALE if i < 4 else 1.0).then_inc(s_hi, 1)
        act.wait_ge(w_used, c0 + 12)
        for i in range(8, 12):
            dst, bank = s_in_out(i, 0)
            nc.scalar.activation(dst, bank, ACT.Copy).then_inc(s_hi, 1)

    def s_in_dve(dve):
        for i in range(12):
            dve.wait_ge(s_hi, i + 1)
            hi, bank = s_in_out(i, 0)
            lo, _ = s_in_out(i, 1)
            nc.vector.scalar_tensor_tensor(out=lo, in0=bank, scalar=SCALE if i < 4 else 1.0, in1=hi.bitcast(F32),
                                           op0=ALU.mult, op1=ALU.subtract).then_inc(s_lo, 1)

    def bias_dve(dve):
        dve.wait_ge(late_landed, 16 * (LATE.index("rel_in") + 1))
        for h in range(8):
            ins = nc.vector.tensor_scalar(rel[:, h, :], rel[:, h, :], relc[:, h:h + 1], None, ALU.subtract)
        link(dve, ins)
        nc.vector.memset(rel[0:HD, :, P + HD:2 * P], -1e30).then_inc(sem("rel_ready"), 1)

    LRU = MODRAW
    lru_wa, lru_wx = at("lru_wa_sb", [KC, P], LRU), at("lru_wx_sb", [KC, P], LRU + KC * P * 4)
    _lru = LRU + 2 * KC * P * 4
    xpad = at("xpad", [S + 8], _lru)
    xconv, gy, rec = (at(n, [2, S], _lru + 4 * (S + 8) + 8 * S * i) for i, n in enumerate(("xconv", "gy", "rec")))
    r_g, i_g, a_g, tau = (at(n, [S], _lru + 4 * (S + 8) + 24 * S + 4 * S * i) for i, n in enumerate(("r_g", "i_g", "a_g", "tau")))
    assert _lru + 4 * (S + 8) + 40 * S <= SCR + 15360
    att = at("att", [KC, S], MIX)
    rec_hi, rec_l = at("rec_hi", [KC, S], MIX + 4 * KC * S, F32R), at("rec_lo", [KC, S], MIX + 8 * KC * S, F32R)
    grs = at("grs", [KC, S], HSPARE)
    sg = at("sg", [2, S], SCR + 8192)
    xp, cv, ga, sig, ex, th, qq, sqr, uu, rc, rhi, gl = (sem("lru_" + n) for n in (
        "xpad", "conv", "gates", "sigmoid", "a", "tanh", "ratio", "sqrt", "u", "rec", "hi", "gelu"))

    def s_atto_pe(pe):
        c0 = FIRST["s_atto"]
        m_done(pe, s_att)
        for b in range(4):
            pe.wait_ge(lo_ready, c0 + b + 1)
            for j in range(2):
                for k in range(4):
                    mm = product(tiles(c0 + b)[4 * j + k], (o_hi[:, k, :], o_lo[:, k, :]), [(ps[:, 2 * b + j, :], 0, S)],
                                 k == 0, k == 3)
            mm.then_inc(w_used, 1)

    def s_atto_dve(dve):
        for b in range(4):
            dve.wait_ge(w_used, FIRST["s_atto"] + b + 1)
            nc.vector.tensor_copy(att[:, 2 * b:2 * b + 2, :], ps[:, 2 * b:2 * b + 2, :]).then_inc(att_done, 1)

    def eight_pe(pe, name, x, free):
        c = FIRST[name]
        with pe.Fori(0, KC // RING) as i:
            for j in range(RING):
                pe.wait_ge(lo_ready, c + j + 1 + i * RING)
                free(i, j)
                project(x[0], x[1], c + j, [(bank_of(j, i), 0, S)]).then_inc(w_used, 1)

    def s_gatt_act(act):
        for n in range(KC):
            split_hi(act, FIRST["s_gatt"] + n + RING)
            act.wait_ge(w_used, FIRST["s_gatt"] + n + 1)
            if n >= 2:
                act.wait_ge(gated, n - 1)
            nc.scalar.activation(sg[:, n % 2, :], ps[:, n, :], ACT.Sigmoid).then_inc(s_sig, 1)

    def s_gatt_dve(dve):
        dve.wait_ge(att_done, 4)
        for n in range(KC):
            dve.wait_ge(s_sig, n + 1)
            nc.vector.tensor_tensor(att[:, n, :], att[:, n, :], sg[:, n % 2, :], ALU.mult).then_inc(gated, 1)

    def s_rec_pe(pe):
        c0 = FIRST["s_rec"]
        pe.wait_ge(late_landed, 16 * (LATE.index("lru_wx_in") + 1))

        def block(c, bank, waits):
            pe.wait_ge(lo_ready, c + 1)
            pe.wait_ge(*waits)
            project(n_hi, n_lo, c, [(ps[:, bank, :], 0, S)]).then_inc(w_used, 1)

        def gates(n):
            pe.wait_ge(cv, n + 1)
            if n >= 2:
                pe.wait_ge(sig, n - 1)
            nc.tensor.matmul(ps[:, 4 + n % 2, :], lru_wa[:, n, :], xconv[:, n % 2, :], start=True, stop=True)
            nc.tensor.matmul(ps[:, 6 + n % 2, :], lru_wx[:, n, :], xconv[:, n % 2, :], start=True, stop=True
                             ).then_inc(ga, 1)

        for n in range(KC):
            block(c0 + 2 * n, n % 2, (xp, n - 1) if n >= 2 else (s_sig, n + 1))
            if n >= 1:
                if n == 1:
                    pe.wait_ge(s_sig, KC)
                gates(n - 1)
            block(c0 + 2 * n + 1, 2 + n % 2, (gl, n - 1) if n >= 2 else (s_sig, 3 + n))
        gates(KC - 1)

    def s_rec_act(act):
        c0 = FIRST["s_rec"]

        def high(n):
            act.wait_ge(rc, n + 1)
            nc.scalar.activation(rec_hi[:, n, :], rec[:, n % 2, :], ACT.Copy).then_inc(rhi, 1)

        for n in range(KC + 1):
            m = n - 1
            if n < KC:
                split_hi(act, c0 + 2 * n + RING)
                act.wait_ge(w_used, c0 + 2 * n + 1)
                if n >= 1:
                    act.wait_ge(cv, n)
                nc.scalar.activation(xpad[:, CONV - 1:CONV - 1 + S], ps[:, n % 2, :], ACT.Copy).then_inc(xp, 1)
            if m >= 0:
                act.wait_ge(ga, m + 1)
                if m >= 1:
                    act.wait_ge(rc, m)
                nc.scalar.activation(r_g[:], ps[:, 4 + m % 2, :], ACT.Sigmoid, bias=lru_ba[:, m:m + 1])
                nc.scalar.activation(i_g[:], ps[:, 6 + m % 2, :], ACT.Sigmoid, bias=lru_bx[:, m:m + 1]
                                     ).then_inc(sig, 1)
                act.wait_ge(sig, m + 1)
                nc.scalar.activation(a_g[:], r_g[:], ACT.Exp, scale=lru_s8[:, m:m + 1]).then_inc(ex, 1)
                nc.scalar.activation(tau[:], r_g[:], ACT.Tanh, scale=lru_n8[:, m:m + 1]).then_inc(th, 1)
            if n < KC:
                split_hi(act, c0 + 2 * n + 1 + RING)
                act.wait_ge(w_used, c0 + 2 * n + 2)
                if n >= 2:
                    act.wait_ge(rc, n - 1)
                nc.scalar.activation(gy[:, n % 2, :], ps[:, 2 + n % 2, :], ACT.Gelu_apprx_tanh).then_inc(gl, 1)
            if m >= 1:
                high(m - 1)
            if m >= 0:
                act.wait_ge(qq, m + 1)
                nc.scalar.activation(tau[:], tau[:], ACT.Sqrt, scale=2.0).then_inc(sqr, 1)
        high(KC - 1)

    def s_rec_dve(dve):
        link(dve, nc.vector.memset(xpad[:, 0:CONV - 1], 0.0))

        def low(n):
            dve.wait_ge(rhi, n + 1)
            nc.vector.tensor_tensor(rec_l[:, n, :], rec[:, n % 2, :], rec_hi[:, n, :].bitcast(F32), ALU.subtract
                                    ).then_inc(rec_lo, 1)
            dve.wait_ge(rec_lo, n + 1)

        for n in range(KC + 1):
            m = n - 1
            if n < KC:
                dve.wait_ge(xp, n + 1)
                if n >= 2:
                    dve.wait_ge(ga, n - 1)
                x = xconv[:, n % 2, :]
                link(dve, nc.vector.tensor_scalar(x, xpad[:, 0:S], conv_w[:, n, 0:1], conv_b[:, n:n + 1], ALU.mult, ALU.add))
                for j in range(1, CONV):
                    ins = nc.vector.scalar_tensor_tensor(out=x, in0=xpad[:, j:j + S], scalar=conv_w[:, n, j:j + 1], in1=x,
                                                         op0=ALU.mult, op1=ALU.add)
                    if j < CONV - 1:
                        link(dve, ins)
                ins.then_inc(cv, 1)
            if m >= 0:
                dve.wait_ge(th, m + 1)
                link(dve, nc.vector.tensor_scalar(r_g[:], tau[:], 1.0, None, ALU.add))
                link(dve, nc.vector.reciprocal(r_g[:], r_g[:]))
                nc.vector.tensor_tensor(tau[:], tau[:], r_g[:], ALU.mult).then_inc(qq, 1)
                link(dve, nc.vector.tensor_tensor(i_g[:], i_g[:], xconv[:, m % 2, :], ALU.mult))
                if m >= 1:
                    low(m - 1)
                dve.wait_ge(sqr, m + 1)
                link(dve, nc.vector.tensor_tensor(i_g[:], i_g[:], tau[:], ALU.mult))
                h = rec[:, m % 2, :]
                link(dve, nc.vector.tensor_tensor_scan(h, a_g[:], i_g[:], 0.0, ALU.mult, ALU.add))
                dve.wait_ge(gl, m + 1)
                nc.vector.tensor_tensor(h, h, gy[:, m % 2, :], ALU.mult).then_inc(rc, 1)
                dve.wait_ge(rc, m + 1)
        low(KC - 1)

    def s_grec_act(act):
        for n in range(KC):
            split_hi(act, FIRST["s_grec"] + n + RING)
            act.wait_ge(w_used, FIRST["s_grec"] + n + 1)
            nc.scalar.activation(grs[:, n, :], ps[:, n, :], ACT.Sigmoid).then_inc(s_grs, 1)

    mg = at("mg", [2, S], SCR)

    def s_reco_act(act):
        for n in range(KC):
            split_hi(act, FIRST["s_reco"] + n + RING)
            act.wait_ge(merged, n + 1)
            nc.scalar.activation(n_hi[:, n, :], att[:, n, :], ACT.Copy).then_inc(merged_hi, 1)

    def s_reco_dve(dve):
        for n in range(KC + 1):
            if n < KC:
                dve.wait_ge(w_used, FIRST["s_reco"] + n + 1)
                dve.wait_ge(s_grs, n + 1)
                link(dve, nc.vector.tensor_tensor(mg[:, n % 2, :], ps[:, n, :], grs[:, n, :], ALU.mult))
                nc.vector.tensor_tensor(att[:, n, :], att[:, n, :], mg[:, n % 2, :], ALU.add).then_inc(merged, 1)
                dve.wait_ge(merged, n + 1)
            if n >= 1:
                dve.wait_ge(merged_hi, n)
                nc.vector.tensor_tensor(n_lo[:, n - 1, :], att[:, n - 1, :], n_hi[:, n - 1, :].bitcast(F32), ALU.subtract
                                        ).then_inc(merged_lo, 1)

    sp_exp, sp_u_ready = sem("softplus_exp"), sem("softplus_u")
    sp_abs, sp_neg, sp_e, sp_u, sp_l, sp_m, sp_d = (at("sp" + n, [KC], SCR + 10240 + 32 * i) for i, n in enumerate(
        ("_abs", "_neg", "_e", "_u", "_l", "_m", "_d")))

    def softplus_dve(dve):
        lam = lru_s8[:]
        link(dve, nc.vector.tensor_scalar(sp_neg[:], lam, -1.0, None, ALU.mult))
        nc.vector.tensor_tensor(sp_abs[:], sp_neg[:], lam, ALU.max).then_inc(setup, 1)
        dve.wait_ge(sp_exp, 1)
        nc.vector.tensor_scalar(sp_u[:], sp_e[:], 1.0, None, ALU.add).then_inc(sp_u_ready, 1)
        dve.wait_ge(sp_u_ready, 1)
        link(dve, nc.vector.tensor_scalar(sp_m[:], sp_u[:], 1.0, None, ALU.is_equal))
        link(dve, nc.vector.scalar_tensor_tensor(out=sp_d[:], in0=sp_u[:], scalar=1.0, in1=sp_m[:], op0=ALU.subtract,
                                                 op1=ALU.add))
        link(dve, nc.vector.reciprocal(sp_d[:], sp_d[:]))
        link(dve, nc.vector.tensor_tensor(sp_d[:], sp_d[:], sp_e[:], ALU.mult))
        link(dve, nc.vector.tensor_tensor(sp_m[:], sp_m[:], sp_e[:], ALU.mult))
        dve.wait_ge(sp_exp, 2)
        link(dve, nc.vector.tensor_tensor(sp_d[:], sp_d[:], sp_l[:], ALU.mult))
        link(dve, nc.vector.tensor_tensor(sp_d[:], sp_d[:], sp_m[:], ALU.add))
        link(dve, nc.vector.scalar_tensor_tensor(out=sp_d[:], in0=sp_neg[:], scalar=0.0, in1=sp_d[:], op0=ALU.max,
                                                 op1=ALU.add))
        link(dve, nc.vector.tensor_scalar(lru_n8[:], sp_d[:], LRU_C, None, ALU.mult))
        link(dve, nc.vector.tensor_scalar(lru_s8[:], sp_d[:], -LRU_C, None, ALU.mult))

    def softplus_act(act):
        act.wait_ge(setup, 2)
        nc.scalar.activation(sp_e[:], sp_abs[:], ACT.Exp, scale=-1.0).then_inc(sp_exp, 1)
        act.wait_ge(sp_u_ready, 1)
        nc.scalar.activation(sp_l[:], sp_u[:], ACT.Ln).then_inc(sp_exp, 1)

    l0_in, l1_in = in_stage(0), in_stage(1)
    for st, name in ((l0_in, "l0_mix_pre"), (l1_in, "l1_mix_pre")):
        st["h_base"] = 8 * before(name, "_pre")
    l0_ffn = ffn("l0_ffn", 2, (h_hi, h_lo), y, "l0_ffn_post", (range(MOD_OUT, MOD1), modv_a, MOD1, (2, 2), modv_b))
    l1_ffn = ffn("l1_ffn", 1, (n_hi, n_lo), y1, "l1_ffn_post", ((), None, MOD_LATE, (2, 2), modv_a))
    ATT_MODS = (2, 5, 8)
    OUT_MODS = [3] * 4 + [2] * 4
    OUT_MODS_1 = [2, 2, 2, 1, 1, 1, 1, 0]
    assert 2 * len(ATT_MODS) == MOD_IN - MOD_FIRST and sum(OUT_MODS) == MOD_OUT - MOD_IN and sum(OUT_MODS_1) == MOD_LATE - MOD_TAIL

    def mods_beside(plan, c0, n):
        c = c0 + sum(plan[:n])
        return range(c, c + plan[n])

    def first_mods_ahead(k):
        if k + FIRST_AHEAD < KC:
            first_mods_pe(nc.tensor, k + FIRST_AHEAD)

    l0_in["beside"] = first_mods_ahead
    s_ffn1 = ffn("s_ffn1", 1, (n_hi, n_lo), y1, "s0_post", ((), None, MOD_LAST, (2, 1), modv_a))
    s_ffn2 = ffn("s_ffn2", 1, (n_hi, n_lo), y1, "s2_post")
    out_stored, c_spread = sem("out_stored"), sem("c_spread")
    LATE = ["mask_in", "rel_in", "lru_wa_in", "lru_wx_in"]

    def stream_x(si, k):
        return xs[si][:, k, :]

    def stream_y(si, k):
        off, n = segs(2)[si]
        return y[:, k, off:off + n]

    def stream_y1(si, k):
        return y1[:, k, :]

    block = ctx.enter_context(nc.Block())

    @block.sync
    def _(sp):
        sp.dma_start(c_cols[:], A["c_cols"]).then_inc(c_landed, 16)
        sp.dma_start(c_line[:], A["c_line"]).then_inc(c_landed, 16)
        sp.dma_start(xl[:], A["x_in"]).then_inc(x_landed, 16)
        sp.dma_start(xc[:], A["ctx_in"]).then_inc(x_landed, 16)
        sp.dma_start(loaded[:], A["consts"]).then_inc(const_landed, 16)
        for k in range(KC):
            if k >= FIRST_SEMS:
                first_there(sp, k - FIRST_SEMS)
            sp.dma_start(mod_pairs[k][:, :, :], A["mod_first"][k]).then_inc(first_landed[k % FIRST_SEMS], 16)
            if k == 1:
                load_block(sp, 0)
                load_block(sp, 1)
        sp.wait_ge(cact_ready, 2)
        load_block(sp, 2)
        load_block(sp, 3)

        def attention_stream(a):
            sp.wait_ge(a["s_pv"], ATT_ITERS * a["nu"])

        def stage(name):
            count = dict(STAGES)[name]
            repeat(sp, FIRST[name] + RING, min(FIRST[name] + count + RING, NBLK), load_block)

        def ffn_stream(f):
            start, _, m0, each, _ = f["mods"]

            def mods(g, part, i):
                for j in range(each[part]):
                    load_mod(sp, m0 + sum(each) * g + part * each[0] + j, i, 2 * sum(each))

            load_block(sp, f["c0"] + RING)
            load_block(sp, f["c0"] + RING + 1)
            for c in start:
                load_mod(sp, c)

            def step(c, d, group, last):
                g, _, i = group
                load_block(sp, c + RING, d)
                load_block(sp, c + RING + 1, d)
                if not last:
                    mods(g, 0, i)
                load_block(sp, c + RING + 2, d)
                load_block(sp, c + RING + 3, d)
                if not last:
                    mods(g, 1, i)
                    load_block(sp, c + RING + 4, d)
                    load_block(sp, c + RING + 5, d)

            ffn_groups(sp, f, step)

        for i in range(10):
            load_block(sp, FIRST["l0_in"] + RING + i)
        sp.wait_ge(h_ready, 2)
        stage("l0_pool")
        for c in range(MOD_FIRST, MOD_IN + MOD_RING):
            load_mod(sp, c)
        attention_stream(l0_att)
        for n in range(KC):
            load_block(sp, FIRST["l0_out"] + RING + n)
            for c in mods_beside(OUT_MODS, MOD_IN, n):
                if c + MOD_RING < MOD_OUT:
                    load_mod(sp, c + MOD_RING)
        ffn_stream(l0_ffn)
        stage("l1_in")
        sp.wait_ge(w_used, FIRST["l1_out"])
        sp.dma_start(mask_raw[:], A["mask_in"]).then_inc(late_landed, 16)
        sp.wait_ge(mod_ops, mods_of(MOD_TAIL)[0])
        sp.dma_start(c2_row, A["c2_row"]).then_inc(c_landed, 16)
        for c in range(MOD_TAIL, MOD_TAIL + MOD_RING):
            load_mod(sp, c)
        attention_stream(l1_att)
        for n in range(KC):
            load_block(sp, FIRST["l1_out"] + RING + n)
            for c in mods_beside(OUT_MODS_1, MOD_TAIL, n):
                if c + MOD_RING < MOD_LATE:
                    load_mod(sp, c + MOD_RING)
        ffn_stream(l1_ffn)
        ffn_stream(s_ffn1)
        sp.wait_ge(w_used, FIRST["s_in"])
        sp.dma_start(rel[:], A["rel_in"]).then_inc(late_landed, 16)
        sp.dma_start(lru_wa[:], A["lru_wa_in"]).then_inc(late_landed, 16)
        sp.dma_start(lru_wx[:], A["lru_wx_in"]).then_inc(late_landed, 16)
        stage("s_in")
        attention_stream(s_att)
        for name in ("s_atto", "s_gatt", "s_rec", "s_grec", "s_reco", "s_out", "s_ffn2"):
            stage(name)
        for k in range(KC):
            x_chunk(sp, before("s2_post", "_post") + 1, k)
            sp.dma_start(A["out"][:, k, :], xl[:, k, :]).then_inc(out_stored, 16)
        sp.wait_ge(out_stored, 16 * KC)

    @block.scalar
    def _(act):
        act.wait_ge(c_landed, 32)
        nc.scalar.activation(c_cols[:], c_cols[:], ACT.Silu).then_inc(cact_ready, 1)
        act.wait_ge(c_spread, 1)
        nc.scalar.activation(c_rows, flat[:, 0:2 * D].rearrange("p (m n) -> p m n", m=2), ACT.Silu).then_inc(cact_ready, 1)
        act.wait_ge(setup, 1)
        norm_act(act, "l0_mix_pre", stream_x, lambda eng, k: eng.wait_ge(x_landed, 32))
        split_hi(act, 0)
        split_hi(act, 1)
        pre_act(act, "l0_mix_pre", 0, h_hi)
        split_hi(act, 2)
        split_hi(act, 3)
        in_act(act, l0_in)
        pool_act(act, l0_in)
        att_act(act, l0_att)
        out_act(act, "l0_out", "l0_mix_post", stream_y)
        norm_act(act, "l0_ffn_pre", stream_x, x_done("l0_ffn_pre"))
        pre_act(act, "l0_ffn_pre", 1, h_hi)
        ffn_act(act, l0_ffn)
        norm_act(act, "l0_ffn_post", stream_y, ffn_y_ready(l0_ffn), ffn_last_blocks(l0_ffn))
        norm_act(act, "l1_mix_pre", stream_x, x_done("l1_mix_pre"))
        pre_act(act, "l1_mix_pre", 0, h_hi)
        in_act(act, l1_in)
        act.wait_ge(c_landed, 48)
        nc.scalar.activation(c2_row, c2_row, ACT.Silu).then_inc(cact_ready, 1)
        att_act(act, l1_att)
        softplus_act(act)
        out_act(act, "l1_out", "l1_mix_post", stream_y1)
        norm_act(act, "l1_ffn_pre", stream_x, x_done("l1_ffn_pre"))
        pre_act(act, "l1_ffn_pre", 1, n_hi)
        ffn_act(act, l1_ffn)
        norm_act(act, "l1_ffn_post", stream_y1, ffn_y_ready(l1_ffn), ffn_last_blocks(l1_ffn))
        norm_act(act, "s0_pre", stream_x, x_done("s0_pre"))
        pre_act(act, "s0_pre", 0, n_hi)
        ffn_act(act, s_ffn1)
        norm_act(act, "s0_post", stream_y1, ffn_y_ready(s_ffn1), ffn_last_blocks(s_ffn1))
        norm_act(act, "s1_pre", stream_x, x_done("s1_pre"))
        pre_act(act, "s1_pre", 1, n_hi)
        s_in_act(act)
        att_act(act, s_att)
        repeat(act, FIRST["s_atto"] + RING, FIRST["s_gatt"] + RING, split_hi)
        s_gatt_act(act)
        s_rec_act(act)
        s_grec_act(act)
        s_reco_act(act)
        out_act(act, "s_out", "s1_post", stream_y1)
        norm_act(act, "s2_pre", stream_x, x_done("s2_pre"))
        pre_act(act, "s2_pre", 2, n_hi)
        ffn_act(act, s_ffn2)
        norm_act(act, "s2_post", stream_y1, ffn_y_ready(s_ffn2), ffn_last_blocks(s_ffn2))

    @block.vector
    def _(dve):
        dve.wait_ge(const_landed, 16)
        nc.vector.tensor_scalar(nsink[:], nsink[:], -1.0, None, ALU.mult)
        dve.wait_ge(cact_ready, 2)
        for k in range(SCALES_AHEAD):
            first_scale(dve, k)
        pre_dve(dve, "l0_mix_pre", 0, h_hi, h_lo, first=True)
        in_dve(dve, l0_in)
        pool_dve(dve, l0_in)

        def att_mods(c, u):
            if u in ATT_MODS:
                c = MOD_FIRST + (0 if c == 0 else len(ATT_MODS)) + ATT_MODS.index(u)
                mod_block(dve, c, [modv_a[m][:, c:c + 1] for m in range(2)], dump_att[:])

        att_dve(dve, l0_att, att_mods)

        def out_mods(n):
            for c in mods_beside(OUT_MODS, MOD_IN, n):
                mod_block(dve, c, [modv_a[m][:, c:c + 1] for m in range(2)], dump[:])

        out_dve(dve, "l0_out", y, 2, out_mods)
        mod_bias(dve, MOD_FIRST, MOD_OUT, modv_a, MOD0)
        vectors(dve, modv_a, 0, 0, None, None, 2)
        vectors(dve, modv_a, 1, 1, 3, 4, None)
        post_dve(dve, "l0_mix_post", 0, y)
        pre_dve(dve, "l0_ffn_pre", 1, h_hi, h_lo)
        ffn_dve(dve, l0_ffn)
        mod_bias(dve, MOD_OUT, MOD1, modv_a, MOD0)
        vectors(dve, modv_a, 1, 1, None, None, 5)
        post_dve(dve, "l0_ffn_post", 1, y)
        dve.wait_ge(n_t, 8 * before("l1_mix_pre"))
        dve.wait_ge(mod_copied, 2 * (NG - 1))
        mod_bias(dve, MOD1, MOD_TAIL, modv_b, MOD1)
        vectors(dve, modv_b, 2, 0, 0, 1, 2)
        vectors(dve, modv_b, 3, 1, 3, 4, None)
        pre_dve(dve, "l1_mix_pre", 0, h_hi, h_lo)
        in_dve(dve, l1_in)
        dve.wait_ge(late_landed, 16)
        nc.vector.tensor_copy(mask[:], mask_raw[:])
        nc.vector.tensor_copy(ident_r[:], ident[:]).then_inc(sem("mask_ready"), 1)
        att_dve(dve, l1_att)
        m_done(dve, l1_att)
        softplus_dve(dve)
        dve.wait_ge(cact_ready, 3)

        def out_mods_1(n):
            for c in mods_beside(OUT_MODS_1, MOD_TAIL, n):
                dst, first = (modv_b, MOD1) if c < MOD2 else (modv_a, MOD2)
                mod_block(dve, c, [dst[0][:, c - first:c - first + 1]], dump[:])

        out_dve(dve, "l1_out", y1, 1, out_mods_1)
        mod_bias(dve, MOD_TAIL, MOD2, modv_b, MOD1)
        vectors(dve, modv_b, 3, 1, None, None, 5, nseg=1)
        post_dve(dve, "l1_mix_post", 0, y1)
        pre_dve(dve, "l1_ffn_pre", 1, n_hi, n_lo)
        ffn_dve(dve, l1_ffn)
        post_dve(dve, "l1_ffn_post", 1, y1)
        dve.wait_ge(n_t, 8 * before("s0_pre"))
        dve.wait_ge(mod_copied, 4 * (NG - 1))
        mod_bias(dve, MOD2, MOD_LAST, modv_a, MOD2)
        vectors(dve, modv_a, 4, 0, 0, 1, 2, 0.5, nseg=1)
        pre_dve(dve, "s0_pre", 0, n_hi, n_lo)
        ffn_dve(dve, s_ffn1)
        post_dve(dve, "s0_post", 0, y1)
        dve.wait_ge(mod_copied, 6 * (NG - 1))
        mod_bias(dve, MOD_LAST, NMOD, modv_a, MOD2)
        for sub, res in ((1, 1.0), (2, 0.5)):
            vectors(dve, modv_a, 4 + sub, sub, 3 * sub, 3 * sub + 1, 3 * sub + 2, res, nseg=1)
        pre_dve(dve, "s1_pre", 1, n_hi, n_lo)
        s_in_dve(dve)
        bias_dve(dve)
        att_dve(dve, s_att)
        s_atto_dve(dve)
        s_gatt_dve(dve)
        s_rec_dve(dve)
        s_reco_dve(dve)
        out_dve(dve, "s_out", y1, 1)
        post_dve(dve, "s1_post", 1, y1)
        pre_dve(dve, "s2_pre", 2, n_hi, n_lo)
        ffn_dve(dve, s_ffn2)
        post_dve(dve, "s2_post", 2, y1)

    @block.gpsimd
    def _(pool):
        nc.gpsimd.memset(ones[:], 1.0)
        nc.gpsimd.memset(eps_col[:], EPS).then_inc(setup, 1)

        def stage(c0, c1):
            repeat(pool, c0 + RING, min(c1 + RING, NBLK), split_lo)

        def ffn_stage(f, pre_name, n):
            x_chunk(pool, before(pre_name, "_post"), DVE_ADDS[-1])
            x_chunk(pool, before(pre_name, "_post"), POOL_ADDS[-1])
            nc.gpsimd.memset(f["y"][:, :, 0:n], 0.0).then_inc(y_zero, 1)
            stage(f["c0"], f["c0"] + FFN_BLOCKS)

        repeat(pool, 0, RING, split_lo)
        in_pool(pool, l0_in)
        split_lo(pool, FIRST["l0_pool"] + RING)
        att_pool(pool, l0_att, lambda eng: eng.wait_ge(l0_in["mix_lo"], 4))
        stage(FIRST["l0_out"], FIRST["l0_ffn"])
        post_pool(pool, "l0_mix_post", y)
        ffn_stage(l0_ffn, "l0_ffn_pre", T)
        post_pool(pool, "l0_ffn_post", y)
        in_pool(pool, l1_in)
        att_pool(pool, l1_att, lambda eng: eng.wait_ge(l1_in["lo"], 10))
        stage(FIRST["l1_out"], FIRST["l1_ffn"])
        post_pool(pool, "l1_mix_post", y1)
        ffn_stage(l1_ffn, "l1_ffn_pre", S)
        post_pool(pool, "l1_ffn_post", y1)
        ffn_stage(s_ffn1, "s0_pre", S)
        post_pool(pool, "s0_post", y1)
        stage(FIRST["s_in"], FIRST["s_atto"])
        att_pool(pool, s_att, lambda eng: eng.wait_ge(s_lo, 12))
        stage(FIRST["s_atto"], FIRST["s_ffn2"])
        post_pool(pool, "s1_post", y1)
        ffn_stage(s_ffn2, "s2_pre", S)
        post_pool(pool, "s2_post", y1)

    @block.tensor
    def _(pe):
        pe.wait_ge(setup, 1)
        pe.wait_ge(c_landed, 32)
        for i in range(2 * D // 512):
            mm = nc.tensor.matmul(ps[:, i, :], ones[0:1, :], c_line[:, i // 2, i % 2 * 512:(i % 2 + 1) * 512],
                                  start=True, stop=True)
        mm.then_inc(c_spread, 1)
        norm_pe(pe, "l0_mix_pre")
        pe.wait_ge(n_turn, 1)
        pe.wait_ge(cact_ready, 1)
        for k in range(FIRST_AHEAD):
            first_mods_pe(pe, k)
        in_pe(pe, l0_in)
        pool_pe(pe, l0_in)

        def l0_free(pe):
            pe.wait_ge(l0_in["mix_lo"], 4)

        att_pe(pe, l0_att, l0_free)
        m_done(pe, l0_att)
        out_pe(pe, "l0_out", (h_hi, h_lo), "l0_mix_post")
        norm_pe(pe, "l0_ffn_pre")
        ffn_pe(pe, l0_ffn)
        norm_pe(pe, "l0_ffn_post", range(KC - SUMS_BEHIND, KC))
        norm_pe(pe, "l1_mix_pre")
        in_pe(pe, l1_in)

        def l1_free(pe):
            pe.wait_ge(l1_in["out"], 10)
            pe.wait_ge(l1_in["v_lo"], 3)
            pe.wait_ge(sem("mask_ready"), 1)

        att_pe(pe, l1_att, l1_free)
        m_done(pe, l1_att)
        out_pe(pe, "l1_out", (n_hi, n_lo), "l1_mix_post")
        norm_pe(pe, "l1_ffn_pre")
        ffn_pe(pe, l1_ffn)
        norm_pe(pe, "l1_ffn_post", range(KC - SUMS_BEHIND, KC))
        norm_pe(pe, "s0_pre")
        ffn_pe(pe, s_ffn1)
        norm_pe(pe, "s0_post", range(KC - SUMS_BEHIND, KC))
        norm_pe(pe, "s1_pre")
        s_in_pe(pe)

        def s_free(pe):
            pe.wait_ge(s_lo, 12)
            pe.wait_ge(sem("rel_ready"), 1)

        att_pe(pe, s_att, s_free)
        s_atto_pe(pe)
        eight_pe(pe, "s_gatt", (n_hi, n_lo), lambda i, j: pe.wait_ge(att_done, i * 2 + j // 2 + 1))
        s_rec_pe(pe)

        def grec_free(i, j):
            pe.wait_ge(gl, KC)
            pe.wait_ge(sig, i * (KC - 1) + 1)

        eight_pe(pe, "s_grec", (n_hi, n_lo), grec_free)
        pe.wait_ge(rec_lo, KC)
        eight_pe(pe, "s_reco", (rec_hi, rec_l), lambda i, j: pe.wait_ge(s_grs, i * RING + j + 1))
        pe.wait_ge(merged_lo, KC)
        out_pe(pe, "s_out", (n_hi, n_lo), "s1_post")
        norm_pe(pe, "s2_pre")
        ffn_pe(pe, s_ffn2)
        norm_pe(pe, "s2_post", range(KC - SUMS_BEHIND, KC))


INPUTS = (("x_in", [P, KC, S]), ("ctx_in", [P, KC, C]), ("consts", [P, PACKED]), ("c_cols", [P, KC, 2]), ("c_line", [1, 2, D]), ("c2_row", [P, D]), ("w_stream", [NBLK, P, BLK]),
          ("mod_first", [KC, P, 2, BLK]), ("mod_stream", [NMOD - MOD_FIRST, P, BLK]), ("mask_in", [P, 2, P]), ("rel_in", [P, 8, 2 * P]),
          ("lru_wa_in", [P, KC, P]), ("lru_wx_in", [P, KC, P]))


def kernel(**inputs):
    import concourse.bacc as _bacc
    from concourse.bass_utils import run_bass_kernel_spmd as _run

    a = {k: np.asarray(v) for k, v in inputs.items()}

    def chunks(v):
        v = v.reshape(v.shape[:-1] + (v.shape[-1] // P, P))
        return np.moveaxis(v, -1, 0)

    def tokens(x):
        return np.ascontiguousarray(x.T.reshape(-1, P, x.shape[0]).transpose(1, 0, 2))

    def blocks(w):
        k, n = w.shape
        return w.reshape(k // P, P, n // P, P).transpose(2, 1, 0, 3)

    def wide(w):
        n = w.shape[1]
        return w.reshape(n // P, BLK // n, P, n).transpose(0, 2, 1, 3).reshape(n // P, P, 8, P)

    def heads(*hs):
        return np.concatenate([np.arange(h * HD, (h + 1) * HD) for h in hs])

    stream = np.empty((NBLK, P, 8, P), np.float32)

    def put(name, *parts):
        c = FIRST[name]
        for part in parts:
            stream[c:c + len(part)] = part
            c += len(part)
        assert c == FIRST[name] + dict(STAGES)[name]

    def put_ffn(name, w_in, w_out):
        gate, up = blocks(w_in[:, :FH]), blocks(w_in[:, FH:])
        out = w_out.reshape(NH, 1, P, 8, P)
        order = [gate[0:1], up[0:1]]
        for g in range(NG):
            b = 2 * g + 1
            order += [gate[b:b + 1], up[b:b + 1]]
            if g < NG - 1:
                order += [gate[b + 1:b + 2], up[b + 1:b + 2]]
            order += [out[2 * g], out[b]]
        put(name, *order)

    we, weo, wo, woo = a["we_in"][0], a["we_out"][0], a["wo_in"][0], a["wo_out"][0]
    q0 = np.concatenate([heads(c, c + 4) for c in range(4)])
    put("l0_in", blocks(we[:, 512:640]), blocks(we[:, q0[:P]]), blocks(we[:, 640:768]), blocks(we[:, q0[P:]]),
        blocks(we[:, 768:])[::-1])
    stream[FIRST["l0_pool"]] = 0.0
    stream[FIRST["l0_pool"], :, 0:4] = a["we_pool"][0].transpose(1, 0, 2)
    put("l0_out", blocks(np.concatenate([weo[q0], weo[512:]])))
    q1 = np.concatenate([heads(8 * (ci % 2) + ci // 2, 8 * (ci % 2) + 4 + ci // 2) for ci in range(8)])
    put("l1_in", blocks(wo[:, 1024:1280]), wide(wo[:, 1280:1536]), blocks(wo[:, q1]))
    put("l1_out", blocks(woo[q1]))
    put_ffn("l0_ffn", a["w_ffn_in"][0], a["w_ffn_out"][0])
    put_ffn("l1_ffn", a["w_ffn_in"][1], a["w_ffn_out"][1])
    put_ffn("s_ffn1", a["ffn1_w_gu_2"][0], a["ffn1_w_down_2"][0])
    put_ffn("s_ffn2", a["ffn2_w_gu_2"][0], a["ffn2_w_down_2"][0])
    ws = blocks(a["w_in_2"][0])
    put("s_in", ws[0:8], wide(a["w_in_2"][0][:, 1024:1536]))
    xr, yr, ga, gr = ws[12:20], ws[20:28], ws[28:36], ws[36:44]
    atto = blocks(a["w_att_o_2"][0])
    put("s_atto", np.concatenate([atto[0::2], atto[1::2]], axis=2))
    put("s_gatt", ga)
    put("s_rec", np.stack([xr, yr], 1).reshape(16, P, 8, P))
    put("s_grec", gr)
    put("s_reco", blocks(a["w_rec_o_2"][0]))
    put("s_out", blocks(a["w_out_2"][0]))
    mods = np.concatenate([a["w_mod"][0].T, a["w_mod"][1].T, a["w_ada_2"][0].T]).reshape(NMOD, P, BLK)
    by_input = blocks(a["w_mod"][0][:, :D]).reshape(KC, P, BLK)
    mod_first = np.stack([np.stack([by_input[k], mods[KC + k]], axis=1) for k in range(KC)])

    p = np.arange(P)
    ident = np.eye(P, dtype=np.float32)
    blkones = (p[:, None] // HD == p[None, :] // HD).astype(np.float32)
    freqs = 10000.0 ** (-np.arange(16) / 16)
    t = np.arange(S)
    pos = np.where((p % HD < 32)[:, None], t[None, :] // 64, t[None, :] % 64)
    ang = (pos.astype(np.float32) * freqs[p % 16].astype(np.float32)[:, None]).astype(np.float32)
    cos = np.cos(ang).astype(np.float32)
    sin = (np.sin(ang) * np.where(p % 32 < 16, -1.0, 1.0)[:, None]).astype(np.float32)
    edges = np.ones((4, 2, 8), np.float32)
    for g, w in enumerate(POOL_W):
        for e in range(8):
            edges[g, 0, e] = w / (e + w - w // 2) if e < w // 2 else 1.0
            left = 7 - e
            edges[g, 1, e] = w / (w // 2 + min(left + 1, w - w // 2))
    prev = np.where(p[None, :] >= p[:, None], 0.0, MASKED)
    nxt = np.where(p[None, :] <= p[:, None], 0.0, MASKED)

    def rows(v):
        return np.broadcast_to(v.reshape(1, -1), (P, v.size))

    gp = np.stack([a["g_pre_mix"][0], a["g_pre_ffn"][0], a["g_pre_mix"][1], a["g_pre_ffn"][1], *a["norm_pre_2"][0]])
    gq = np.stack([a["g_post_mix"][0], a["g_post_ffn"][0], a["g_post_mix"][1], a["g_post_ffn"][1], *a["norm_post_2"][0]])
    sink = a["wo_sink"][0][[8 * (ci % 2) + 4 * half + ci // 2 for ci in range(8) for half in range(2)]]
    rb = a["rel_bias_2"][0]
    packed = dict(
        ident=ident, blkones=blkones, cos=cos, sin=sin,
        bmod=chunks(np.concatenate([a["b_mod"][0], a["b_mod"][1], a["b_ada_2"][0]])), gpre=chunks(gp), gpost=chunks(gq),
        qk_gain=np.stack([np.tile(a["we_q_gain"][0], 2), np.tile(a["we_k_gain"][0], 2)], axis=1),
        pool_scale=chunks(a["we_pool_scale"][0]), edges=rows(edges), nsink=rows(sink), relc=rows(rb[:, 256]),
        conv_w=np.moveaxis(chunks(a["conv_w_2"][0]), 1, 2), conv_b=chunks(a["conv_b_2"][0]),
        lru_ba=chunks(a["lru_ba_2"][0]), lru_bx=chunks(a["lru_bx_2"][0]), lru_s8=chunks(a["lru_lambda_2"][0]))
    consts = np.zeros((P, PACKED), np.float32)
    off = 0
    for name, cols in CONSTS:
        n = int(np.prod(cols))
        consts[:, off:off + n] = packed[name].reshape(P, n)
        off += padded(cols)

    index = np.minimum(256 + p[:, None] - np.arange(2 * P)[None, :], 256)
    rel = np.ascontiguousarray(rb[:, index].transpose(1, 0, 2))

    def diagonal(w):
        out = np.zeros((P, KC, P), np.float32)
        out[0:HD, :, 0:HD] = w[0::2].transpose(1, 0, 2)
        out[HD:P, :, HD:P] = w[1::2].transpose(1, 0, 2)
        return out

    c_line = np.stack([a["c"][0], a["c_ctx"]])[None]
    c_cols = np.stack([chunks(a["c"][0]), chunks(a["c_ctx"])], axis=2)
    arrays = dict(
        c_cols=c_cols, c_line=c_line, c2_row=np.ascontiguousarray(rows(a["c_2"][0])),
        x_in=tokens(a["x"][0]), ctx_in=tokens(a["ctx"][0]), consts=consts, w_stream=stream.reshape(NBLK, P, BLK),
        mod_first=mod_first, mod_stream=mods[MOD_FIRST:],
        mask_in=np.stack([prev, nxt], axis=1).astype(np.float32), rel_in=rel,
        lru_wa_in=diagonal(a["lru_wa_2"][0]), lru_wx_in=diagonal(a["lru_wx_2"][0]))

    nc = _bacc.Bacc("TRN2", target_bir_lowering=False, num_devices=1)
    A = {name: nc.dram_tensor(name, shape, F32, kind="ExternalInput").ap() for name, shape in INPUTS}
    A["out"] = nc.dram_tensor("out", [P, KC, S], F32, kind="ExternalOutput").ap()
    build(nc, A)
    r = _run(nc, [arrays], core_ids=[0])
    out = r.results[0]["out"]
    return np.ascontiguousarray(out.transpose(2, 1, 0).reshape(1, S, D))
```
